# Optimizing a Trainium2 kernel written in Bass

```python
import jax, jax.numpy as jnp
from jax import lax
import numpy as np

D_MODEL = 1024
BATCH = 1
SEQ = 256
DEPTH = 2

N_A = DEPTH // 2
N_B = DEPTH - N_A
MEM_LEN = 256
MEM_HEADS = 4
MEM_DH = D_MODEL // (2 * MEM_HEADS)
MEM_WIDTH = MEM_HEADS * MEM_DH
GLA_HEADS = 4
GLA_DV = D_MODEL // (2 * GLA_HEADS)
GLA_DK = GLA_DV // 2
GLA_QK = GLA_HEADS * GLA_DK
GLA_V = GLA_HEADS * GLA_DV
GLA_RANK = 16
GLA_TAU = 16.0
GLA_CHUNK = 64
NSA_HEADS = 8
NSA_GROUPS = 2
NSA_HPG = NSA_HEADS // NSA_GROUPS
NSA_DH = D_MODEL // (2 * NSA_HEADS)
NSA_WIDTH = NSA_HEADS * NSA_DH
KV_WIDTH = NSA_GROUPS * NSA_DH
CMP_BLOCK = 32
CMP_STRIDE = 16
CMP_HIDDEN = 256
SEL_BLOCK = 64
SEL_TOPN = 16
WINDOW = 512
Q_BLOCK = 128
FFN_DIM = ((8 * D_MODEL // 3 + 127) // 128) * 128
CONV_WIDTH = 3
EPS = 1e-6
A_PROJ = 2 * GLA_QK + 2 * GLA_V + GLA_RANK + MEM_WIDTH
B_PROJ = NSA_WIDTH + 3 * NSA_HEADS + MEM_WIDTH
SHARED_KV_PROJ = 6 * KV_WIDTH


F32 = jnp.float32

def rmsnorm(x, g):
    xf = x.astype(F32)
    y = xf * lax.rsqrt(jnp.mean(xf * xf, axis=-1, keepdims=True) + EPS)
    return y.astype(x.dtype) * g

def split_cols(z, widths):
    idx = [int(i) for i in np.cumsum(widths)[:-1]]
    return jnp.split(z, idx, axis=-1)

def masked_softmax(s, mask):
    s = jnp.where(mask, s.astype(F32), -jnp.inf)
    m = jnp.max(s, axis=-1, keepdims=True)
    m = jnp.where(jnp.isfinite(m), m, 0.0)
    e = jnp.exp(s - m)
    return e / jnp.maximum(jnp.sum(e, axis=-1, keepdims=True), 1e-30)

def alibi_slopes(n):
    return jnp.exp2(-8.0 * jnp.arange(1, n + 1, dtype=F32) / n)

def mem_attend(mq, mem_k, mem_v):
    B, T, _ = mq.shape
    qh = mq.reshape(B, T, MEM_HEADS, MEM_DH) * (MEM_DH ** -0.5)
    s = jnp.einsum('bthd,bmhd->bhtm', qh, mem_k)
    p = jax.nn.softmax(s.astype(F32), axis=-1).astype(mem_v.dtype)
    return jnp.einsum('bhtm,bmhd->bthd', p, mem_v).reshape(B, T, MEM_WIDTH)

def gla_chunked(q, k, v, log_a):
    B, T, H, DK = q.shape
    DV = v.shape[-1]
    C = GLA_CHUNK
    NC = T // C

    def chunks(a):
        return a.astype(F32).reshape(B, NC, C, H, a.shape[-1]).transpose(1, 0, 3, 2, 4)

    causal = jnp.tril(jnp.ones((C, C), dtype=bool))[:, :, None]

    def step(S, inp):
        qc, kc, vc, gc = inp
        b = jnp.cumsum(gc, axis=2)
        b_last = b[:, :, -1:, :]
        o_inter = jnp.einsum('bhtd,bhde->bhte', qc * jnp.exp(b), S)
        decay = jnp.exp(jnp.where(causal, b[:, :, :, None, :] - b[:, :, None, :, :], -jnp.inf))
        attn = jnp.einsum('bhtd,bhsd,bhtsd->bhts', qc, kc, decay)
        o = o_inter + jnp.einsum('bhts,bhse->bhte', attn, vc)
        S = jnp.exp(b_last[:, :, 0, :])[..., None] * S + jnp.einsum('bhsd,bhse->bhde', kc * jnp.exp(b_last - b), vc)
        return S, o

    S0 = jnp.zeros((B, H, DK, DV), F32)
    _, o = lax.scan(step, S0, (chunks(q), chunks(k), chunks(v), chunks(log_a)))
    return o.transpose(1, 0, 3, 2, 4).reshape(B, T, H, DV)

def gla_layer_mix(h, mem_k, mem_v, w_in, w_alpha, b_alpha, g_head, w_out):
    B, T, _ = h.shape
    q, k, v, r, alr, mq = split_cols(h @ w_in, [GLA_QK, GLA_QK, GLA_V, GLA_V, GLA_RANK, MEM_WIDTH])
    q = q.reshape(B, T, GLA_HEADS, GLA_DK) * (GLA_DK ** -0.5)
    k = k.reshape(B, T, GLA_HEADS, GLA_DK)
    v = v.reshape(B, T, GLA_HEADS, GLA_DV)
    log_a = jax.nn.log_sigmoid((alr @ w_alpha + b_alpha).astype(F32)) / GLA_TAU
    log_a = log_a.reshape(B, T, GLA_HEADS, GLA_DK)
    o = gla_chunked(q, k, v, log_a).astype(h.dtype)
    o = rmsnorm(o, g_head).reshape(B, T, GLA_V) * jax.nn.silu(r)
    m = mem_attend(mq, mem_k, mem_v)
    return jnp.concatenate([o, m], axis=-1) @ w_out

def compress_blocks(a, pe, w1, w2):
    B, T, G, DH = a.shape
    n_sub = CMP_BLOCK // CMP_STRIDE
    sub = a.reshape(B, T // CMP_STRIDE, CMP_STRIDE, G, DH)
    ncmp = T // CMP_STRIDE - n_sub + 1
    blocks = jnp.concatenate([sub[:, i:i + ncmp] for i in range(n_sub)], axis=2)
    blocks = blocks + pe[:, None, :]
    flat = blocks.transpose(0, 1, 3, 2, 4).reshape(B, ncmp, G, CMP_BLOCK * DH)
    return jax.nn.gelu(flat @ w1) @ w2

def nsa_shared_kv(x, g_kv, w_kv, pe_k, pe_v, w_ck1, w_ck2, w_cv1, w_cv2):
    B, T, _ = x.shape
    kv = (rmsnorm(x, g_kv) @ w_kv).reshape(B, T, 6, NSA_GROUPS, NSA_DH)
    k_c, v_c, k_s, v_s, k_w, v_w = [kv[:, :, i] for i in range(6)]
    return (compress_blocks(k_c, pe_k, w_ck1, w_ck2), compress_blocks(v_c, pe_v, w_cv1, w_cv2),
            k_s, v_s, k_w, v_w)

def selection_overlap(ncmp, ns):
    cs = jnp.arange(ncmp) * CMP_STRIDE
    ss = jnp.arange(ns) * SEL_BLOCK
    ov = jnp.minimum(cs[:, None] + CMP_BLOCK, ss[None, :] + SEL_BLOCK) - jnp.maximum(cs[:, None], ss[None, :])
    return jnp.clip(ov, 0, None).astype(F32) / CMP_BLOCK

def nsa_attend(q, gates, k_cmp, v_cmp, k_slc, v_slc, k_win, v_win):
    B, T, H, DH = q.shape
    G, HPG = NSA_GROUPS, NSA_HPG
    nqb = T // Q_BLOCK
    ncmp = k_cmp.shape[1]
    ns = T // SEL_BLOCK
    n_sel = min(SEL_TOPN, ns)
    slope = alibi_slopes(H).reshape(G, HPG)[None, None, :, :, None]
    cmp_end = jnp.arange(ncmp) * CMP_STRIDE + CMP_BLOCK - 1
    overlap = selection_overlap(ncmp, ns)

    def to_blocks(a):
        return a.reshape(B, ns, SEL_BLOCK, G, DH).transpose(0, 3, 1, 2, 4)

    ks_b, vs_b = to_blocks(k_slc), to_blocks(v_slc)
    pad = ((0, 0), (WINDOW, 0), (0, 0), (0, 0))
    kw_pad, vw_pad = jnp.pad(k_win, pad), jnp.pad(v_win, pad)
    gather = jax.vmap(jax.vmap(lambda blocks, ix: blocks[ix]))
    sel_off = jnp.arange(SEL_BLOCK)
    win_off = jnp.arange(Q_BLOCK + WINDOW)
    blk = jnp.arange(ns)

    def one_block(inp):
        qi, gi, bi = inp
        t = bi * Q_BLOCK + jnp.arange(Q_BLOCK)
        dist_c = (t[:, None] - cmp_end[None, :])
        s = jnp.einsum('bqghd,bngd->bqghn', qi, k_cmp).astype(F32) - slope * dist_c.astype(F32)[None, :, None, None, :]
        p_c = masked_softmax(s, (dist_c >= 0)[None, :, None, None, :])
        o_c = jnp.einsum('bqghn,bngd->bqghd', p_c.astype(v_cmp.dtype), v_cmp)
        cur = t // SEL_BLOCK
        imp = jnp.einsum('bqghn,nj->bqgj', p_c, overlap)
        valid = (blk[None, :] <= cur[:, None])[None, :, None, :]
        forced = ((blk[None, :] == 0) | (blk[None, :] == cur[:, None]) | (blk[None, :] == cur[:, None] - 1))[None, :, None, :]
        imp = jnp.where(forced, jnp.inf, jnp.where(valid, imp, -jnp.inf))
        _, idx = lax.top_k(imp, n_sel)
        idx = idx.transpose(0, 2, 1, 3)
        kg = gather(ks_b, idx).reshape(B, G, Q_BLOCK, n_sel * SEL_BLOCK, DH)
        vg = gather(vs_b, idx).reshape(B, G, Q_BLOCK, n_sel * SEL_BLOCK, DH)
        pos = (idx[..., None] * SEL_BLOCK + sel_off).reshape(B, G, Q_BLOCK, n_sel * SEL_BLOCK)
        dist_s = (t[None, None, :, None] - pos).transpose(0, 2, 1, 3)[:, :, :, None, :]
        s = jnp.einsum('bqghd,bgqsd->bqghs', qi, kg).astype(F32) - slope * dist_s.astype(F32)
        p_s = masked_softmax(s, dist_s >= 0)
        o_s = jnp.einsum('bqghs,bgqsd->bqghd', p_s.astype(vg.dtype), vg)
        start = bi * Q_BLOCK
        kw = lax.dynamic_slice_in_dim(kw_pad, start, Q_BLOCK + WINDOW, axis=1)
        vw = lax.dynamic_slice_in_dim(vw_pad, start, Q_BLOCK + WINDOW, axis=1)
        kpos = start - WINDOW + win_off
        dist_w = t[:, None] - kpos[None, :]
        mask_w = ((dist_w >= 0) & (dist_w < WINDOW) & (kpos >= 0)[None, :])[None, :, None, None, :]
        s = jnp.einsum('bqghd,bkgd->bqghk', qi, kw).astype(F32) - slope * dist_w.astype(F32)[None, :, None, None, :]
        p_w = masked_softmax(s, mask_w)
        o_w = jnp.einsum('bqghk,bkgd->bqghd', p_w.astype(vw.dtype), vw)
        return gi[..., 0:1] * o_c + gi[..., 1:2] * o_s + gi[..., 2:3] * o_w

    qb = q.reshape(B, nqb, Q_BLOCK, G, HPG, DH).transpose(1, 0, 2, 3, 4, 5)
    gb = gates.reshape(B, nqb, Q_BLOCK, G, HPG, 3).transpose(1, 0, 2, 3, 4, 5).astype(q.dtype)
    out = lax.map(one_block, (qb, gb, jnp.arange(nqb)))
    return out.transpose(1, 0, 2, 3, 4, 5).reshape(B, T, H * DH)

def nsa_layer_mix(h, shared, mem_k, mem_v, w_in, w_out):
    B, T, _ = h.shape
    q, gl, mq = split_cols(h @ w_in, [NSA_WIDTH, 3 * NSA_HEADS, MEM_WIDTH])
    q = q.reshape(B, T, NSA_HEADS, NSA_DH) * (NSA_DH ** -0.5)
    gates = jax.nn.sigmoid(gl.reshape(B, T, NSA_HEADS, 3))
    o = nsa_attend(q, gates, *shared)
    m = mem_attend(mq, mem_k, mem_v)
    return jnp.concatenate([o, m], axis=-1) @ w_out

def conv_ffn(h, w_up, conv_w, conv_b, w_down):
    T = h.shape[1]
    a, b = jnp.split(h @ w_up, 2, axis=-1)
    a_pad = jnp.pad(a, ((0, 0), (CONV_WIDTH - 1, 0), (0, 0)))
    a = sum(a_pad[:, j:j + T] * conv_w[j] for j in range(CONV_WIDTH)) + conv_b
    return (jax.nn.silu(a) * b) @ w_down

def first_inputs(seed: int = 0) -> dict:
    key = jax.random.key(seed)
    ks = jax.random.split(key, 26)

    def nrm(k, shape, scale):
        return jax.random.normal(k, shape, F32) * scale

    def gain(k, shape):
        return 1.0 + 0.02 * jax.random.normal(k, shape, F32)

    D = D_MODEL
    return {
        'x': nrm(ks[0], (BATCH, SEQ, D), 1.0),
        'mem': nrm(ks[1], (BATCH, MEM_LEN, D), 1.0),
        'g_mix': gain(ks[2], (DEPTH, D)),
        'g_ffn': gain(ks[3], (DEPTH, D)),
        'g_mem': gain(ks[4], (DEPTH, D)),
        'w_mem_kv': nrm(ks[5], (DEPTH, D, 2 * MEM_WIDTH), D ** -0.5),
        'w_up': nrm(ks[6], (DEPTH, D, 2 * FFN_DIM), D ** -0.5),
        'conv_w': nrm(ks[7], (DEPTH, CONV_WIDTH, FFN_DIM), CONV_WIDTH ** -0.5),
        'conv_b': nrm(ks[8], (DEPTH, FFN_DIM), 0.01),
        'w_down': nrm(ks[9], (DEPTH, FFN_DIM, D), FFN_DIM ** -0.5),
        'a_w_in': nrm(ks[10], (N_A, D, A_PROJ), D ** -0.5),
        'a_w_alpha': nrm(ks[11], (N_A, GLA_RANK, GLA_QK), GLA_RANK ** -0.5),
        'a_b_alpha': nrm(ks[12], (N_A, GLA_QK), 0.01),
        'a_g_head': gain(ks[13], (N_A, GLA_DV)),
        'a_w_out': nrm(ks[14], (N_A, GLA_V + MEM_WIDTH, D), (GLA_V + MEM_WIDTH) ** -0.5),
        'g_kv': gain(ks[15], (D,)),
        'w_kv': nrm(ks[16], (D, SHARED_KV_PROJ), D ** -0.5),
        'pe_k': nrm(ks[17], (CMP_BLOCK, NSA_DH), 0.1),
        'pe_v': nrm(ks[18], (CMP_BLOCK, NSA_DH), 0.1),
        'w_ck1': nrm(ks[19], (CMP_BLOCK * NSA_DH, CMP_HIDDEN), (CMP_BLOCK * NSA_DH) ** -0.5),
        'w_ck2': nrm(ks[20], (CMP_HIDDEN, NSA_DH), CMP_HIDDEN ** -0.5),
        'w_cv1': nrm(ks[21], (CMP_BLOCK * NSA_DH, CMP_HIDDEN), (CMP_BLOCK * NSA_DH) ** -0.5),
        'w_cv2': nrm(ks[22], (CMP_HIDDEN, NSA_DH), CMP_HIDDEN ** -0.5),
        'b_w_in': nrm(ks[23], (N_B, D, B_PROJ), D ** -0.5),
        'b_w_out': nrm(ks[24], (N_B, NSA_WIDTH + MEM_WIDTH, D), (NSA_WIDTH + MEM_WIDTH) ** -0.5),
        'g_final': gain(ks[25], (D,)),
    }

def first_block(x, mem, g_mix, g_ffn, g_mem, w_mem_kv, w_up, conv_w, conv_b, w_down,
              a_w_in, a_w_alpha, a_b_alpha, a_g_head, a_w_out,
              g_kv, w_kv, pe_k, pe_v, w_ck1, w_ck2, w_cv1, w_cv2,
              b_w_in, b_w_out, g_final):
    B, M, _ = mem.shape
    shared = None
    for l in range(DEPTH):
        if l == N_A:
            shared = nsa_shared_kv(x, g_kv, w_kv, pe_k, pe_v, w_ck1, w_ck2, w_cv1, w_cv2)
        mkv = (rmsnorm(mem, g_mem[l]) @ w_mem_kv[l]).reshape(B, M, 2, MEM_HEADS, MEM_DH)
        mem_k, mem_v = mkv[:, :, 0], mkv[:, :, 1]
        h = rmsnorm(x, g_mix[l])
        if l < N_A:
            x = x + gla_layer_mix(h, mem_k, mem_v, a_w_in[l], a_w_alpha[l], a_b_alpha[l], a_g_head[l], a_w_out[l])
        else:
            j = l - N_A
            x = x + nsa_layer_mix(h, shared, mem_k, mem_v, b_w_in[j], b_w_out[j])
        x = x + conv_ffn(rmsnorm(x, g_ffn[l]), w_up[l], conv_w[l], conv_b[l], w_down[l])
    return rmsnorm(x, g_final)


DEPTH_2 = 1

CHUNK = 64
N_META = 16
D_MIX = D_MODEL
D_ATTN = D_MIX // 2
HEAD_DIM = 64
N_HEADS = D_ATTN // HEAD_DIM
D_POOL = D_MIX - D_ATTN
POOL_WINDOWS = (2, 4, 8, 16)
N_POOL_GROUPS = len(POOL_WINDOWS)
POOL_GROUP_DIM = D_POOL // N_POOL_GROUPS
D_IN = 3 * D_ATTN + N_HEADS + D_POOL
D_FF = ((8 * D_MODEL + 3 * 256 - 1) // (3 * 256)) * 256


def _rmsnorm(x, w):
    x32 = x.astype(jnp.float32)
    y = x32 * lax.rsqrt(jnp.mean(x32 * x32, axis=-1, keepdims=True) + EPS)
    return (y * w.astype(jnp.float32)).astype(x.dtype)

def _forgetting_attention(q, k, v, cum_logf):
    L = q.shape[2]
    scale = HEAD_DIM ** -0.5
    outs = []
    for q0 in range(0, L, Q_BLOCK):
        q1 = min(q0 + Q_BLOCK, L)
        qb = q[:, :, q0:q1]
        kp = k[:, :, :q1]
        vp = v[:, :, :q1]
        s = jnp.einsum("bhqd,bhkd->bhqk", qb, kp).astype(jnp.float32) * scale
        s = s + (cum_logf[:, :, q0:q1, None] - cum_logf[:, :, None, :q1])
        t_idx = jnp.arange(q0, q1)[:, None]
        s_idx = jnp.arange(q1)[None, :]
        s = jnp.where(s_idx <= t_idx, s, -jnp.inf)
        p = jax.nn.softmax(s, axis=-1).astype(v.dtype)
        outs.append(jnp.einsum("bhqk,bhkd->bhqd", p, vp))
    return jnp.concatenate(outs, axis=2)

def _trailing_mean_minus_self(u, window):
    L = u.shape[1]
    cs = jnp.concatenate([jnp.zeros_like(u[:, :1]), jnp.cumsum(u, axis=1)], axis=1)
    t = jnp.arange(L)
    lo = jnp.maximum(t + 1 - window, 0)
    total = cs[:, 1:] - cs[:, lo]
    count = (t + 1 - lo).astype(jnp.float32)[None, :, None]
    return total / count - u

def _layer(h, norm1_w, w_in, b_fgate, q_norm_w, k_norm_w, w_pool, pool_scale,
           w_out, norm2_w, w_gate, w_up, w_down):
    B, L, _ = h.shape
    n1 = _rmsnorm(h, norm1_w)
    proj = n1 @ w_in.astype(h.dtype)
    q, k, v, fg, u = jnp.split(
        proj, [D_ATTN, 2 * D_ATTN, 3 * D_ATTN, 3 * D_ATTN + N_HEADS], axis=-1)

    q = _rmsnorm(q.reshape(B, L, N_HEADS, HEAD_DIM), q_norm_w).transpose(0, 2, 1, 3)
    k = _rmsnorm(k.reshape(B, L, N_HEADS, HEAD_DIM), k_norm_w).transpose(0, 2, 1, 3)
    v = v.reshape(B, L, N_HEADS, HEAD_DIM).transpose(0, 2, 1, 3)
    log_f = jax.nn.log_sigmoid((fg + b_fgate.astype(fg.dtype)).astype(jnp.float32))
    cum_logf = jnp.cumsum(log_f.transpose(0, 2, 1), axis=-1)
    a_out = _forgetting_attention(q, k, v, cum_logf)
    a_out = a_out.transpose(0, 2, 1, 3).reshape(B, L, D_ATTN)

    u32 = u.astype(jnp.float32)
    pooled = jnp.stack(
        [_trailing_mean_minus_self(u32[..., g * POOL_GROUP_DIM:(g + 1) * POOL_GROUP_DIM], w)
         for g, w in enumerate(POOL_WINDOWS)], axis=2).astype(h.dtype)
    p_out = jnp.einsum("blgc,gcd->blgd", pooled, w_pool.astype(h.dtype)).reshape(B, L, D_POOL)
    p_out = p_out * pool_scale.astype(h.dtype)

    mix = jnp.concatenate([a_out, p_out], axis=-1) @ w_out.astype(h.dtype)
    h = h + mix

    n2 = _rmsnorm(h, norm2_w)
    ffn = (jax.nn.silu(n2 @ w_gate.astype(h.dtype)) * (n2 @ w_up.astype(h.dtype))) @ w_down.astype(h.dtype)
    return h + ffn

def second_inputs(seed: int = 0) -> dict:
    key = jax.random.key(seed)
    ks = jax.random.split(key, 16)
    x = jax.random.normal(ks[0], (BATCH, SEQ, D_MODEL), jnp.float32)
    meta_tokens = jax.random.normal(ks[1], (N_META, D_MODEL), jnp.float32)
    norm1_w = 1.0 + 0.05 * jax.random.normal(ks[2], (DEPTH_2, D_MODEL), jnp.float32)
    w_in = jax.random.normal(ks[3], (DEPTH_2, D_MODEL, D_IN), jnp.float32) * D_MODEL ** -0.5
    w_in = w_in.at[:, :, 3 * D_ATTN:3 * D_ATTN + N_HEADS].multiply(0.1)
    b_fgate = 2.0 + 2.0 * jax.random.uniform(ks[4], (DEPTH_2, N_HEADS), jnp.float32)
    q_norm_w = 1.0 + 0.05 * jax.random.normal(ks[5], (DEPTH_2, HEAD_DIM), jnp.float32)
    k_norm_w = 1.0 + 0.05 * jax.random.normal(ks[6], (DEPTH_2, HEAD_DIM), jnp.float32)
    w_pool = jax.random.normal(ks[7], (DEPTH_2, N_POOL_GROUPS, POOL_GROUP_DIM, POOL_GROUP_DIM),
                               jnp.float32) * POOL_GROUP_DIM ** -0.5
    pool_scale = 1.0 + 0.1 * jax.random.normal(ks[8], (DEPTH_2, D_POOL), jnp.float32)
    w_out = jax.random.normal(ks[9], (DEPTH_2, D_MIX, D_MODEL), jnp.float32) * D_MIX ** -0.5
    norm2_w = 1.0 + 0.05 * jax.random.normal(ks[10], (DEPTH_2, D_MODEL), jnp.float32)
    w_gate = jax.random.normal(ks[11], (DEPTH_2, D_MODEL, D_FF), jnp.float32) * D_MODEL ** -0.5
    w_up = jax.random.normal(ks[12], (DEPTH_2, D_MODEL, D_FF), jnp.float32) * D_MODEL ** -0.5
    w_down = jax.random.normal(ks[13], (DEPTH_2, D_FF, D_MODEL), jnp.float32) * D_FF ** -0.5
    return {"x": x, "meta_tokens": meta_tokens, "norm1_w": norm1_w, "w_in": w_in,
            "b_fgate": b_fgate, "q_norm_w": q_norm_w, "k_norm_w": k_norm_w,
            "w_pool": w_pool, "pool_scale": pool_scale, "w_out": w_out,
            "norm2_w": norm2_w, "w_gate": w_gate, "w_up": w_up, "w_down": w_down}

def second_block(x, meta_tokens, norm1_w, w_in, b_fgate, q_norm_w, k_norm_w, w_pool,
              pool_scale, w_out, norm2_w, w_gate, w_up, w_down):
    B = x.shape[0]
    meta = jnp.broadcast_to(meta_tokens.astype(x.dtype)[None], (B, N_META, D_MODEL))
    h = jnp.concatenate([meta, x], axis=1)
    for layer in range(DEPTH_2):
        h = _layer(h, norm1_w[layer], w_in[layer], b_fgate[layer], q_norm_w[layer],
                   k_norm_w[layer], w_pool[layer], pool_scale[layer], w_out[layer],
                   norm2_w[layer], w_gate[layer], w_up[layer], w_down[layer])
    return h[:, N_META:]


def setup_inputs(seed=0):
    out = dict(first_inputs(seed))
    for name, value in second_inputs(seed + 1).items():
        if name != "x":
            out[name + "_2"] = value
    return out


def reference(
    x, mem, g_mix, g_ffn, g_mem, w_mem_kv, w_up, conv_w, conv_b, w_down, a_w_in, a_w_alpha,
    a_b_alpha, a_g_head, a_w_out, g_kv, w_kv, pe_k, pe_v, w_ck1, w_ck2, w_cv1, w_cv2, b_w_in,
    b_w_out, g_final, meta_tokens_2, norm1_w_2, w_in_2, b_fgate_2, q_norm_w_2, k_norm_w_2,
    w_pool_2, pool_scale_2, w_out_2, norm2_w_2, w_gate_2, w_up_2, w_down_2,
):
    x = first_block(
        x, mem, g_mix, g_ffn, g_mem, w_mem_kv, w_up, conv_w, conv_b, w_down, a_w_in, a_w_alpha,
        a_b_alpha, a_g_head, a_w_out, g_kv, w_kv, pe_k, pe_v, w_ck1, w_ck2, w_cv1, w_cv2,
        b_w_in, b_w_out, g_final,
    )
    return second_block(
        x, meta_tokens_2, norm1_w_2, w_in_2, b_fgate_2, q_norm_w_2, k_norm_w_2, w_pool_2,
        pool_scale_2, w_out_2, norm2_w_2, w_gate_2, w_up_2, w_down_2,
    )


_drawn_inputs = setup_inputs


def setup_inputs(seed=0):
    import zlib

    import numpy as np

    out = dict(_drawn_inputs(seed))
    spreads = {}
    factors = {'g_mem': 8.0,
     'conv_b': 7.468,
     'a_b_alpha': 8.0,
     'a_g_head': 5.127,
     'g_kv': 8.0,
     'pe_k': 8.0,
     'pe_v': 2.681,
     'q_norm_w_2': 6.156,
     'k_norm_w_2': 8.0}
    for name, (base, spread) in spreads.items():
        noise = np.random.default_rng([zlib.crc32(name.encode()), seed]).standard_normal(out[name].shape)
        drawn = base * np.exp(spread * noise) if base else spread * noise
        out[name] = __import__('jax').numpy.asarray(drawn.astype(out[name].dtype))
    for name, factor in factors.items():
        out[name] = (out[name] * factor).astype(out[name].dtype)
    return out
```

```python
import numpy as np

import concourse.bass as bass
from concourse import mybir
from contextlib import ExitStack

F32 = mybir.dt.float32
F32R = mybir.dt.float32r
U32 = mybir.dt.uint32
ALU = mybir.AluOpType
ACT = mybir.ActivationFunctionType
AX = mybir.AxisListType
EPS = 1e-6
NEG = -1.0e30

D = 1024
T = 256
NM = 16
TM = T + NM
NF = 22
UW = 2048
LEVELS = [64, 32, 16, 8, 4, 2, 1, 0]


def unit_names():
    up = lambda tag: [f"{tag}u0", f"{tag}u1"] + [
        n for p in range(1, 11) for n in (f"{tag}u{2 * p}", f"{tag}u{2 * p + 1}", f"{tag}d{p - 1}")
    ] + [f"{tag}d10"]
    return (
        ["Aq", "Ak", "m0k0", "m0k1", "m0v0", "m0v1", "Av0", "Av1", "Ar0", "Ar1", "Am0", "Am1",
         "m1k0", "m1k1", "m1v0", "m1v1", "Ao0", "Ao1", "Ao2", "Ao3"]
        + up("f0")
        + ["kvc", "kvk", "kvv", "ck0", "ck1", "cv0", "cv1", "Bm0", "Bm1", "Bq0", "Bq1",
           "Bo0", "Bo1", "Bo2", "Bo3"]
        + up("f1")
        + ["Cq0", "Cq1", "Ck0", "Ck1", "Cv0", "Cv1", "Cu0", "Cu1", "Co0", "Co1", "Co2", "Co3"]
        + up("f2")
    )


RAW = {"ck0", "ck1", "cv0", "cv1"}

SMALL = [
    ("gmix0", 8), ("gmix1", 8), ("gffn0", 8), ("gffn1", 8), ("gmem0", 8), ("gmem1", 8),
    ("gkv", 8), ("gfin", 8), ("n1", 8), ("n2", 8), ("ghead", 1), ("pscale", 4), ("qn", 1),
    ("kn", 1), ("bfg", 8), ("pek", 16), ("pev", 16), ("cw0", 66), ("cw1", 66), ("cb0", 22),
    ("cb1", 22), ("walr", 128), ("wgl", 192), ("wfg", 64), ("balpha", 256), ("walpha", 256),
    ("wck2", 128), ("wcv2", 128), ("wpool", 512),
]
CONST = [
    ("ident", 128), ("ones", 128), ("half", 128), ("tri", 128), ("one2", 128), ("trim", TM),
    ("mask2", TM), ("sel", 8 * 128), ("valid", 2), ("eps", 1), ("one", 1),
]
NSAC = [("alibi", 8 * 256), ("cmpb", 8 * 32)]


def columns(table):
    at, out = 0, {}
    for name, n in table:
        out[name] = (at, n)
        at += n
    return out, at


SM, NSM = columns(SMALL)
CN, NCN = columns(CONST)
NS, NNS = columns(NSAC)


class Queue:

    def __init__(self, eng, sem):
        self.eng, self.sem, self.n, self.past, self.last = eng, sem, 0, {}, None

    def wait(self, *toks):
        for t in toks:
            if t is None:
                continue
            if isinstance(t, list):
                self.wait(*t)
                continue
            sem, v = t
            if self.past.get(id(sem), 0) < v:
                self.past[id(sem)] = v
                self.eng.wait_ge(sem, v)

    def do(self, f, *toks):
        self.wait(*toks)
        self.n += 1
        self.last = f(self.eng).then_inc(self.sem, 1)
        return (self.sem, self.n)

    def quiet(self, f, *toks):
        self.wait(*toks)
        self.last = f(self.eng)

    def mark(self):
        self.last.then_inc(self.sem, 1)
        self.n += 1
        return (self.sem, self.n)


def build(nc, w_d, x_d, mem_d, meta_d, small_d, const_d, gmask_d, nsac_d, out_d):
    ctx = ExitStack()
    with ctx:
        def sb(name, cols, dt=F32):
            return ctx.enter_context(nc.sbuf_tensor(name, [128, cols], dt))

        def sem(name):
            return ctx.enter_context(nc.semaphore(name))

        PE = Queue(nc.tensor, sem("s_pe"))
        ACTE = Queue(nc.scalar, sem("s_act"))
        DVE = Queue(nc.vector, sem("s_dve"))
        SP = Queue(nc.sync, sem("s_sp"))

        NR, NH, AHEAD = 3, 3, 2
        raw = sb("raw", NR * UW)
        wh = sb("wh", NH * UW, F32R)
        wl = sb("wl", NH * UW, F32R)
        xt_ = sb("xt", 8 * T)
        xh_ = sb("xh", 8 * TM, F32R)
        xl_ = sb("xl", 8 * TM, F32R)
        coh_ = sb("coh", 8 * T, F32R)
        col_ = sb("col", 8 * T, F32R)
        memkv = sb("memkv", 4 * 1024)
        small = sb("small", NSM)
        smh = sb("smh", 384, F32R)
        sml = sb("sml", 384, F32R)
        cst = sb("cst", NCN)
        ARW = 12000
        arena = sb("arena", ARW)
        fh_ = sb("fh", 4 * T, F32R)
        fl_ = sb("fl", 4 * T, F32R)
        rs_ = sb("rs", TM)
        rst_ = sb("rst", 4)
        banks = [ctx.enter_context(nc.psum_tensor(f"ps{i}", [128, 512], F32)) for i in range(8)]

        v3 = lambda ap, n: ap.rearrange("p (a b) -> p a b", b=n)
        xt = v3(xt_[:, :], T)
        xh, xl = v3(xh_[:, :], TM), v3(xl_[:, :], TM)
        coh, col = v3(coh_[:, :], T), v3(col_[:, :], T)
        f32 = lambda ap: ap.bitcast(F32)

        def sm(name, a=0, b=None):
            at, n = SM[name]
            return small[:, at + a:at + (n if b is None else b)]

        def cn(name, a=0, b=None):
            at, n = CN[name]
            return cst[:, at + a:at + (n if b is None else b)]

        at_ = [0]

        def area(n):
            at_[0] += n
            assert at_[0] <= ARW, at_[0]
            return arena[:, at_[0] - n:at_[0]]

        def load(dst, src, s, *toks):
            SP.wait(*toks)
            SP.quiet(lambda e: e.dma_start(dst, src).then_inc(s, 16))
            return (s, 16)

        memT_ = area(8 * T)
        memT = v3(memT_, T)
        t_small = load(small[:, :], small_d, sem("d_small"))
        t_x = load(xt_[:, :], x_d, sem("d_x"))

        names = unit_names()
        ring_sem = [sem(f"d_w{i}") for i in range(NR)]

        class Stream:

            dma_n = split_n = got = hslots = 0
            raw_free = {}
            part_free = {}
            landed = {}
            parts = {}

            def fetch(self):
                i = self.dma_n
                if i >= len(names) or (i >= NR and (i - NR) not in self.raw_free):
                    return
                s = ring_sem[i % NR]
                SP.wait(self.raw_free.get(i - NR))
                dst = raw[:, (i % NR) * UW:(i % NR + 1) * UW]
                SP.quiet(lambda e: e.dma_start(dst, w_d[i]).then_inc(s, 16))
                self.landed[i] = (s, 16 * (i // NR + 1))
                self.dma_n += 1
                self.fetch()

            def split(self):
                i = self.split_n
                self.split_n += 1
                src = raw[:, (i % NR) * UW:(i % NR + 1) * UW]
                if names[i] in RAW:
                    self.parts[i] = (src, None, None)
                    return
                k = self.hslots
                self.hslots += 1
                free = self.part_free[k - NH] if k >= NH else None
                H = wh[:, (k % NH) * UW:(k % NH + 1) * UW]
                L = wl[:, (k % NH) * UW:(k % NH + 1) * UW]
                hw = UW // 2
                tl = []
                for a in (0, hw):
                    th = ACTE.do(lambda e, a=a: e.copy(H[:, a:a + hw], src[:, a:a + hw]), self.landed[i], free)
                    tl.append(DVE.do(lambda e, a=a: e.tensor_tensor(
                        L[:, a:a + hw], src[:, a:a + hw], f32(H[:, a:a + hw]), ALU.subtract),
                        self.landed[i], free, th))
                self.raw_free[i] = tl[1]
                self.parts[i] = (H, L, tl, k)
                self.fetch()

            def get(self, name):
                i = self.got
                self.got += 1
                assert names[i] == name, (names[i], name)
                while self.split_n <= min(i + AHEAD, len(names) - 1):
                    if self.split_n > i and self.split_n >= self.dma_n:
                        break
                    self.split()
                return i, self.parts[i]

            def release(self, i, tok):
                p = self.parts[i]
                if p[1] is None:
                    self.raw_free[i] = tok
                    self.fetch()
                else:
                    self.part_free[p[3]] = tok

        W = Stream()
        W.fetch()
        t_mem = load(memT_, mem_d, sem("d_mem"))
        t_cst = load(cst[:, :], const_d, sem("d_cst"))
        for _ in range(NR - 1):
            W.fetch()

        free = [None] * 8
        turn = {"A": [0, 1, 2, 3], "B": [4, 5, 6, 7]}

        def bank(ring):
            b = turn[ring].pop(0)
            turn[ring].append(b)
            assert free[b] != "held", b
            PE.wait(free[b])
            free[b] = "held"
            return b, banks[b]

        def mm(out, lhsT, rhs, start, stop, *toks, skip=False):
            PE.quiet(lambda e: e.matmul(out, lhsT, rhs, start=start, stop=stop, skip_group_check=skip), *toks)

        def mark():
            return PE.mark()

        def mm3(out, wH, wL, XH, XL, start, stop, *toks, skip=False):
            mm(out, wH, XH, start, False, *toks, skip=skip)
            mm(out, wH, XL, False, False, skip=skip)
            mm(out, wL, XH, False, stop, skip=skip)

        def V(f, *t):
            return DVE.do(f, *t)

        def A(f, *t):
            return ACTE.do(f, *t)

        def split_x(src, g, H, L, *toks, war=None):
            th = A(lambda e: e.activation(H, src, ACT.Copy, scale=g), war, *toks)
            return V(lambda e: e.scalar_tensor_tensor(L, src, g, f32(H), ALU.mult, ALU.subtract), th, war, *toks)

        def rsqrt(dst, src_ps, n, scale, tmp, *toks):
            va, ta = tmp[:, 0:n], tmp[:, n:2 * n]
            t0 = V(lambda e: e.tensor_scalar(va, src_ps, scale, EPS, ALU.mult, ALU.add), *toks)
            t1 = A(lambda e: e.activation(ta, va, ACT.Ln), t0, *toks)
            t2 = A(lambda e: e.activation(dst, ta, ACT.Exp, scale=-0.5), t1)
            t3 = V(lambda e: e.tensor_tensor(ta, dst, dst, ALU.mult), t2)
            t4 = V(lambda e: e.tensor_tensor(ta, ta, va, ALU.mult), t3)
            t5 = V(lambda e: e.tensor_scalar(ta, ta, -0.5, 1.5, ALU.mult, ALU.add), t4)
            t6 = V(lambda e: e.tensor_tensor(dst, dst, ta, ALU.mult), t5)
            return t0, t6

        sqb = area(2 * TM)
        sq2 = [sqb[:, 0:TM], sqb[:, TM:2 * TM]]
        sq_free = [None, None]
        nt = area(2 * TM)

        def sumsq(srcs, toks, w, ring="B"):
            b, P = bank(ring)
            for c in range(8):
                s = sq2[c % 2][:, 0:w]
                t = A(lambda e, c=c, s=s: e.activation(s, srcs[c], ACT.Square), toks[c], sq_free[c % 2])
                mm(P[:, 0:w], cn("ones"), s, c == 0, c == 7, t, t_cst)
                sq_free[c % 2] = mark()
            return b, P, sq_free[1]

        def rows_to_tokens(dst, row, nt_, tok, w0=0):
            b, P = bank("B")
            for i in range(nt_):
                mm(P[:, i:i + 1], row[0:1, w0 + i * 128:w0 + (i + 1) * 128], cn("one")[0:1, :], True, True, tok, t_cst)
            t = mark()
            t2 = V(lambda e: e.tensor_copy(dst, P[:, 0:nt_]), t)
            free[b] = t2
            return t2

        def projF(name, XH, XL, xtoks, out_w, ring="A"):
            i, (H, L, tl, k) = W.get(name)
            H3, L3 = v3(H, 256), v3(L, 256)
            res = []
            if out_w <= 256:
                b, P = bank(ring)
            for j in range(2):
                if out_w > 256:
                    b, P = bank(ring)
                    O = P[:, 0:out_w]
                else:
                    O = P[:, j * 256:j * 256 + out_w]
                for c in range(8):
                    mm3(O, H3[:, c, j * 128:(j + 1) * 128], L3[:, c, j * 128:(j + 1) * 128],
                        XH(c), XL(c), c == 0, c == 7, xtoks[c], tl[c // 4])
                if out_w > 256:
                    res.append((b, P, mark()))
            if out_w <= 256:
                res.append((b, P, mark()))
            W.release(i, res[-1][2])
            return res

        def projT(name, XH, XL, xtoks, tiles, ring="A"):
            i, (H, L, tl, k) = W.get(name)
            H3, L3 = v3(H, 256), v3(L, 256)
            res = []
            for n, a in enumerate(tiles):
                if n % 2 == 0:
                    b, P = bank(ring)
                O = P[:, (n % 2) * 256:(n % 2) * 256 + 256]
                for c in range(8):
                    mm(O, XH(c)[:, a:a + 128], H3[:, c, :], c == 0, False, xtoks[c], tl[c // 4])
                    mm(O, XL(c)[:, a:a + 128], H3[:, c, :], False, False)
                    mm(O, XH(c)[:, a:a + 128], L3[:, c, :], False, c == 7)
                if n % 2 == 1 or n == len(tiles) - 1:
                    res.append((b, P, mark()))
            W.release(i, res[-1][2])
            return res

        def bc2(ap, n=2):
            return ap.unsqueeze(1).broadcast_to([128, n, ap.shape[-1]])

        X = lambda c: xh[:, c, NM:TM]
        XLo = lambda c: xl[:, c, NM:TM]

        def enter(srcs, toks, g, war, sums=True):
            xt_tok = []
            for c in range(8):
                xt_tok.append(split_x(srcs[c], sm(g, c, c + 1), X(c), XLo(c), toks[c], t_small, war=war))
            return xt_tok

        def token_rstd(srcs, toks, w, war):
            b, P, t = sumsq(srcs, toks, w)
            t0, t6 = rsqrt(rs_[:, 0:w], P[:, 0:w], w, 1.0 / D, nt, t, war)
            free[b] = t0
            return t6

        at0 = SM["walr"][0]
        t = A(lambda e: e.copy(smh[:, :], small[:, at0:at0 + 384]), t_small)
        t_sml = V(lambda e: e.tensor_tensor(sml[:, :], small[:, at0:at0 + 384], f32(smh[:, :]), ALU.subtract), t)

        def softplus_neg(dst, z, w, tok, tmpa, tmpb):
            t1 = A(lambda e: e.activation(tmpa, z, ACT.Abs), tok)
            t2 = A(lambda e: e.activation(tmpb, tmpa, ACT.Exp, scale=-1.0), t1)
            t3 = A(lambda e: e.activation(tmpa, tmpb, ACT.Ln, bias=cn("one")), t2, t_cst)
            return V(lambda e: e.scalar_tensor_tensor(dst, z, 0.0, tmpa, ALU.min, ALU.subtract), t3)

        xs = [xt[:, c, :] for c in range(8)]
        ms = [memT[:, c, :] for c in range(8)]
        xtok = enter(xs, [t_x] * 8, "gmix0", None)
        t_rs = token_rstd(xs, [t_x] * 8, T, None)
        mrs = area(T)
        mrst = area(2)
        MH = lambda c: coh[:, c, :]
        ML = lambda c: col[:, c, :]

        def enter_mem(g, war):
            return [split_x(ms[c], sm(g, c, c + 1), MH(c), ML(c), t_mem, t_small, war=war) for c in range(8)]

        alrT = area(256)

        b, P = bank("A")
        for c in range(8):
            a = c * 16
            mm3(P[:, 0:T], smh[:, a:a + 128], sml[:, a:a + 128], X(c), XLo(c), c == 0, c == 7, xtok[c], t_sml)
        t = mark()
        t_alr = V(lambda e: e.tensor_tensor(alrT[0:16, :], P[0:16, 0:T], rs_[0:16, 0:T], ALU.mult), t, t_rs)
        free[b] = t_alr
        t_rst = rows_to_tokens(rst_[:, 0:2], rs_, 2, t_rs)

        qkb = area(1024)
        q_, k_ = qkb[:, 0:512], qkb[:, 512:1024]
        qk_tok = []
        for nm, dst, scl in (("Aq", q_, 0.125), ("Ak", k_, 1.0)):
            (b, P, t), = projF(nm, X, XLo, xtok, T)
            t = V(lambda e, dst=dst, P=P, scl=scl: e.scalar_tensor_tensor(
                v3(dst, T), v3(P[:, :], T), scl, bc2(rs_[:, 0:T]), ALU.mult, ALU.mult), t, t_rs)
            free[b] = t
            qk_tok.append(t)

        la = area(512)
        b, P = bank("B")
        for i in range(2):
            mm(P[:, i * 256:(i + 1) * 256], alrT[0:16, i * 128:(i + 1) * 128], sm("walpha")[0:16, :], True, True, t_alr)
        t = mark()
        t = V(lambda e: e.tensor_tensor(v3(la, 256), v3(P[:, :], 256), bc2(sm("balpha")), ALU.add), t, t_small)
        free[b] = t
        ea = area(512)
        eb = area(512)
        t_la = softplus_neg(la, la, 512, t, ea, eb)
        b_ = area(512)
        b, P = bank("B")
        for dt in range(2):
            for i in range(2):
                mm(P[:, (dt * 2 + i) * 128:(dt * 2 + i + 1) * 128], la[:, i * 256 + dt * 128:i * 256 + dt * 128 + 128],
                   cn("tri"), True, True, t_la, t_cst)
        t = mark()
        t_b = V(lambda e: e.tensor_scalar(b_, P[:, :], 1.0 / 16, None, ALU.mult), t)
        free[b] = t_b

        mtok = enter_mem("gmem0", None)
        bm, Pm, t = sumsq(ms, [t_mem] * 8, T)
        t0, t_mrs = rsqrt(mrs, Pm[:, 0:T], T, 1.0 / D, nt, t)
        free[bm] = t0
        t_mrst = rows_to_tokens(mrst, mrs, 2, t_mrs)

        mem_tok = {}
        mk = lambda l: v3(memkv[:, l * 2048:l * 2048 + 1024], T)
        mv = lambda l: v3(memkv[:, l * 2048 + 1024:l * 2048 + 2048], 512)

        def mem_unit(l, kind, j, mtok):
            if kind == "k":
                (b, P, t), = projF(f"m{l}k{j}", MH, ML, mtok, T)
                t2 = V(lambda e: e.tensor_tensor(mk(l)[:, 2 * j:2 * j + 2, :], v3(P[:, :], T), bc2(mrs), ALU.mult), t, t_mrs)
                free[b] = t2
            else:
                (b, P, t), = projT(f"m{l}v{j}", MH, ML, mtok, [0, 128])
                for i in range(2):
                    t2 = V(lambda e, i=i: e.tensor_scalar(mv(l)[:, i, j * 256:(j + 1) * 256], P[:, i * 256:(i + 1) * 256],
                                                          mrst[:, i:i + 1], None, ALU.mult), t, t_mrst)
                free[b] = t2
            mem_tok.setdefault(l, []).append(t2)
            return t

        mem_unit(0, "k", 0, mtok)
        mem_unit(0, "k", 1, mtok)

        gm = area(1024)
        t_gm = load(gm, gmask_d, sem("d_gm"))
        v_ = area(1024)
        v4 = v3(v_, 512)
        AT_ = area(1024)
        ATo = area(512)
        t_at0 = V(lambda e: e.memset(AT_, 0.0))
        E_, Q_, K_ = ea, eb, area(512)
        lev = {"t": t_at0, "pe": None}

        def level(li):
            m = LEVELS[li]
            if m:
                bv = b_.rearrange("p (a c) -> p a c", c=2 * m)
                ev = E_.rearrange("p (a c) -> p a c", c=2 * m)
                t = V(lambda e: e.tensor_tensor(ev, bv, bv[:, :, m - 1:m].broadcast_to([128, 512 // (2 * m), 2 * m]),
                                                ALU.subtract), t_b)
                t = A(lambda e: e.activation(E_, E_, ACT.Abs), t)
                t = A(lambda e: e.activation(E_, E_, ACT.Exp, scale=-1.0), t)
                ta = V(lambda e: e.tensor_tensor(Q_, q_, E_, ALU.mult), t, qk_tok[0], lev["pe"])
                tb = V(lambda e: e.tensor_tensor(K_, k_, E_, ALU.mult), t, qk_tok[1], lev["pe"])
                QQ, KK, tt = Q_, K_, [ta, tb]
            else:
                QQ, KK, tt = q_, k_, qk_tok
            for half in range(2):
                b, P = bank("B")
                r = half * 64
                for hh in range(2):
                    for i in range(2):
                        s = (hh * 2 + i) * 128
                        mm(P[:, (hh * 2 + i) * 128:(hh * 2 + i + 1) * 128], KK[r:r + 64, s:s + 128],
                           QQ[r:r + 64, s:s + 128], True, True, tt)
                t = mark()
                mask = gm[:, li * 128:(li + 1) * 128].bitcast(U32)
                t2 = V(lambda e, half=half, P=P: e.copy_predicated(
                    v3(AT_[:, half * 512:(half + 1) * 512], 128), bc2(mask, 4), v3(P[:, :], 128)), t, t_gm, lev["t"])
                free[b] = t2
            lev["pe"] = t
            lev["t"] = t2

        t = mem_unit(0, "v", 0, mtok)
        level(0)
        level(1)
        t_mpe = mem_unit(0, "v", 1, mtok)
        mtok1 = enter_mem("gmem1", t_mpe)

        v_tok = []
        for j in range(2):
            (b, P, t), = projT(f"Av{j}", X, XLo, xtok, [0, 128])
            for i in range(2):
                t2 = V(lambda e, i=i, P=P, j=j: e.tensor_scalar(v4[:, i, j * 256:(j + 1) * 256], P[:, i * 256:(i + 1) * 256],
                                                                rst_[:, i:i + 1], None, ALU.mult), t, t_rst)
            free[b] = t2
            v_tok.append(t2)
            level(2 + j)
        tmpo, r_ = memT_[:, 0:1024], memT_[:, 1024:2048]
        r_tok = []
        for j in range(2):
            (b, P, t), = projF(f"Ar{j}", X, XLo, xtok, T)
            t = V(lambda e, j=j, P=P: e.tensor_tensor(v3(r_[:, j * 512:(j + 1) * 512], T), v3(P[:, :], T),
                                                      bc2(rs_[:, 0:T]), ALU.mult), t, t_rs, mtok1)
            free[b] = t
            r_tok.append(t)
            level(4 + 2 * j)
            level(5 + 2 * j)
        mq_ = area(1024)
        mq = v3(mq_, T)
        mq_tok = []
        for j in range(2):
            (b, P, t), = projF(f"Am{j}", X, XLo, xtok, T)
            t = V(lambda e, j=j, P=P: e.scalar_tensor_tensor(mq[:, 2 * j:2 * j + 2, :], v3(P[:, :], T), 128.0 ** -0.5,
                                                             bc2(rs_[:, 0:T]), ALU.mult, ALU.mult), t, t_rs)
            free[b] = t
            mq_tok.append(t)
        Eo = E_
        t_on = [None] * 4
        tq = []
        for dt in range(2):
            s0, s1 = (dt * 2) * 128, (dt * 2 + 1) * 128
            t = A(lambda e, s0=s0: e.activation(Eo[:, s0:s0 + 128], b_[:, s0:s0 + 128], ACT.Exp, scale=-1.0,
                                                bias=b_[:, s0 + 127:s0 + 128]), t_b, lev["t"])
            t2 = A(lambda e, s1=s1: e.activation(Eo[:, s1:s1 + 128], b_[:, s1:s1 + 128], ACT.Exp), t_b)
            t3 = V(lambda e, s0=s0: e.tensor_tensor(K_[:, s0:s0 + 128], k_[:, s0:s0 + 128], Eo[:, s0:s0 + 128], ALU.mult),
                   t, lev["pe"])
            t4 = V(lambda e, s1=s1: e.tensor_tensor(Q_[:, s1:s1 + 128], q_[:, s1:s1 + 128], Eo[:, s1:s1 + 128], ALU.mult),
                   t2, lev["pe"])
            tq += [t3, t4]
        for r in (0, 64):
            b, P = bank("B")
            for dt in range(2):
                mm(P[:, dt * 128:(dt + 1) * 128], K_[r:r + 64, dt * 256:dt * 256 + 128],
                   Q_[r:r + 64, dt * 256 + 128:dt * 256 + 256], True, True, tq)
            t = mark()
            t_ao = V(lambda e: e.tensor_copy(ATo[:, r * 4:r * 4 + 256], P[:, 0:256]), t)
            free[b] = t_ao

        mem_unit(1, "k", 0, mtok1)
        AT4 = v3(AT_, 128)
        ob = []
        for half in range(2):
            b, P = bank("B")
            for hh in range(2):
                h = half * 2 + hh
                vc = lambda i: v4[:, i, h * 128:(h + 1) * 128]
                ha = (h % 2) * 4 + h // 2 * 2
                ho = (h % 2) * 256 + h // 2 * 128
                mm(P[:, hh * 256:hh * 256 + 128], vc(0), AT4[:, ha, :], True, True, lev["t"], t_ao, v_tok)
                mm(P[:, hh * 256 + 128:hh * 256 + 256], vc(0), ATo[:, ho:ho + 128], True, False)
                mm(P[:, hh * 256 + 128:hh * 256 + 256], vc(1), AT4[:, ha + 1, :], False, True)
            ob.append((b, P, mark()))
        mem_unit(1, "k", 1, mtok1)
        so = AT_
        ro = E_
        gated = []
        nbs = []
        t_sr = A(lambda e: e.activation(v_, r_, ACT.Silu), r_tok, ob[1][2])
        for half in range(2):
            b, P, t = ob[half]
            sqh = so[:, half * 512:(half + 1) * 512]
            t = A(lambda e, P=P, sqh=sqh: e.activation(sqh, P[:, :], ACT.Square), t, ob[1][2])
            b2, P2 = bank("B")
            mm(P2[:, :], cn("ones"), sqh, True, True, t)
            nbs.append((b2, P2, mark(), t))
        mem_unit(1, "v", 0, mtok1)
        co_war = None
        rtoks = []
        tprev = None
        for half in range(2):
            b2, P2, t, tsq = nbs[half]
            dstr = [ro, la][half]
            t0, t6 = rsqrt(dstr, P2[:, :], 512, 1.0 / 128, tmpo, t, tq, tprev)
            free[b2] = t0
            tprev = t6
            rtoks.append((dstr, t6))
        t_m1 = mem_unit(1, "v", 1, mtok1)
        co_tok = [None] * 8
        for half in range(2):
            b, P, t = ob[half]
            dstr, t6 = rtoks[half]
            o1 = tmpo[:, half * 512:half * 512 + 512]
            t7 = V(lambda e, P=P, dstr=dstr, o1=o1: e.scalar_tensor_tensor(o1, P[:, :], sm("ghead"), dstr, ALU.mult, ALU.mult),
                   t6, nbs[half][3], rtoks[1][1])
            free[b] = t7
            t8 = V(lambda e, o1=o1, half=half: e.tensor_tensor(o1, o1, v_[:, half * 512:half * 512 + 512], ALU.mult), t7, t_sr)
            dst = slice(half * 512, half * 512 + 512)
            t9 = A(lambda e, o1=o1, dst=dst: e.copy(coh_[:, dst], o1), t8, t_m1)
            t10 = V(lambda e, o1=o1, dst=dst: e.tensor_tensor(col_[:, dst], o1, f32(coh_[:, dst]), ALU.subtract), t9, t_m1)
            co_tok[2 * half] = co_tok[2 * half + 1] = t10

        def mem_attention(mq, mq_tok, l, S, sc, war):
            pt_pe = [war, war]
            for h in range(4):
                k = h % 2
                Eh, PT = S[:, k * 1024:k * 1024 + 512], S[:, k * 1024 + 512:k * 1024 + 1024]
                mx, su = sc[:, k * 6:k * 6 + 2], sc[:, k * 6 + 2:k * 6 + 4]
                b, P = bank("B")
                for i in range(2):
                    mm(P[:, i * 256:(i + 1) * 256], mq[:, h, i * 128:(i + 1) * 128], mk(l)[:, h, :], True, True,
                       mq_tok, mem_tok[l])
                t = mark()
                t1 = V(lambda e, P=P, mx=mx: e.tensor_reduce(mx, v3(P[:, :], 256), AX.X, ALU.max, negate=True), t, pt_pe[k])
                for i in range(2):
                    t2 = A(lambda e, P=P, i=i, Eh=Eh, mx=mx, su=su: e.activation(
                        Eh[:, i * 256:(i + 1) * 256], P[:, i * 256:(i + 1) * 256], ACT.Exp, bias=mx[:, i:i + 1],
                        accum_out=su[:, i:i + 1]), t1, pt_pe[k])
                free[b] = t2
                t3 = V(lambda e, su=su: e.reciprocal(su, su), t2)
                t4 = V(lambda e, Eh=Eh, su=su: e.tensor_tensor(v3(Eh, 256), v3(Eh, 256),
                                                               su.unsqueeze(2).broadcast_to([128, 2, 256]), ALU.mult), t3)
                b, P = bank("B")
                for mi in range(2):
                    for i in range(2):
                        o = P[:, mi * 256 + i * 128:mi * 256 + (i + 1) * 128]
                        src = Eh[:, i * 256 + mi * 128:i * 256 + (mi + 1) * 128]
                        PE.quiet(lambda e, o=o, src=src: e.transpose(o, src, cn("ident")), t4, t_cst)
                t5 = mark()
                t6 = A(lambda e, PT=PT, P=P: e.copy(PT, P[:, :]), t5)
                free[b] = t6
                b, P = bank("B")
                for mi in range(2):
                    mm(P[:, 0:T], mv(l)[:, mi, h * 128:(h + 1) * 128], PT[:, mi * 256:(mi + 1) * 256], mi == 0, mi == 1, t6)
                t7 = mark()
                pt_pe[k] = t7
                t8 = A(lambda e, h=h, P=P: e.copy(coh[:, 4 + h, :], P[:, 0:T]), t7, war)
                t9 = V(lambda e, h=h, P=P: e.tensor_tensor(col[:, 4 + h, :], P[:, 0:T], f32(coh[:, 4 + h, :]), ALU.subtract), t8)
                free[b] = t9
                co_tok[4 + h] = t9

        scb = area(12)
        mem_attention(mq, mq_tok, 0, memT_, scb, [t_m1, t10, mtok1[7], t_mpe])

        def out_proj(names4, g, next_norm=True):
            toks, xk = [], []
            for j, nm in enumerate(names4):
                (b, P, t), = projF(nm, lambda c: coh[:, c, :], lambda c: col[:, c, :], co_tok, T)
                t = V(lambda e, j=j, P=P: e.tensor_tensor(xt[:, 2 * j:2 * j + 2, :], v3(P[:, :], T),
                                                          xt[:, 2 * j:2 * j + 2, :], ALU.add), t)
                free[b] = t
                toks += [t, t]
                for c in (2 * j, 2 * j + 1):
                    xk.append(split_x(xs[c], sm(g, c, c + 1), X(c), XLo(c), t))
            return toks, xk

        def ffn(tag, xk, toks, cw, cb, g_next, last=False):
            acc = [banks[4 + o // 2][:, (o % 2) * 256:(o % 2) * 256 + 256] for o in range(8)]
            f_pe = [None] * 4
            units = {}
            ftok = {}
            y_free = [None, None]
            t_rs_box = [None]

            def up(p):
                work = []
                for j in range(2):
                    (b, P, t), = projF(f"{tag}u{2 * p + j}", X, XLo, xk, T)
                    work.append((j, b, P, t))
                return work

            def mix(p, work):
                t_rs = t_rs_box[0]
                for j, b, P, t in work:
                    f = 2 * p + j
                    s = f % 2
                    y, g2 = yb[s][:, 0:T], yb[s][:, T:2 * T]
                    rs = rs_[:, 0:T]
                    if cw is not None:
                        Ab = abuf[s]
                        w = lambda n: sm(cw, n * 22 + f, n * 22 + f + 1)
                        t1 = V(lambda e, P=P, Ab=Ab: e.tensor_tensor(Ab[:, 2:2 + T], P[:, 0:T], rs, ALU.mult),
                               t, t_rs, y_free[s], t_pad)
                        t2 = A(lambda e, Ab=Ab, w=w, y=y: e.activation(y, Ab[:, 0:T], ACT.Copy, scale=w(0)), t1, y_free[s])
                        t3 = V(lambda e, P=P, g2=g2: e.tensor_tensor(g2, P[:, T:2 * T], rs, ALU.mult), t, t_rs, y_free[s])
                        free[b] = t3
                        t4 = V(lambda e, Ab=Ab, w=w, y=y: e.scalar_tensor_tensor(y, Ab[:, 1:1 + T], w(1), y, ALU.mult, ALU.add), t2)
                        t5 = V(lambda e, Ab=Ab, w=w, y=y: e.scalar_tensor_tensor(y, Ab[:, 2:2 + T], w(2), y, ALU.mult, ALU.add), t4)
                        t6 = A(lambda e, y=y, f=f: e.activation(y, y, ACT.Silu, bias=sm(cb, f, f + 1)), t5)
                    else:
                        t1 = V(lambda e, P=P, y=y: e.tensor_tensor(y, P[:, 0:T], rs, ALU.mult), t, t_rs, y_free[s])
                        t3 = V(lambda e, P=P, g2=g2: e.tensor_tensor(g2, P[:, T:2 * T], rs, ALU.mult), t, t_rs, y_free[s])
                        free[b] = t3
                        t6 = A(lambda e, y=y: e.activation(y, y, ACT.Silu), t1)
                    t7 = V(lambda e, y=y, g2=g2: e.tensor_tensor(g2, y, g2, ALU.mult), t6, t3)
                    H, L = fh_[:, (f % 4) * T:(f % 4 + 1) * T], fl_[:, (f % 4) * T:(f % 4 + 1) * T]
                    t8 = A(lambda e, H=H, g2=g2: e.copy(H, g2), t7, f_pe[f % 4])
                    t9 = V(lambda e, H=H, L=L, g2=g2: e.tensor_tensor(L, g2, f32(H), ALU.subtract), t8, f_pe[f % 4])
                    y_free[s] = t9
                    ftok[f] = t9

            def down(p):
                i, (H, L, tl, _) = W.get(f"{tag}d{p}")
                H, L = v3(H, 1024), v3(L, 1024)
                if p == 0:
                    for b in range(4, 8):
                        assert free[b] != "held"
                        PE.wait(free[b])
                        free[b] = "held"
                marks = []
                for j in range(2):
                    f = 2 * p + j
                    FH, FL = fh_[:, (f % 4) * T:(f % 4 + 1) * T], fl_[:, (f % 4) * T:(f % 4 + 1) * T]
                    for o in range(8):
                        cs = slice(o * 128, (o + 1) * 128)
                        mm3(acc[o], H[:, j, cs], L[:, j, cs], FH, FL, f == 0 and o % 2 == 0, f == NF - 1,
                            ftok[f], tl[j], skip=True)
                        if f == NF - 1:
                            marks.append(mark())
                    f_pe[f % 4] = marks[-1] if f == NF - 1 else mark()
                W.release(i, f_pe[f % 4])
                return marks

            prev = up(0)
            t_rs_box[0] = token_rstd(xs, toks, T, None)
            mix(0, prev)
            for p in range(1, 11):
                w = up(p)
                down(p - 1)
                mix(p, w)
            marks = down(10)
            new = []
            for o in range(8):
                t = V(lambda e, o=o: e.tensor_tensor(xs[o], acc[o], xs[o], ALU.add), marks[o | 1])
                new.append(t)
                free[4 + o // 2] = t
            return new, marks[-1]

        toks, xk = out_proj(["Ao0", "Ao1", "Ao2", "Ao3"], "gffn0")
        yb_ = qkb
        yb = [yb_[:, 0:512], yb_[:, 512:1024]]
        ab_ = gm[:, 0:2 * (T + 2)]
        abuf = [ab_[:, 0:T + 2], ab_[:, T + 2:2 * (T + 2)]]
        V(lambda e: e.memset(abuf[0][:, 0:2], 0.0), toks[-1])
        t_pad = V(lambda e: e.memset(abuf[1][:, 0:2], 0.0))
        new, t_pe = ffn("f0", xk, toks, "cw0", "cb0", None)
        at_[0] = 0
        nsac = area(NNS)
        t_nsac = load(nsac, nsac_d, sem("d_nsac"), toks[-1])
        al = lambda h: nsac[:, h * 256:(h + 1) * 256]
        cb_ = lambda h: nsac[:, 2048 + h * 32:2048 + (h + 1) * 32]
        sqb = area(2 * TM)
        sq2[0], sq2[1] = sqb[:, 0:TM], sqb[:, TM:2 * TM]
        sq_free[0] = sq_free[1] = t_pe
        nt = area(2 * TM)
        xk = enter(xs, new, "gkv", t_pe)
        kvb = []
        for nm in ("kvc", "kvk"):
            kvb += projF(nm, X, XLo, xk, T)
        kvb += projT("kvv", X, XLo, xk, [0, 128])
        t_kvpe = kvb[-1][2]
        t_rs = token_rstd(xs, new, T, [new[-1]])
        t_rst = rows_to_tokens(rst_[:, 0:2], rs_, 2, t_rs)
        xk = enter(xs, new, "gmix1", t_kvpe)
        kc = area(512)
        kk = area(512)
        vv = area(512)
        ktoks = []
        for dst, (b, P, t) in zip((kc, kk), kvb[:2]):
            t = V(lambda e, dst=dst, P=P: e.tensor_tensor(v3(dst, T), v3(P[:, :], T), bc2(rs_[:, 0:T]), ALU.mult), t, t_rs)
            free[b] = t
            ktoks.append(t)
        b, P, t = kvb[2]
        for i in range(2):
            t2 = V(lambda e, P=P, i=i: e.tensor_scalar(vv[:, i * 256:(i + 1) * 256], P[:, i * 256:(i + 1) * 256],
                                                       rst_[:, i:i + 1], None, ALU.mult), t, t_rst)
        free[b] = t2
        t_vv = t2
        cblk = area(1984)
        X2, ev = cblk[:, 0:512], cblk[:, 512:1024]
        S1 = cblk[:, 0:1600]
        d_x2 = sem("d_x2")
        t_ev = V(lambda e: e.tensor_copy(ev.rearrange("p (v two m) -> p v m two", two=2, m=128),
                                         kc.rearrange("p (v m two) -> p v m two", two=2, m=128)), ktoks[0])
        for g in range(2):
            for par in range(2):
                src = ev.rearrange("p (v two m) -> p v two m", two=2, m=128)[g * 64:(g + 1) * 64, :, par, :]
                dst = X2.rearrange("p (v g m) -> p v g m", g=2, m=128)[par * 64:(par + 1) * 64, :, g, :]
                ACTE.quiet(lambda e, dst=dst, src=src: e.dma_start(dst, src).then_inc(d_x2, 16), t_ev)
        t_x2 = (d_x2, 64)
        R = [cblk[:, 1024:1504], cblk[:, 1504:1984]]
        r_t = []
        X2v = X2.rearrange("p (v g m) -> p v g m", g=2, m=128)
        for kv, pe_n in enumerate(("pek", "pev")):
            for g in range(2):
                if True:
                    Rv = R[kv].rearrange("p (c g n) -> p c g n", g=2, n=15)[:, :, g, :]
                    base = X2v[:, kv, g, :].rearrange("p (n c) -> p c n", c=8)
                    pe = sm(pe_n).unsqueeze(2)
                    for hf in range(2):
                        t = V(lambda e, Rv=Rv, base=base, pe=pe, hf=hf: e.tensor_tensor(
                            Rv[:, hf * 8:(hf + 1) * 8, :], base[:, :, hf:hf + 15],
                            pe[:, hf * 8:(hf + 1) * 8, :].broadcast_to([128, 8, 15]), ALU.add), t_x2)
            r_t.append(t)
        gT = area(120)
        for kv in range(2):
            b, P = bank("B")
            nm = "ck" if kv == 0 else "cv"
            for half in range(2):
                i, (src, _, _) = W.get(f"{nm}{half}")
                for hid in range(2):
                    for c in range(8):
                        cc = half * 8 + c
                        mm(P[:, hid * 32:hid * 32 + 30], v3(src, 256)[:, c, hid * 128:(hid + 1) * 128],
                           R[kv][:, cc * 30:(cc + 1) * 30], half == 0 and hid == 0 and c == 0,
                           half == 1 and c == 7, r_t[kv], W.landed[i], skip=True)
                W.release(i, mark())
            t = (PE.sem, PE.n)
            t = A(lambda e, kv=kv, P=P: e.activation(
                v3(gT[:, kv * 60:(kv + 1) * 60], 30), v3(P[:, 0:64], 32)[:, :, 0:30], ACT.Gelu_apprx_tanh), t)
            free[b] = t
            if kv == 0:
                t_g0 = t
        t_g1 = t
        kcm = area(16)
        vcm = area(128)
        b, P = bank("B")
        g4 = gT.rearrange("p (v c g n) -> p v c g n", v=2, c=2, g=2)
        for g in range(2):
            for c in range(2):
                mm(P[g * 64:(g + 1) * 64, 0:15], sm("wck2")[:, c * 64:(c + 1) * 64], g4[:, 0, c, g, :], c == 0, c == 1, t_g0)
        t = mark()
        t = V(lambda e, P=P: e.tensor_copy(kcm[:, 0:15], P[:, 0:15]), t)
        free[b] = t
        t_kcm = t
        b, P = bank("B")
        for g in range(2):
            for c in range(2):
                mm(P[0:15, g * 64:(g + 1) * 64], g4[:, 1, c, g, :], sm("wcv2")[:, c * 64:(c + 1) * 64], c == 0, c == 1, t_g1)
        t = mark()
        t_vcm = V(lambda e, P=P: e.tensor_copy(vcm[0:15, :], P[0:15, 0:128]), t)
        free[b] = t_vcm
        gt = area(48)
        b, P = bank("A")
        for i in range(2):
            for c in range(8):
                a = 128 + c * 24
                mm(P[:, i * 24:i * 24 + 24], X(c)[:, i * 128:(i + 1) * 128], smh[:, a:a + 24], c == 0, False, xk[c])
                mm(P[:, i * 24:i * 24 + 24], XLo(c)[:, i * 128:(i + 1) * 128], smh[:, a:a + 24], False, False)
                mm(P[:, i * 24:i * 24 + 24], X(c)[:, i * 128:(i + 1) * 128], sml[:, a:a + 24], False, c == 7)
        t = mark()
        for i in range(2):
            t2 = A(lambda e, P=P, i=i: e.activation(gt[:, i * 24:i * 24 + 24], P[:, i * 24:i * 24 + 24], ACT.Sigmoid,
                                                    scale=rst_[:, i:i + 1]), t, t_rst)
        free[b] = t2
        g0 = gt[:, 0:24].rearrange("p (h n) -> p h n", n=3)[:, :, 0]
        t_gt = V(lambda e: e.tensor_scalar(g0, g0, cn("valid", 0, 1), None, ALU.mult), t2, t_cst)
        mq_ = area(1024)
        mq = v3(mq_, T)
        mq_tok = []
        for j in range(2):
            (b, P, t), = projF(f"Bm{j}", X, XLo, xk, T)
            t = V(lambda e, j=j, P=P: e.scalar_tensor_tensor(mq[:, 2 * j:2 * j + 2, :], v3(P[:, :], T), 128.0 ** -0.5,
                                                             bc2(rs_[:, 0:T]), ALU.mult, ALU.mult), t, t_rs)
            free[b] = t
            mq_tok.append(t)
        bq_ = area(1024)
        bq = v3(bq_, T)
        bq_tok = []
        for j in range(2):
            (b, P, t), = projF(f"Bq{j}", X, XLo, xk, T)
            t = V(lambda e, j=j, P=P: e.scalar_tensor_tensor(bq[:, 2 * j:2 * j + 2, :], v3(P[:, :], T), 0.125,
                                                             bc2(rs_[:, 0:T]), ALU.mult, ALU.mult), t, t_rs)
            free[b] = t
            bq_tok.append(t)
        scb = area(12 + 24)
        Sb = area(2048)
        mem_attention(mq, mq_tok, 1, Sb, scb, [t_pe, new[-1]])

        pt_pe = [None, None]
        sc2 = scb[:, 12:36]
        for j in range(4):
            bo, Po = None, None
            for g in range(2):
                h = g * 4 + j
                k = h // 4 % 2
                r = g * 64
                sm_, EE = None, S1[:, k * 800:(k + 1) * 800]
                PT = Sb[:, k * 1024:(k + 1) * 1024]
                st = sc2[:, k * 12:(k + 1) * 12]
                war = pt_pe[k] if pt_pe[k] is not None else co_tok[7]
                q = lambda i: bq[r:r + 64, j, i * 128:(i + 1) * 128]
                ks = lambda w: kk[r:r + 64, w * 256:(w + 1) * 256]
                b1, P1 = bank("A")
                for w in range(2):
                    mm(P1[:, w * 256:(w + 1) * 256], q(1), ks(w), True, True, bq_tok, ktoks, t_kcm)
                t1 = mark()
                b0, P0 = bank("A")
                for w in range(2):
                    mm(P0[:, w * 128:(w + 1) * 128], q(0), ks(w)[:, 0:128], True, True)
                for i in range(2):
                    mm(P0[:, 256 + i * 16:256 + i * 16 + 15], q(i), kcm[r:r + 64, 0:15], True, True)
                t0 = mark()
                t2 = V(lambda e, P1=P1, EE=EE, h=h: e.tensor_tensor(v3(EE[:, 0:512], 256), v3(P1[:, :], 256),
                                                                    bc2(al(h)[:, 0:256]), ALU.add), t1, t_nsac, war)
                free[b1] = t2
                t3 = V(lambda e, P0=P0, EE=EE, h=h: e.tensor_tensor(v3(EE[:, 512:768], 128), v3(P0[:, 0:256], 128),
                                                                    bc2(al(h)[:, 128:256]), ALU.add), t0, t_nsac, war)
                t4 = V(lambda e, P0=P0, EE=EE, h=h: e.tensor_tensor(
                    v3(EE[:, 768:798], 15), v3(P0[:, 256:288], 16)[:, :, 0:15], v3(cb_(h), 16)[:, :, 0:15], ALU.add), t0)
                free[b0] = t4
                t5 = V(lambda e, EE=EE, st=st: e.tensor_reduce(st[:, 0:2], v3(EE[:, 0:512], 256), AX.X, ALU.max, negate=True), t2)
                t6 = V(lambda e, EE=EE, st=st: e.tensor_reduce(st[:, 2:4], v3(EE[:, 512:768], 128), AX.X, ALU.max, negate=True), t3)
                t7 = V(lambda e, EE=EE, st=st: e.tensor_reduce(st[:, 4:6], v3(EE[:, 768:798], 15), AX.X, ALU.max, negate=True), t4)
                segs = [(0, 256), (256, 512), (512, 640), (640, 768), (768, 783), (783, 798)]
                for n, (a, z) in enumerate(segs):
                    t8 = A(lambda e, EE=EE, st=st, n=n, a=a, z=z: e.activation(
                        EE[:, a:z], EE[:, a:z], ACT.Exp, bias=st[:, n:n + 1], accum_out=st[:, 6 + n:7 + n]), t7)
                t9 = V(lambda e, st=st: e.reciprocal(st[:, 6:12], st[:, 6:12]), t8)
                ga = gt[:, 24 + 3 * h + 1:24 + 3 * h + 3]
                gb = gt[:, 3 * h + 1:3 * h + 3]
                gc = gt.rearrange("p (i x) -> p i x", i=2)[:, :, 3 * h]
                t10 = V(lambda e, st=st, ga=ga: e.tensor_tensor(st[:, 6:8], st[:, 6:8], ga, ALU.mult), t9, t_gt)
                t11 = V(lambda e, st=st, gb=gb: e.tensor_tensor(st[:, 8:10], st[:, 8:10], gb, ALU.mult), t9)
                t12 = V(lambda e, st=st, gc=gc: e.tensor_tensor(st[:, 10:12], st[:, 10:12], gc, ALU.mult), t9)
                for a, z, n, o in ((0, 512, 256, 6), (512, 768, 128, 8), (768, 798, 15, 10)):
                    t13 = V(lambda e, EE=EE, st=st, a=a, z=z, n=n, o=o: e.tensor_tensor(
                        v3(EE[:, a:z], n), v3(EE[:, a:z], n),
                        st[:, o:o + 2].unsqueeze(2).broadcast_to([128, 2, n]), ALU.mult), t12)
                bx, Px = bank("B")
                tr = lambda o, s: PE.quiet(lambda e: e.transpose(o, s, cn("ident")), t13)
                for w in range(2):
                    tr(Px[:, w * 256:w * 256 + 128], EE[:, 512 + w * 128:640 + w * 128])
                    tr(Px[:, w * 256 + 128:w * 256 + 256], EE[:, w * 256:w * 256 + 128])
                tx = mark()
                by, Py = bank("B")
                for w in range(2):
                    tr(Py[:, w * 128:w * 128 + 128], EE[:, w * 256 + 128:w * 256 + 256])
                for i in range(2):
                    tr(Py[0:15, 256 + i * 128:384 + i * 128], EE[:, 768 + i * 15:783 + i * 15])
                ty = mark()
                t14 = A(lambda e, PT=PT, Px=Px: e.copy(PT[:, 0:512], Px[:, :]), tx, war)
                free[bx] = t14
                t15 = V(lambda e, PT=PT, Py=Py: e.tensor_copy(PT[:, 512:768], Py[:, 0:256]), ty, war)
                t16 = V(lambda e, PT=PT, Py=Py: e.tensor_copy(PT[0:15, 768:1024], Py[0:15, 256:512]), ty)
                free[by] = t16
                if Po is None:
                    bo, Po = bank("A")
                O = Po[r:r + 64, 0:256]
                vs = lambda i, w: vv[:, i * 256 + w * 128 + g * 64:i * 256 + w * 128 + g * 64 + 64]
                mm(O, vcm[0:15, g * 64:(g + 1) * 64], PT[0:15, 768:1024], True, False, t_vcm, t_vv, t14, t16, skip=True)
                mm(O, vs(0, 0), PT[:, 0:256], False, False, skip=True)
                mm(O, vs(0, 1), PT[:, 256:512], False, False, skip=True)
                mm(O[:, 128:256], vs(1, 0), PT[:, 512:640], False, False, skip=True)
                mm(O[:, 128:256], vs(1, 1), PT[:, 640:768], False, True, skip=True)
                pt_pe[k] = mark()
            t = pt_pe[1]
            t17 = A(lambda e, j=j, Po=Po: e.copy(coh[:, j, :], Po[:, 0:T]), pt_pe)
            t18 = V(lambda e, j=j, Po=Po: e.tensor_tensor(col[:, j, :], Po[:, 0:T], f32(coh[:, j, :]), ALU.subtract), t17)
            free[bo] = t18
            co_tok[j] = t18
        toks, xk = out_proj(["Bo0", "Bo1", "Bo2", "Bo3"], "gffn1")
        assert at_[0] <= ARW
        at_[0] = 0
        area(NNS)
        sqb = area(2 * TM)
        nt = area(2 * TM)
        yb_ = area(2 * 512)
        yb = [yb_[:, 0:512], yb_[:, 512:1024]]
        ab_ = area(2 * (T + 2))
        abuf = [ab_[:, 0:T + 2], ab_[:, T + 2:2 * (T + 2)]]
        V(lambda e: e.memset(abuf[0][:, 0:2], 0.0), toks[-1])
        t_pad = V(lambda e: e.memset(abuf[1][:, 0:2], 0.0))
        new, t_pe = ffn("f1", xk, toks, "cw1", "cb1", None)

        t_rs = token_rstd(xs, new, T, [new[-1]])
        at_[0] = NNS + 4 * TM
        meta_ = area(8 * NM)
        meta = v3(meta_, NM)
        t_meta = load(meta_, meta_d, sem("d_meta"), toks[-1])
        XF = lambda c: xh[:, c, :]
        XFL = lambda c: xl[:, c, :]
        xk = []
        for c in range(8):
            t = V(lambda e, c=c: e.scalar_tensor_tensor(xs[c], xs[c], sm("gfin", c, c + 1), rs_[:, 0:T], ALU.mult, ALU.mult),
                  t_rs)
            new[c] = t
            ta = split_x(xs[c], sm("n1", c, c + 1), X(c), XLo(c), t, war=t_pe)
            tb = split_x(meta[:, c, :], sm("n1", c, c + 1), xh[:, c, 0:NM], xl[:, c, 0:NM], t_meta, war=t_pe)
            xk.append([ta, tb])
        b, P = bank("B")
        for c in range(8):
            s = sq2[c % 2]
            ta = A(lambda e, c=c, s=s: e.activation(s[:, NM:TM], xs[c], ACT.Square), new[c], sq_free[c % 2])
            tb = A(lambda e, c=c, s=s: e.activation(s[:, 0:NM], meta[:, c, :], ACT.Square), t_meta, sq_free[c % 2])
            mm(P[:, 0:TM], cn("ones"), s[:, 0:TM], c == 0, c == 7, ta, tb)
            sq_free[c % 2] = mark()
        t0, t_rs = rsqrt(rs_[:, :], P[:, 0:TM], TM, 1.0 / D, nt, sq_free[1], new[-1])
        free[b] = t0
        b, P = bank("B")
        mm(P[0:NM, 2:3], rs_[0:1, 0:NM], cn("one")[0:1, :], True, True, t_rs)
        for i in range(2):
            mm(P[:, i:i + 1], rs_[0:1, NM + i * 128:NM + (i + 1) * 128], cn("one")[0:1, :], True, True)
        t = mark()
        V(lambda e, P=P: e.tensor_copy(rst_[0:NM, 2:3], P[0:NM, 2:3]), t)
        t_rst = V(lambda e, P=P: e.tensor_copy(rst_[:, 0:2], P[:, 0:2]), t)
        free[b] = t_rst

        cq_, ck_ = area(1024), area(4 * TM)
        cqs = area(TM * 2)
        cr = area(TM * 2)
        crt = area(TM * 4)
        sfree = [None, None]
        cq, ck = v3(cq_, T), v3(ck_, TM)
        n_hn = [0]

        def head_norm(dst, w, gn, scl, tok):
            s = n_hn[0] % 2
            n_hn[0] += 1
            sqs, rr, tp = cqs[:, s * TM:s * TM + w], cr[:, s * TM:s * TM + w], crt[:, s * 2 * TM:s * 2 * TM + 2 * w]
            t = A(lambda e: e.activation(sqs, dst, ACT.Square), tok, sfree[s])
            b, P = bank("B")
            mm(P[:, 0:w], cn("half"), sqs, True, True, t)
            t = mark()
            t0, t6 = rsqrt(rr, P[:, 0:w], w, 1.0 / 64, tp, t, sfree[s])
            free[b] = t0
            t = V(lambda e: e.scalar_tensor_tensor(dst, dst, gn, rr, ALU.mult, ALU.mult), t6)
            if scl != 1.0:
                t = V(lambda e: e.tensor_scalar(dst, dst, scl, None, ALU.mult), t)
            sfree[s] = t
            return t

        cq_tok, ck_tok = [], []
        pend = []
        for j in range(2):
            (b, P, t), = projF(f"Cq{j}", X, XLo, xk, T)
            t = V(lambda e, j=j, P=P: e.tensor_tensor(cq[:, 2 * j:2 * j + 2, :], v3(P[:, :], T),
                                                      bc2(rs_[:, NM:TM]), ALU.mult), t, t_rs)
            free[b] = t
            pend += [(cq[:, 2 * j + n, :], T, "qn", 0.125, t) for n in range(2)]
        for j in range(2):
            for n, (b, P, t) in enumerate(projF(f"Ck{j}", XF, XFL, xk, TM)):
                t = V(lambda e, j=j, n=n, P=P: e.tensor_tensor(ck[:, 2 * j + n, :], P[:, 0:TM], rs_[:, :], ALU.mult), t, t_rs)
                free[b] = t
                pend.append((ck[:, 2 * j + n, :], TM, "kn", 1.0, t))
            for _ in range(2):
                d, w, gn, scl, t = pend.pop(0)
                cq_tok.append(head_norm(d, w, sm(gn), scl, t))
        cv_ = area(3 * 512)
        cvv = v3(cv_, 512)
        cv_tok = []
        for j in range(2):
            r = projT(f"Cv{j}", XF, XFL, xk, [NM, NM + 128, 0])
            for i in range(3):
                b, P, t = r[i // 2]
                n = 128 if i < 2 else NM
                t = V(lambda e, P=P, i=i, j=j, n=n: e.tensor_scalar(
                    cvv[0:n, i, j * 256:(j + 1) * 256], P[0:n, (i % 2) * 256:(i % 2) * 256 + 256], rst_[0:n, i:i + 1],
                    None, ALU.mult), t, t_rst)
                if i > 0:
                    free[b] = t
            cv_tok.append(t)
            for _ in range(2):
                d, w, gn, scl, t = pend.pop(0)
                ck_tok.append(head_norm(d, w, sm(gn), scl, t))
        fz = area(24)
        b, P = bank("A")
        for n, a in enumerate((NM, NM + 128, 0)):
            for c in range(8):
                o, s = P[:, n * 8:n * 8 + 8], 320 + c * 8
                mm(o, XF(c)[:, a:a + 128], smh[:, s:s + 8], c == 0, False, xk[c])
                mm(o, XFL(c)[:, a:a + 128], smh[:, s:s + 8], False, False)
                mm(o, XF(c)[:, a:a + 128], sml[:, s:s + 8], False, c == 7)
        t = mark()
        fza = area(48)
        t1 = V(lambda e: e.memset(fz, 0.0))
        for n in range(3):
            m = 128 if n < 2 else NM
            t2 = V(lambda e, P=P, n=n, m=m: e.scalar_tensor_tensor(
                fz[0:m, n * 8:n * 8 + 8], P[0:m, n * 8:n * 8 + 8], rst_[0:m, n:n + 1], sm("bfg")[0:m, :],
                ALU.mult, ALU.add), t, t_rst, t1)
        free[b] = t2
        lf = area(24)
        t_lf = softplus_neg(lf, fz, 24, t2, fza[:, 0:24], fza[:, 24:48])
        cT = area(TM)
        t1 = V(lambda e: e.memset(cT, 0.0))
        b, P = bank("B")
        two = cst[:, CN["tri"][0]:CN["tri"][0] + 256]
        for r in (0, 64):
            mm(P[r:r + 8, 0:TM], lf[0:NM, 16:24], cn("trim")[0:NM, :], True, False, t_lf, skip=True)
            mm(P[r:r + 8, NM:TM], lf[:, 0:8], two, False, False, skip=True)
            mm(P[r:r + 8, NM + 128:TM], lf[:, 8:16], cn("tri"), False, True, skip=True)
        t = mark()
        for r in (0, 64):
            t_cT = V(lambda e: e.tensor_copy(cT[r:r + 8, :], P[r:r + 8, 0:TM]), t, t1)
        free[b] = t_cT
        uT = area(4 * TM)
        uu = v3(uT, TM)
        pa, pb = area(TM), area(TM)
        pool_tok = [None] * 4
        po_pe = None
        ub = []
        for j in range(2):
            for n, (b, P, t) in enumerate(projF(f"Cu{j}", XF, XFL, xk, TM)):
                t = V(lambda e, j=j, n=n, P=P: e.tensor_tensor(uu[:, 2 * j + n, :], P[:, 0:TM], rs_[:, :], ALU.mult), t, t_rs)
                free[b] = t
                ub.append(t)
        for g in range(4):
            u = uu[:, g, :]
            src, t, bufs, n = u, [ub[g], po_pe], [pa, pb], 1
            lo = 0
            for s in range(g + 1):
                dst = bufs[s % 2]
                lo += n
                t = V(lambda e, dst=dst, src=src, lo=lo, n=n: e.tensor_tensor(
                    dst[:, lo:TM], src[:, lo:TM], src[:, lo - n:TM - n], ALU.add), t)
                src = dst
                n *= 2
            dst = bufs[(g + 1) % 2]
            t = V(lambda e, dst=dst, src=src, u=u, n=n: e.scalar_tensor_tensor(
                dst[:, NM:TM], src[:, NM:TM], 1.0 / n, u[:, NM:TM], ALU.mult, ALU.subtract), t)
            b, P = bank("A")
            mm(P[:, 0:T], sm("wpool", g * 128, (g + 1) * 128), dst[:, NM:TM], True, True, t)
            po_pe = mark()
            H, L = coh[:, 4 + g, :], col[:, 4 + g, :]
            t = A(lambda e, P=P, H=H, g=g: e.activation(H, P[:, 0:T], ACT.Copy, scale=sm("pscale", g, g + 1)), po_pe)
            t = V(lambda e, P=P, H=H, L=L, g=g: e.scalar_tensor_tensor(L, P[:, 0:T], sm("pscale", g, g + 1), f32(H),
                                                                       ALU.mult, ALU.subtract), t)
            free[b] = t
            co_tok[4 + g] = t
        at_[0] = 0
        S2 = area(2 * 1024)
        st2 = area(16)
        pm_ = area(512)
        pt_pe = [t, t]
        S2 = [S2[:, 0:1024], S2[:, 1024:2048]]
        for j in range(4):
            Po = None
            for hh in range(2):
                h, r, k = 2 * j + hh, hh * 64, hh
                EE, PT, st = S2[k][:, 0:416], S2[k][:, 416:416 + 608], st2[:, k * 8:k * 8 + 8]
                b, P = bank("A")
                sel = cst[r:r + 64, CN["sel"][0] + h * 128:CN["sel"][0] + (h + 1) * 128]
                for i, (o, n) in enumerate(((272, 144), (0, 272))):
                    mm(P[:, o:o + n], cq[r:r + 64, j, i * 128:(i + 1) * 128], ck[r:r + 64, j, 0:n],
                       True, False, cq_tok, ck_tok, t_cT)
                    mm(P[:, o:o + n], sel, cT[r:r + 64, 0:n], False, True)
                t = mark()
                m2 = cn("mask2")
                t1 = V(lambda e, P=P, EE=EE: e.tensor_tensor(EE[:, 0:272], P[:, 0:272], m2, ALU.add), t, pt_pe[k])
                t2 = V(lambda e, P=P, EE=EE: e.tensor_tensor(EE[:, 272:416], P[:, 272:416], m2[:, 128:272], ALU.add), t)
                free[b] = t2
                t3 = V(lambda e, EE=EE, st=st: e.tensor_reduce(st[:, 0:1], EE[:, 0:272], AX.X, ALU.max, negate=True), t1)
                t4 = V(lambda e, EE=EE, st=st: e.tensor_reduce(st[:, 1:2], EE[:, 272:416], AX.X, ALU.max, negate=True), t2)
                for n, (a, z) in enumerate(((0, 272), (272, 416))):
                    t5 = A(lambda e, EE=EE, st=st, n=n, a=a, z=z: e.activation(
                        EE[:, a:z], EE[:, a:z], ACT.Exp, bias=st[:, n:n + 1], accum_out=st[:, 2 + n:3 + n]), t4)
                t6 = V(lambda e, st=st: e.reciprocal(st[:, 2:4], st[:, 2:4]), t5)
                for n, (a, z) in enumerate(((0, 272), (272, 416))):
                    t7 = V(lambda e, EE=EE, st=st, n=n, a=a, z=z: e.tensor_scalar(
                        EE[:, a:z], EE[:, a:z], st[:, 2 + n:3 + n], None, ALU.mult), t6)
                bx, Px = bank("B")
                tr = lambda o, s: PE.quiet(lambda e: e.transpose(o, s, cn("ident")), t7)
                tr(Px[:, 0:128], EE[:, 272 + NM:416])
                tr(Px[:, 128:256], EE[:, NM:NM + 128])
                tr(Px[:, 256:384], EE[:, NM + 128:272])
                tx = mark()
                by, Py = bank("B")
                tr(Py[0:NM, 0:128], EE[:, 272:272 + NM])
                tr(Py[0:NM, 128:256], EE[:, 0:NM])
                ty = mark()
                t8 = A(lambda e, PT=PT, Px=Px: e.copy(PT[:, 0:384], Px[:, 0:384]), tx, pt_pe[k])
                free[bx] = t8
                PMm = pm_[:, k * 256:(k + 1) * 256]
                t9 = V(lambda e, PMm=PMm, Py=Py: e.tensor_copy(PMm[0:NM, :], Py[0:NM, 0:256]), ty, pt_pe[k])
                free[by] = t9
                if Po is None:
                    bo, Po = bank("A")
                O = Po[r:r + 64, 0:256]
                vs = lambda i, n: cvv[0:n, i, h * 64:(h + 1) * 64]
                mm(O, vs(2, NM), PMm[0:NM, :], True, False, cv_tok, t8, t9, skip=True)
                mm(O, vs(0, 128), PT[:, 0:256], False, False, skip=True)
                mm(O[:, 128:256], vs(1, 128), PT[:, 256:384], False, True, skip=True)
                pt_pe[k] = mark()
            t17 = A(lambda e, j=j, Po=Po: e.copy(coh[:, j, :], Po[:, 0:T]), pt_pe)
            t18 = V(lambda e, j=j, Po=Po: e.tensor_tensor(col[:, j, :], Po[:, 0:T], f32(coh[:, j, :]), ALU.subtract), t17)
            free[bo] = t18
            co_tok[j] = t18
        toks, xk = out_proj(["Co0", "Co1", "Co2", "Co3"], "n2")
        at_[0] = NNS + 4 * TM
        yb_ = area(2 * 512)
        yb = [yb_[:, 0:512], yb_[:, 512:1024]]
        new, t_pe = ffn("f2", xk, toks, None, None, None)
        s_out = sem("s_out")
        for c in range(8):
            SP.wait(new[c])
            SP.quiet(lambda e, c=c: e.dma_start(out_d[:, c * T:(c + 1) * T], xs[c]).then_inc(s_out, 16))
        SP.wait((s_out, 128))


def constants():
    f = np.float32
    p = np.arange(128)
    tri = (p[:, None] <= p[None, :]).astype(f)
    c = {
        "ident": np.eye(128, dtype=f), "ones": np.ones((128, 128), f),
        "half": (p[:, None] // 64 == p[None, :] // 64).astype(f), "tri": tri, "one2": np.ones((128, 128), f),
        "trim": (p[:, None] <= np.arange(TM)[None, :]).astype(f),
        "valid": np.stack([(p >= 31).astype(f), np.ones(128, f)], 1), "eps": np.full((128, 1), EPS, f),
        "one": np.ones((128, 1), f),
    }
    causal = np.where(p[None, :] <= p[:, None], 0, NEG).astype(f)
    c["mask2"] = np.concatenate([np.zeros((128, 144), f), causal], 1)
    sel = np.zeros((128, 8, 128), f)
    for h in range(8):
        sel[h, h] = sel[64 + h, h] = -1
    c["sel"] = sel.reshape(128, -1)
    cst = np.concatenate([c[n] for n, _ in CONST], 1)
    gm = []
    for m in LEVELS:
        s, t = p[:, None], p[None, :]
        if m:
            gm.append((s // (2 * m) == t // (2 * m)) & (s % (2 * m) < m) & (t % (2 * m) >= m))
        else:
            gm.append(s == t)
    gm = np.concatenate(gm, 1).astype(f)
    al, cb = [], []
    for h in range(8):
        slope = f(2.0 ** -(h + 1))
        t, s = p[:, None], p[None, :]
        diag = np.where(s <= t, -slope * (t - s), NEG).astype(f)
        off = (-slope * (128 + t - s)).astype(f)
        al.append(np.concatenate([off, diag], 1))
        e = np.arange(16)[None, :] * 16 + 31
        for i in range(2):
            d = i * 128 + t - e
            cb.append(np.where(d >= 0, -slope * d, NEG).astype(f))
    ns = np.concatenate(al + cb, 1)
    return cst, gm, ns


def pack(i):
    d = {}

    def cols(w, a, b):
        k = w.shape[0] // 128
        return w.reshape(k, 128, -1)[:, :, a:b].transpose(1, 0, 2).reshape(128, -1)

    units = {}

    def put(prefix, w, a, n):
        for j in range(n):
            units[f"{prefix}{j}"] = cols(w, a + 256 * j, a + 256 * (j + 1))

    aw = i["a_w_in"][0]
    units["Aq"], units["Ak"] = cols(aw, 0, 256), cols(aw, 256, 512)
    put("Av", aw, 512, 2)
    put("Ar", aw, 1024, 2)
    put("Am", aw, 1552, 2)
    for l in range(2):
        put(f"m{l}k", i["w_mem_kv"][l], 0, 2)
        put(f"m{l}v", i["w_mem_kv"][l], 512, 2)
    put("Ao", i["a_w_out"][0], 0, 4)

    def ffn(tag, wa, wb, wd):
        for f in range(NF):
            c = slice(f * 128, (f + 1) * 128)
            units[f"{tag}u{f}"] = cols(np.concatenate([wa[:, c], wb[:, c]], 1), 0, 256)
        for p in range(11):
            units[f"{tag}d{p}"] = cols(wd[p * 256:(p + 1) * 256], 0, 1024)

    for l in range(2):
        ffn(f"f{l}", i["w_up"][l][:, :2816], i["w_up"][l][:, 2816:], i["w_down"][l])
    ffn("f2", i["w_gate_2"][0], i["w_up_2"][0], i["w_down_2"][0])
    kv = i["w_kv"]
    seg = lambda n: kv[:, n * 128:(n + 1) * 128]
    units["kvc"] = cols(kv[:, 0:256], 0, 256)
    units["kvk"] = cols(np.concatenate([seg(2), seg(4)], 1), 0, 256)
    units["kvv"] = cols(np.concatenate([seg(3), seg(5)], 1), 0, 256)
    for n, w in (("ck", i["w_ck1"]), ("cv", i["w_cv1"])):
        for j in range(2):
            units[f"{n}{j}"] = cols(w[j * 1024:(j + 1) * 1024], 0, 256)
    bw = i["b_w_in"][0]
    order = [0, 4, 1, 5, 2, 6, 3, 7]
    bq = bw[:, :512].reshape(D, 8, 64)[:, order].reshape(D, 512)
    put("Bq", bq, 0, 2)
    put("Bm", bw, 536, 2)
    bo = i["b_w_out"][0]
    bo = np.concatenate([bo[:512].reshape(8, 64, D)[order].reshape(512, D), bo[512:]], 0)
    put("Bo", bo, 0, 4)
    cw = i["w_in_2"][0]
    put("Cq", cw, 0, 2)
    put("Ck", cw, 512, 2)
    put("Cv", cw, 1024, 2)
    put("Cu", cw, 1544, 2)
    put("Co", i["w_out_2"][0], 0, 4)
    d["w"] = np.stack([units[n] for n in unit_names()])

    vec = lambda v: v.reshape(-1, 128).T
    bc = lambda v: np.broadcast_to(v.reshape(1, -1), (128, v.size))
    s = {
        "gmix0": vec(i["g_mix"][0]), "gmix1": vec(i["g_mix"][1]), "gffn0": vec(i["g_ffn"][0]),
        "gffn1": vec(i["g_ffn"][1]), "gmem0": vec(i["g_mem"][0]), "gmem1": vec(i["g_mem"][1]),
        "gkv": vec(i["g_kv"]), "gfin": vec(i["g_final"]), "n1": vec(i["norm1_w_2"][0]), "n2": vec(i["norm2_w_2"][0]),
        "ghead": vec(i["a_g_head"][0]), "pscale": vec(i["pool_scale_2"][0]),
        "qn": vec(np.concatenate([i["q_norm_w_2"][0]] * 2)), "kn": vec(np.concatenate([i["k_norm_w_2"][0]] * 2)),
        "bfg": bc(i["b_fgate_2"][0]),
        "pek": i["pe_k"].reshape(16, 128).T, "pev": i["pe_v"].reshape(16, 128).T,
        "cb0": vec(i["conv_b"][0]), "cb1": vec(i["conv_b"][1]),
        "walr": cols(aw, 1536, 1552), "wgl": cols(bw, 512, 536), "wfg": cols(cw, 1536, 1544),
        "balpha": bc(i["a_b_alpha"][0]), "wck2": cols(i["w_ck2"], 0, 64), "wcv2": cols(i["w_cv2"], 0, 64),
        "wpool": i["w_pool_2"][0].transpose(1, 0, 2).reshape(128, 512),
    }
    for l in range(2):
        s[f"cw{l}"] = np.concatenate([vec(i["conv_w"][l][n]) for n in range(3)], 1)
    wa = np.zeros((128, 256), np.float32)
    wa[:16] = i["a_w_alpha"][0]
    s["walpha"] = wa
    d["small"] = np.concatenate([s[n] for n, _ in SMALL], 1)
    d["x"] = cols(i["x"][0].T, 0, T)
    d["mem"] = cols(i["mem"][0].T, 0, T)
    d["meta"] = cols(i["meta_tokens_2"].T, 0, NM)
    d["const"], d["gmask"], d["nsac"] = constants()
    return {k: np.ascontiguousarray(v) for k, v in d.items()}


_ORDER = ["w", "x", "mem", "meta", "small", "const", "gmask", "nsac"]


def kernel(**inputs):
    import concourse.bacc as _bacc
    from concourse.bass_utils import run_bass_kernel_spmd as _run

    d = pack({k: np.asarray(v) for k, v in inputs.items()})
    nc = _bacc.Bacc("TRN2", target_bir_lowering=False, num_devices=1)
    args, arrays = [], {}
    for n in _ORDER:
        arrays[f"in_{n}"] = d[n]
        args.append(nc.dram_tensor(f"in_{n}", d[n].shape, F32, kind="ExternalInput").ap())
    args.append(nc.dram_tensor("out_0", (128, 8 * T), F32, kind="ExternalOutput").ap())
    build(nc, *args)
    r = _run(nc, [arrays], core_ids=[0])
    o = np.asarray(r.results[0]["out_0"])
    return np.ascontiguousarray(o.reshape(128, 8, T).transpose(2, 1, 0).reshape(1, T, D))
```

```python
import numpy as np

import concourse.bass as bass
from concourse import mybir
from contextlib import ExitStack

F32 = mybir.dt.float32
F32R = mybir.dt.float32r
U32 = mybir.dt.uint32
ALU = mybir.AluOpType
ACT = mybir.ActivationFunctionType
AX = mybir.AxisListType
EPS = 1e-6
NEG = -1.0e30

D = 1024
T = 256
NM = 16
TM = T + NM
NF = 22
UW = 2048
LEVELS = [64, 32, 16, 8, 4, 2, 1, 0]


def unit_names():
    up = lambda tag: [f"{tag}u0", f"{tag}u1"] + [
        n for p in range(1, 11) for n in (f"{tag}u{2 * p}", f"{tag}u{2 * p + 1}", f"{tag}d{p - 1}")
    ] + [f"{tag}d10"]
    return (
        ["Aq", "Ak", "m0k0", "m0k1", "m0v0", "m0v1", "Av0", "Av1", "Ar0", "Ar1", "Am0", "Am1",
         "m1k0", "m1k1", "m1v0", "m1v1", "Ao0", "Ao1", "Ao2", "Ao3"]
        + up("f0")
        + ["kvc", "kvk", "kvv", "Bm0", "Bm1", "ck0", "ck1", "cv0", "cv1", "Bq0", "Bq1",
           "Bo0", "Bo1", "Bo2", "Bo3"]
        + up("f1")
        + ["Cq0", "Cq1", "Ck0", "Ck1", "Cv0", "Cv1", "Cu0", "Cu1", "Co0", "Co1", "Co2", "Co3"]
        + up("f2")
    )


RAW = {"ck0", "ck1", "cv0", "cv1"}

SMALL = [
    ("gmix0", 8), ("gmix1", 8), ("gffn0", 8), ("gffn1", 8), ("gmem0", 8), ("gmem1", 8),
    ("gkv", 8), ("gfin", 8), ("n1", 8), ("n2", 8), ("ghead", 1), ("pscale", 4), ("qn", 1),
    ("kn", 1), ("bfg", 8), ("pek", 16), ("pev", 16), ("cw0", 66), ("cw1", 66), ("cb0", 22),
    ("cb1", 22), ("walr", 128), ("wgl", 192), ("wfg", 64), ("balpha", 256), ("walpha", 256),
    ("wck2", 128), ("wcv2", 128), ("wpool", 512),
]
CONST = [
    ("ident", 128), ("tri", 128), ("ones", 128), ("trim", TM), ("mask2", TM), ("halves", 2),
    ("valid", 2), ("one", 1), ("mhalf", 32),
]
NSAC = [("alibi", 8 * 256), ("cmpb", 8 * 32)]


def columns(table):
    at, out = 0, {}
    for name, n in table:
        out[name] = (at, n)
        at += n
    return out, at


SM, NSM = columns(SMALL)
CN, NCN = columns(CONST)
NS, NNS = columns(NSAC)


class Queue:

    def __init__(self, eng, sem):
        self.eng, self.sem, self.n, self.past, self.last = eng, sem, 0, {}, None

    def wait(self, *toks):
        for t in toks:
            if t is None:
                continue
            if isinstance(t, list):
                self.wait(*t)
                continue
            sem, v = t
            if self.past.get(id(sem), 0) < v:
                self.past[id(sem)] = v
                self.eng.wait_ge(sem, v)

    def do(self, f, *toks):
        self.wait(*toks)
        self.n += 1
        self.last = f(self.eng).then_inc(self.sem, 1)
        return (self.sem, self.n)

    def quiet(self, f, *toks):
        self.wait(*toks)
        self.last = f(self.eng)

    def mark(self):
        self.last.then_inc(self.sem, 1)
        self.n += 1
        return (self.sem, self.n)


def build(nc, w_d, x_d, mem_d, meta_d, small_d, const_d, gmask_d, nsac_d, sel_d, out_d):
    ctx = ExitStack()
    with ctx:
        def sb(name, cols, dt=F32):
            return ctx.enter_context(nc.sbuf_tensor(name, [128, cols], dt))

        def sem(name):
            return ctx.enter_context(nc.semaphore(name))

        PE = Queue(nc.tensor, sem("s_pe"))
        ACTE = Queue(nc.scalar, sem("s_act"))
        DVE = Queue(nc.vector, sem("s_dve"))
        SP = Queue(nc.sync, sem("s_sp"))
        POOL = Queue(nc.gpsimd, sem("s_pool"))

        NR, NH, AHEAD = 3, 3, 2
        raw = sb("raw", NR * UW)
        wh = sb("wh", NH * UW, F32R)
        wl = sb("wl", NH * UW, F32R)
        xt_ = sb("xt", 8 * T)
        xh_ = sb("xh", 8 * TM, F32R)
        xl_ = sb("xl", 8 * TM, F32R)
        coh_ = sb("coh", 8 * T, F32R)
        col_ = sb("col", 8 * T, F32R)
        memkv = sb("memkv", 4 * 1024)
        small = sb("small", NSM)
        smh = sb("smh", 384, F32R)
        sml = sb("sml", 384, F32R)
        cst = sb("cst", NCN)
        ARW = 13200
        arena = sb("arena", ARW)
        fh_ = sb("fh", 4 * T, F32R)
        fl_ = sb("fl", 4 * T, F32R)
        rs_ = sb("rs", TM)
        rst_ = sb("rst", 16)
        banks = [ctx.enter_context(nc.psum_tensor(f"ps{i}", [128, 512], F32)) for i in range(8)]

        v3 = lambda ap, n: ap.rearrange("p (a b) -> p a b", b=n)
        xt = v3(xt_[:, :], T)
        xh, xl = v3(xh_[:, :], TM), v3(xl_[:, :], TM)
        coh, col = v3(coh_[:, :], T), v3(col_[:, :], T)
        f32 = lambda ap: ap.bitcast(F32)

        def sm(name, a=0, b=None):
            at, n = SM[name]
            return small[:, at + a:at + (n if b is None else b)]

        def cn(name, a=0, b=None):
            at, n = CN[name]
            return cst[:, at + a:at + (n if b is None else b)]

        at_ = [0]

        def area(n):
            at_[0] += n
            assert at_[0] <= ARW, at_[0]
            return arena[:, at_[0] - n:at_[0]]

        def load(dst, src, s, *toks):
            SP.wait(*toks)
            SP.quiet(lambda e: e.dma_start(dst, src).then_inc(s, 16))
            return (s, 16)

        memT_ = area(8 * T)
        memT = v3(memT_, T)
        t_x = [load(xt_[:, 1024 * n:1024 * n + 1024], x_d[:, 1024 * n:1024 * n + 1024], sem(f"d_x{n}")) for n in range(2)]
        t_small = load(small[:, :], small_d, sem("d_small"))

        names = unit_names()
        ring_sem = [sem(f"d_w{i}") for i in range(NR)]

        class Stream:

            dma_n = split_n = got = hslots = 0
            raw_free = {}
            part_free = {}
            landed = {}
            parts = {}

            def fetch(self, upto=None):
                i = self.dma_n
                if i == upto or i >= len(names) or (i >= NR and (i - NR) not in self.raw_free):
                    return
                s = ring_sem[i % NR]
                SP.wait(self.raw_free.get(i - NR))
                dst = raw[:, (i % NR) * UW:(i % NR + 1) * UW]
                SP.quiet(lambda e: e.dma_start(dst, w_d[i]).then_inc(s, 16))
                self.landed[i] = (s, 16 * (i // NR + 1))
                self.dma_n += 1
                self.fetch(upto)

            def split(self):
                i = self.split_n
                self.split_n += 1
                src = raw[:, (i % NR) * UW:(i % NR + 1) * UW]
                if names[i] in RAW:
                    self.parts[i] = (src, None, None)
                    return
                k = self.hslots
                self.hslots += 1
                free = self.part_free[k - NH] if k >= NH else None
                H = wh[:, (k % NH) * UW:(k % NH + 1) * UW]
                L = wl[:, (k % NH) * UW:(k % NH + 1) * UW]
                hw = UW // 2
                tl = []
                for a in (0, hw):
                    th = ACTE.do(lambda e, a=a: e.copy(H[:, a:a + hw], src[:, a:a + hw]), self.landed[i], free)
                    tl.append(DVE.do(lambda e, a=a: e.tensor_tensor(
                        L[:, a:a + hw], src[:, a:a + hw], f32(H[:, a:a + hw]), ALU.subtract),
                        self.landed[i], free, th))
                self.raw_free[i] = tl[1]
                self.parts[i] = (H, L, tl, k)
                self.fetch()

            def get(self, name):
                i = self.got
                self.got += 1
                assert names[i] == name, (names[i], name)
                while self.split_n <= min(i + AHEAD, len(names) - 1):
                    if self.split_n > i and self.split_n >= self.dma_n:
                        break
                    self.split()
                return i, self.parts[i]

            def release(self, i, tok):
                p = self.parts[i]
                if p[1] is None:
                    self.raw_free[i] = tok
                    self.fetch()
                else:
                    self.part_free[p[3]] = tok

        W = Stream()
        W.fetch(1)
        t_cst = load(cst[:, :], const_d, sem("d_cst"))
        W.fetch(2)
        t_mem = load(memT_, mem_d, sem("d_mem"))
        W.fetch()

        free = [None] * 8
        turn = {"A": [0, 1, 2, 3], "B": [4, 5, 6, 7]}

        def bank(ring):
            b = next(n for n in turn[ring] if free[n] != "held")
            turn[ring].remove(b)
            turn[ring].append(b)
            PE.wait(free[b])
            free[b] = "held"
            return b, banks[b]

        def mm(out, lhsT, rhs, start, stop, *toks, skip=False):
            PE.quiet(lambda e: e.matmul(out, lhsT, rhs, start=start, stop=stop, skip_group_check=skip), *toks)

        def mark():
            return PE.mark()

        def mm3(out, wH, wL, XH, XL, start, stop, *toks, skip=False):
            mm(out, wH, XH, start, False, *toks, skip=skip)
            mm(out, wH, XL, False, False, skip=skip)
            mm(out, wL, XH, False, stop, skip=skip)

        def V(f, *t):
            return DVE.do(f, *t)

        def A(f, *t):
            return ACTE.do(f, *t)

        def split_x(src, g, H, L, *toks, war=None):
            th = A(lambda e: e.activation(H, src, ACT.Copy, scale=g), war, *toks)
            return V(lambda e: e.scalar_tensor_tensor(L, src, g, f32(H), ALU.mult, ALU.subtract), th, war, *toks)

        def split_p(H, L, P, *toks):
            th = A(lambda e: e.copy(H, P), *toks)
            return V(lambda e: e.tensor_tensor(L, P, f32(H), ALU.subtract), th)

        def power(dst, src, n, *toks):
            m = src.shape[0]
            return POOL.do(lambda e: e.tensor_tensor(dst, src, cn("mhalf")[0:m, 0:n], ALU.pow), t_cst, *toks)

        def transpose(out, src, *toks):
            m = src.shape[0]
            PE.quiet(lambda e: e.transpose(out, src, cn("ident")[0:m, 0:m]), t_cst, *toks)

        def spread(dst, col, tiles, tok, war=None):
            b, P = bank("B")
            for n, a, m in tiles:
                transpose(P[:, a:a + m], col[0:m, n:n + 1].broadcast_to([m, 128]), tok)
            w = max(a + m for _, a, m in tiles)
            t = V(lambda e: e.tensor_copy(dst, P[:, 0:w]), mark(), war)
            free[b] = t
            return t

        sqb = area(4 * TM)
        sq2 = [sqb[:, n * TM:(n + 1) * TM] for n in range(4)]
        sq_free = [None] * 4
        sq_n = [0]
        TT = [(0, 0, 128), (1, 128, 128)]

        def square(src, tok, scale=1.0):
            k = sq_n[0] % 4
            sq_n[0] += 1
            s = sq2[k][:, 0:src.shape[-1]]
            return k, s, A(lambda e: e.activation(s, src, ACT.Square, scale=scale), tok, sq_free[k])

        def token_rstd(srcs, toks, rowd, cold, war=None):
            b, P = bank("B")
            for c in range(8):
                k, s, t = square(srcs[c], toks[c])
                for n in range(2):
                    mm(P[:, n:n + 1], s[:, n * 128:(n + 1) * 128], cn("one"), c == 0 and n == 0, c == 7, t, t_cst, skip=True)
                sq_free[k] = mark()
            t = V(lambda e: e.tensor_scalar(rst_[:, 8:10], P[:, 0:2], 1.0 / D, EPS, ALU.mult, ALU.add), sq_free[k], war)
            free[b] = t
            t_c = power(cold, rst_[:, 8:10], 2, t, war)
            return t_c, spread(rowd, cold, TT, t_c, war)

        KORD = list(range(8))

        def projF(name, XH, XL, xtoks, out_w, order=KORD):
            i, (H, L, tl, k) = W.get(name)
            H3, L3 = v3(H, 256), v3(L, 256)
            res = []
            if out_w <= 256:
                b, P = bank("A")
            for j in range(2):
                if out_w > 256:
                    b, P = bank("A")
                    O = P[:, 0:out_w]
                else:
                    O = P[:, j * 256:j * 256 + out_w]
                for n, c in enumerate(order):
                    mm3(O, H3[:, c, j * 128:(j + 1) * 128], L3[:, c, j * 128:(j + 1) * 128],
                        XH(c), XL(c), n == 0, n == 7, xtoks[c], tl[c // 4])
                if out_w > 256:
                    res.append((b, P, mark()))
            if out_w <= 256:
                res.append((b, P, mark()))
            W.release(i, res[-1][2])
            return res

        def projT(name, XH, XL, xtoks, tiles):
            i, (H, L, tl, k) = W.get(name)
            H3, L3 = v3(H, 256), v3(L, 256)
            res = []
            for n, a in enumerate(tiles):
                if n % 2 == 0:
                    b, P = bank("A")
                O = P[:, (n % 2) * 256:(n % 2) * 256 + 256]
                for c in range(8):
                    mm(O, XH(c)[:, a:a + 128], H3[:, c, :], c == 0, False, xtoks[c], tl[c // 4])
                    mm(O, XL(c)[:, a:a + 128], H3[:, c, :], False, False)
                    mm(O, XH(c)[:, a:a + 128], L3[:, c, :], False, c == 7)
                if n % 2 == 1 or n == len(tiles) - 1:
                    res.append((b, P, mark()))
            W.release(i, res[-1][2])
            return res

        def bc2(ap, n=2):
            return ap.unsqueeze(1).broadcast_to([128, n, ap.shape[-1]])

        X = lambda c: xh[:, c, NM:TM]
        XLo = lambda c: xl[:, c, NM:TM]
        CH = lambda c: coh[:, c, :]
        CL = lambda c: col[:, c, :]

        def enter(srcs, toks, g, war, H=X, L=XLo):
            return [split_x(srcs[c], sm(g, c, c + 1), H(c), L(c), toks[c], t_small, war=war) for c in range(8)]

        def softplus_neg(dst, z, tok, tmpa, tmpb):
            t1 = A(lambda e: e.activation(tmpa, z, ACT.Abs), tok)
            t2 = A(lambda e: e.activation(tmpb, tmpa, ACT.Exp, scale=-1.0), t1)
            t3 = A(lambda e: e.activation(tmpa, tmpb, ACT.Ln, bias=cn("one")), t2, t_cst)
            return V(lambda e: e.scalar_tensor_tensor(dst, z, 0.0, tmpa, ALU.min, ALU.subtract), t3)

        def weave(*gens):
            live = list(gens)
            while live:
                for g in list(live):
                    try:
                        next(g)
                    except StopIteration:
                        live.remove(g)

        def pipeline(gens, depth):
            todo, live = list(gens), []
            while todo or live:
                if todo and len(live) < depth:
                    live.append(todo.pop(0))
                for g in list(live):
                    try:
                        next(g)
                    except StopIteration:
                        live.remove(g)
                yield

        def after(n, gen):
            for _ in range(n):
                yield
            yield from gen

        co_tok = [None] * 8
        mem_tok = {0: [], 1: []}
        mk = lambda l: v3(memkv[:, l * 2048:l * 2048 + 1024], T)
        mv = lambda l: v3(memkv[:, l * 2048 + 1024:l * 2048 + 2048], 512)

        def mem_head(l, h, mq, mq_tok, Eh, PT, sc, key, last, war):
            mx, su = sc[:, 0:2], sc[:, 2:4]
            was = last.get(key)
            b, P = bank("B")
            for i in range(2):
                mm(P[:, i * 256:(i + 1) * 256], mq[:, h, i * 128:(i + 1) * 128], mk(l)[:, h, :], True, True,
                   mq_tok, mem_tok[l])
            t = mark()
            t1 = V(lambda e: e.tensor_reduce(mx, v3(P[:, :], 256), AX.X, ALU.max, negate=True), t, was, war)
            for i in range(2):
                t2 = A(lambda e: e.activation(Eh[:, i * 256:(i + 1) * 256], P[:, i * 256:(i + 1) * 256], ACT.Exp,
                                              bias=mx[:, i:i + 1], accum_out=su[:, i:i + 1]), t1, was, war)
            free[b] = t2
            t3 = V(lambda e: e.reciprocal(su, su), t2)
            t4 = V(lambda e: e.tensor_tensor(v3(Eh, 256), v3(Eh, 256), su.unsqueeze(2).broadcast_to([128, 2, 256]),
                                             ALU.mult), t3)
            yield
            b, P = bank("B")
            for mi in range(2):
                for i in range(2):
                    transpose(P[:, mi * 256 + i * 128:mi * 256 + (i + 1) * 128],
                              Eh[:, i * 256 + mi * 128:i * 256 + (mi + 1) * 128], t4)
            t6 = A(lambda e: e.copy(PT, P[:, :]), mark(), was, war)
            free[b] = t6
            yield
            b, P = bank("B")
            for mi in range(2):
                mm(P[:, 0:T], mv(l)[:, mi, h * 128:(h + 1) * 128], PT[:, mi * 256:(mi + 1) * 256], mi == 0, mi == 1, t6)
            last[key] = mark()
            t9 = split_p(coh[:, 4 + h, :], col[:, 4 + h, :], P[:, 0:T], last[key], war)
            free[b] = t9
            co_tok[4 + h] = t9
            yield

        xs = [xt[:, c, :] for c in range(8)]
        ms = [memT[:, c, :] for c in range(8)]
        xtok = enter(xs, [t_x[c // 4] for c in range(8)], "gmix0", None)
        at0 = SM["walr"][0]
        t = A(lambda e: e.copy(smh[:, :], small[:, at0:at0 + 384]), t_small)
        t_sml = V(lambda e: e.tensor_tensor(sml[:, :], small[:, at0:at0 + 384], f32(smh[:, :]), ALU.subtract), t)

        r_ = area(1024)
        alrT = r_[:, 0:256]
        b0, P0 = bank("A")
        for c in range(8):
            a = c * 16
            mm3(P0[:, 0:T], smh[:, a:a + 128], sml[:, a:a + 128], X(c), XLo(c), c == 0, c == 7, xtok[c], t_sml)
        t_alr0 = mark()
        qkb = area(1024)
        q_, k_ = qkb[:, 0:512], qkb[:, 512:1024]
        (bq0, Pq0, tq0), = projF("Aq", X, XLo, xtok, T)
        t_rst, t_rs = token_rstd(xs, [t_x[c // 4] for c in range(8)], rs_[:, 0:T], rst_[:, 0:2])
        t_alr = V(lambda e: e.tensor_tensor(alrT[0:16, :], P0[0:16, 0:T], rs_[0:16, 0:T], ALU.mult), t_alr0, t_rs)
        free[b0] = t_alr
        t_q = V(lambda e: e.scalar_tensor_tensor(v3(q_, T), v3(Pq0[:, :], T), 0.125, bc2(rs_[:, 0:T]), ALU.mult, ALU.mult),
                tq0, t_rs)
        free[bq0] = t_q
        mtok = enter(ms, [t_mem] * 8, "gmem0", None, CH, CL)
        (b, P, t), = projF("Ak", X, XLo, xtok, T)
        t_k = V(lambda e: e.tensor_tensor(v3(k_, T), v3(P[:, :], T), bc2(rs_[:, 0:T]), ALU.mult), t, t_rs)
        free[b] = t_k
        qk_tok = [t_q, t_k]

        mrs = area(T)
        mrst = area(2)
        t_mrst, t_mrs = token_rstd(ms, [t_mem] * 8, mrs, mrst)
        gm = area(1024)
        t_gm = load(gm, gmask_d, sem("d_gm"))
        v_ = area(1024)
        v4 = v3(v_, 512)
        AT_ = area(1024)
        ATo = area(512)
        t_at0 = V(lambda e: e.memset(AT_, 0.0))
        b_ = area(512)
        lv = area(5 * 512)
        E_ = lv[:, 0:512]
        QK = [(lv[:, 512:1024], lv[:, 1024:1536]), (lv[:, 1536:2048], lv[:, 2048:2560])]
        mq_ = area(1024)
        mq = v3(mq_, T)
        scb = area(16)
        tk = {}

        def mem_unit(l, kind, j, mtok):
            if kind == "k":
                (b, P, t), = projF(f"m{l}k{j}", CH, CL, mtok, T)
                t2 = V(lambda e: e.tensor_tensor(mk(l)[:, 2 * j:2 * j + 2, :], v3(P[:, :], T), bc2(mrs), ALU.mult), t, t_mrs)
            else:
                (b, P, t), = projT(f"m{l}v{j}", CH, CL, mtok, [0, 128])
                for i in range(2):
                    t2 = V(lambda e: e.tensor_scalar(mv(l)[:, i, j * 256:(j + 1) * 256], P[:, i * 256:(i + 1) * 256],
                                                     mrst[:, i:i + 1], None, ALU.mult), t, t_mrst)
            free[b] = t2
            mem_tok[l].append(t2)
            return t

        def units():
            for kind in "kv":
                for j in range(2):
                    tk["m0"] = mem_unit(0, kind, j, mtok)
                    yield
            tk["v"] = []
            for j in range(2):
                (b, P, t), = projT(f"Av{j}", X, XLo, xtok, [0, 128])
                for i in range(2):
                    t2 = V(lambda e: e.tensor_scalar(v4[:, i, j * 256:(j + 1) * 256], P[:, i * 256:(i + 1) * 256],
                                                     rst_[:, i:i + 1], None, ALU.mult), t, t_rst)
                free[b] = t2
                tk["v"].append(t2)
                if j == 0:
                    tk["m1"] = enter(ms, [t_mem] * 8, "gmem1", tk["m0"], CH, CL)
                yield
            tk["r"] = []
            for j in range(2):
                (b, P, t), = projF(f"Ar{j}", X, XLo, xtok, T)
                t = V(lambda e: e.tensor_tensor(v3(r_[:, j * 512:(j + 1) * 512], T), v3(P[:, :], T),
                                                bc2(rs_[:, 0:T]), ALU.mult), t, t_rs, tk["z"])
                free[b] = t
                tk["r"].append(t)
                yield
            tk["mq"] = []
            for j in range(2):
                (b, P, t), = projF(f"Am{j}", X, XLo, xtok, T)
                t = V(lambda e: e.scalar_tensor_tensor(mq[:, 2 * j:2 * j + 2, :], v3(P[:, :], T), 128.0 ** -0.5,
                                                       bc2(rs_[:, 0:T]), ALU.mult, ALU.mult), t, t_rs)
                free[b] = t
                tk["mq"].append(t)
                yield
            for kind in "kv":
                for j in range(2):
                    tk["m1pe"] = mem_unit(1, kind, j, tk["m1"])
                    yield

        def decay():
            la, (ea, eb) = E_, QK[1]
            b, P = bank("B")
            for i in range(2):
                mm(P[:, i * 256:(i + 1) * 256], alrT[0:16, i * 128:(i + 1) * 128], sm("walpha")[0:16, :], True, True, t_alr)
            tk["z"] = mark()
            t = V(lambda e: e.tensor_tensor(v3(la, 256), v3(P[:, :], 256), bc2(sm("balpha")), ALU.add), tk["z"], t_small)
            free[b] = t
            t_la = softplus_neg(la, la, t, ea, eb)
            yield
            b, P = bank("B")
            for dt in range(2):
                for i in range(2):
                    mm(P[:, (dt * 2 + i) * 128:(dt * 2 + i + 1) * 128],
                       la[:, i * 256 + dt * 128:i * 256 + dt * 128 + 128], cn("tri"), True, True, t_la, t_cst)
            t = mark()
            tk["b"] = V(lambda e: e.tensor_scalar(b_, P[:, :], 1.0 / 16, None, ALU.mult), t)
            free[b] = tk["b"]
            yield
            used = [None, None]

            def prep(li):
                m = LEVELS[li]
                if not m:
                    return q_, k_, qk_tok
                Q, K = QK[li % 2]
                bv = b_.rearrange("p (a c) -> p a c", c=2 * m)
                ev = E_.rearrange("p (a c) -> p a c", c=2 * m)
                t = V(lambda e: e.tensor_tensor(ev, bv, bv[:, :, m - 1:m].broadcast_to([128, 512 // (2 * m), 2 * m]),
                                                ALU.subtract), tk["b"], tk.get("E"))
                t = A(lambda e: e.activation(E_, E_, ACT.Abs), t)
                t = A(lambda e: e.activation(E_, E_, ACT.Exp, scale=-1.0), t)
                ta = V(lambda e: e.tensor_tensor(Q, q_, E_, ALU.mult), t, qk_tok[0], used[li % 2])
                tb = V(lambda e: e.tensor_tensor(K, k_, E_, ALU.mult), t, qk_tok[1], used[li % 2])
                tk["E"] = [ta, tb]
                return Q, K, [ta, tb]

            ready = prep(0)
            at_tok = [t_at0, t_at0]
            yield
            for li in range(8):
                nxt = prep(li + 1) if li < 7 else None
                QQ, KK, tt = ready
                for half in range(2):
                    b, P = bank("B")
                    r = half * 64
                    for hh in range(2):
                        for i in range(2):
                            s = (hh * 2 + i) * 128
                            mm(P[:, s:s + 128], KK[r:r + 64, s:s + 128], QQ[r:r + 64, s:s + 128], True, True, tt)
                    t = mark()
                    mask = gm[:, li * 128:(li + 1) * 128].bitcast(U32)
                    t2 = V(lambda e: e.copy_predicated(v3(AT_[:, half * 512:(half + 1) * 512], 128), bc2(mask, 4),
                                                       v3(P[:, :], 128)), t, t_gm, at_tok[half])
                    free[b] = at_tok[half] = t2
                used[li % 2] = t
                ready = nxt
                yield
            Q, K = QK[1]
            tq = []
            for dt in range(2):
                s0, s1 = (dt * 2) * 128, (dt * 2 + 1) * 128
                t = A(lambda e: e.activation(E_[:, s0:s0 + 128], b_[:, s0:s0 + 128], ACT.Exp, scale=-1.0,
                                             bias=b_[:, s0 + 127:s0 + 128]), tk["b"], tk["E"])
                t3 = V(lambda e: e.tensor_tensor(K[:, s0:s0 + 128], k_[:, s0:s0 + 128], E_[:, s0:s0 + 128], ALU.mult),
                       t, used)
                t = A(lambda e: e.activation(E_[:, s1:s1 + 128], b_[:, s1:s1 + 128], ACT.Exp), tk["b"], tk["E"])
                t4 = V(lambda e: e.tensor_tensor(Q[:, s1:s1 + 128], q_[:, s1:s1 + 128], E_[:, s1:s1 + 128], ALU.mult),
                       t, used)
                tq += [t3, t4]
            t_lev = at_tok
            yield
            for r in (0, 64):
                b, P = bank("B")
                for dt in range(2):
                    mm(P[:, dt * 128:(dt + 1) * 128], K[r:r + 64, dt * 256:dt * 256 + 128],
                       Q[r:r + 64, dt * 256 + 128:dt * 256 + 256], True, True, tq)
                t = mark()
                t_ao = V(lambda e: e.tensor_copy(ATo[:, r * 4:r * 4 + 256], P[:, 0:256]), t)
                free[b] = t_ao
            yield
            AT4 = v3(AT_, 128)
            t_sr = A(lambda e: e.activation(r_, r_, ACT.Silu), tk["r"])
            rr, RB = area(24), lv[:, 512:1536]
            for half in range(2):
                b, P = bank("B")
                for hh in range(2):
                    h = half * 2 + hh
                    vc = lambda i: v4[:, i, h * 128:(h + 1) * 128]
                    ha = (h % 2) * 4 + h // 2 * 2
                    ho = (h % 2) * 256 + h // 2 * 128
                    mm(P[:, hh * 256:hh * 256 + 128], vc(0), AT4[:, ha, :], True, True, t_lev, t_ao, tk["v"])
                    mm(P[:, hh * 256 + 128:hh * 256 + 256], vc(0), ATo[:, ho:ho + 128], True, False)
                    mm(P[:, hh * 256 + 128:hh * 256 + 256], vc(1), AT4[:, ha + 1, :], False, True)
                t_o = mark()
                o = qkb[:, half * 512:(half + 1) * 512]
                t_c = V(lambda e: e.tensor_copy(o, P[:, :]), t_o)
                free[b] = t_c
                sq = b_ if half == 0 else E_
                t = A(lambda e: e.activation(sq, o, ACT.Square), t_c, tq)
                yield
                b, P = bank("B")
                for n in range(4):
                    mm(P[:, n:n + 1], sq[:, n * 128:(n + 1) * 128], cn("one"), n == 0, n == 3, t, skip=True)
                ra, rb = rr[:, half * 12:half * 12 + 4], rr[:, half * 12 + 4:half * 12 + 8]
                t = V(lambda e: e.tensor_scalar(ra, P[:, 0:4], 1.0 / 128, EPS, ALU.mult, ALU.add), mark())
                free[b] = t
                t = power(rb, ra, 4, t)
                R = RB[:, half * 512:(half + 1) * 512]
                yield
                b, P = bank("B")
                for n in range(4):
                    transpose(P[:, n * 128:(n + 1) * 128], rb[:, n:n + 1].broadcast_to([128, 128]), t)
                t = V(lambda e: e.scalar_tensor_tensor(o, o, sm("ghead"), P[:, :], ALU.mult, ALU.mult), mark(), t_c)
                free[b] = t
                t = V(lambda e: e.tensor_tensor(o, o, r_[:, half * 512:half * 512 + 512], ALU.mult), t, t_sr)
                dst = slice(half * 512, half * 512 + 512)
                th = A(lambda e: e.copy(coh_[:, dst], o), t, tk["m1pe"])
                t = V(lambda e: e.tensor_tensor(col_[:, dst], o, f32(coh_[:, dst]), ALU.subtract), th)
                co_tok[2 * half] = co_tok[2 * half + 1] = t

        memlast = {}

        def mem_heads0():
            S = memT_
            war = tk["m1"] + [tk["m1pe"]]
            yield from pipeline([mem_head(0, h, mq, tk["mq"], S[:, (h % 2) * 1024:(h % 2) * 1024 + 512],
                                          S[:, (h % 2) * 1024 + 512:(h % 2) * 1024 + 1024],
                                          scb[:, (h % 2) * 4:(h % 2) * 4 + 4], h % 2, memlast, war) for h in range(4)], 2)

        weave(decay(), units(), after(14, mem_heads0()))

        def out_proj(names4, g):
            toks, xk = [], []
            for j, nm in enumerate(names4):
                (b, P, t), = projF(nm, CH, CL, co_tok, T, KOUT)
                t = V(lambda e: e.tensor_tensor(xt[:, 2 * j:2 * j + 2, :], v3(P[:, :], T), xt[:, 2 * j:2 * j + 2, :],
                                                ALU.add), t)
                free[b] = t
                toks += [t, t]
                for c in (2 * j, 2 * j + 1):
                    xk.append(split_x(xs[c], sm(g, c, c + 1), X(c), XLo(c), t))
            return toks, xk

        base = ARW - 1024 - 2 * (T + 2)
        YB, AB = arena[:, base:base + 1024], arena[:, base + 1024:ARW]

        def ffn(tag, xk, toks, cw, cb):
            yb = [YB[:, 0:512], YB[:, 512:1024]]
            abuf = [AB[:, 0:T + 2], AB[:, T + 2:2 * (T + 2)]]
            t_pad = None
            if cw is not None:
                for n in range(2):
                    t_pad = V(lambda e: e.memset(abuf[n][:, 0:2], 0.0))
            acc = [banks[4 + o // 2][:, (o % 2) * 256:(o % 2) * 256 + 256] for o in range(8)]
            f_pe = [None] * 4
            ftok = {}
            y_free = [None, None]
            rs = rs_[:, 0:T]

            def mix(f, b, P, t, t_rs):
                s = f % 2
                y, g2 = yb[s][:, 0:T], yb[s][:, T:2 * T]
                if cw is not None:
                    Ab = abuf[s]
                    w = lambda n: sm(cw, n * 22 + f, n * 22 + f + 1)
                    t1 = V(lambda e: e.tensor_tensor(Ab[:, 2:2 + T], P[:, 0:T], rs, ALU.mult), t, t_rs, y_free[s], t_pad)
                    t2 = A(lambda e: e.activation(y, Ab[:, 0:T], ACT.Copy, scale=w(0)), t1, y_free[s])
                    t3 = V(lambda e: e.tensor_tensor(g2, P[:, T:2 * T], rs, ALU.mult), t, t_rs, y_free[s])
                    free[b] = t3
                    t4 = V(lambda e: e.scalar_tensor_tensor(y, Ab[:, 1:1 + T], w(1), y, ALU.mult, ALU.add), t2)
                    t5 = V(lambda e: e.scalar_tensor_tensor(y, Ab[:, 2:2 + T], w(2), y, ALU.mult, ALU.add), t4)
                    t6 = A(lambda e: e.activation(y, y, ACT.Silu, bias=sm(cb, f, f + 1)), t5)
                else:
                    t1 = V(lambda e: e.tensor_tensor(y, P[:, 0:T], rs, ALU.mult), t, t_rs, y_free[s])
                    t3 = V(lambda e: e.tensor_tensor(g2, P[:, T:2 * T], rs, ALU.mult), t, t_rs, y_free[s])
                    free[b] = t3
                    t6 = A(lambda e: e.activation(y, y, ACT.Silu), t1)
                t7 = V(lambda e: e.tensor_tensor(g2, y, g2, ALU.mult), t6, t3)
                H, L = fh_[:, (f % 4) * T:(f % 4 + 1) * T], fl_[:, (f % 4) * T:(f % 4 + 1) * T]
                t8 = A(lambda e: e.copy(H, g2), t7, f_pe[f % 4])
                y_free[s] = ftok[f] = V(lambda e: e.tensor_tensor(L, g2, f32(H), ALU.subtract), t8, f_pe[f % 4])

            def down(p):
                i, (H, L, tl, _) = W.get(f"{tag}d{p}")
                H, L = v3(H, 1024), v3(L, 1024)
                if p == 0:
                    for b in range(4, 8):
                        assert free[b] != "held"
                        PE.wait(free[b])
                        free[b] = "held"
                marks = []
                for j in range(2):
                    f = 2 * p + j
                    FH, FL = fh_[:, (f % 4) * T:(f % 4 + 1) * T], fl_[:, (f % 4) * T:(f % 4 + 1) * T]
                    for o in range(8):
                        cs = slice(o * 128, (o + 1) * 128)
                        mm3(acc[o], H[:, j, cs], L[:, j, cs], FH, FL, f == 0 and o % 2 == 0, f == NF - 1,
                            ftok[f], tl[j], skip=True)
                        if f == NF - 1:
                            marks.append(mark())
                    f_pe[f % 4] = marks[-1] if f == NF - 1 else mark()
                W.release(i, f_pe[f % 4])
                return marks

            first = projF(f"{tag}u0", X, XLo, xk, T)[0]
            _, t_rs = token_rstd(xs, toks, rs, rst_[:, 0:2])
            mix(0, *first, t_rs)
            mix(1, *projF(f"{tag}u1", X, XLo, xk, T)[0], t_rs)
            for p in range(1, 11):
                u = [projF(f"{tag}u{2 * p + j}", X, XLo, xk, T)[0] for j in range(2)]
                down(p - 1)
                for j in range(2):
                    mix(2 * p + j, *u[j], t_rs)
            marks = down(10)
            new = []
            for o in range(8):
                t = V(lambda e: e.tensor_tensor(xs[o], acc[o], xs[o], ALU.add), marks[o | 1])
                new.append(t)
                free[4 + o // 2] = t
            return new, marks[-1]

        KOUT = [4, 5, 6, 7, 0, 1, 2, 3]
        toks, xk = out_proj(["Ao0", "Ao1", "Ao2", "Ao3"], "gffn0")
        new, t_pe = ffn("f0", xk, toks, "cw0", "cb0")

        at_[0] = 0
        slot = [area(1824), None, None]
        assert at_[0] <= 2048
        at_[0] = 2048 + 4 * TM
        nsac = area(NNS)
        t_nsac = load(nsac, nsac_d, sem("d_nsac"), toks[-1])
        al = lambda h: nsac[:, h * 256:(h + 1) * 256]
        cb_ = lambda h: nsac[:, 2048 + h * 32:2048 + (h + 1) * 32]
        slot[1] = area(1824)
        cblk = area(2496)
        slot[2] = cblk[:, 0:1824]
        X2, ev, kc = cblk[:, 0:512], cblk[:, 512:1024], cblk[:, 1984:2496]
        R = [cblk[:, 1024:1504], cblk[:, 1504:1984]]
        kk, vv = area(512), area(512)
        gT, kcm, vcm, gt = area(120), area(16), area(128), area(48)
        scb = area(3 * 16)
        mq_ = area(1024)
        mq = v3(mq_, T)
        bq_ = area(1024)
        bq = v3(bq_, T)

        ktk = enter(xs, new, "gkv", t_pe, CH, CL)
        kvb = projF("kvc", CH, CL, ktk, T)
        xk = enter(xs, new, "gmix1", t_pe)
        kvb += projF("kvk", CH, CL, ktk, T)
        t_rst, t_rs = token_rstd(xs, new, rs_[:, 0:T], rst_[:, 0:2])
        ktoks = []
        for dst, (b, P, t) in zip((kc, kk), kvb):
            t = V(lambda e: e.tensor_tensor(v3(dst, T), v3(P[:, :], T), bc2(rs_[:, 0:T]), ALU.mult), t, t_rs)
            free[b] = t
            ktoks.append(t)
        ev5 = ev.rearrange("p (v two m) -> p v two m", two=2, m=128)
        X25 = X2.rearrange("p (v g m) -> p v g m", g=2, m=128)
        t_ev = V(lambda e: e.tensor_copy(ev5, kc.rearrange("p (v m two) -> p v two m", two=2, m=128)), ktoks[0])
        d_x2 = sem("d_x2")
        for g in range(2):
            for par in range(2):
                src = ev5[g * 64:(g + 1) * 64, :, par, :]
                dst = X25[par * 64:(par + 1) * 64, :, g, :]
                ACTE.quiet(lambda e: e.dma_start(dst, src).then_inc(d_x2, 16), t_ev)
        t_x2 = (d_x2, 64)
        (b, P, t), = projT("kvv", CH, CL, ktk, [0, 128])
        t_kvpe = t
        for i in range(2):
            t_vv = V(lambda e: e.tensor_scalar(vv[:, i * 256:(i + 1) * 256], P[:, i * 256:(i + 1) * 256],
                                               rst_[:, i:i + 1], None, ALU.mult), t, t_rst)
        free[b] = t_vv

        def queries(tag, dst3, scl, toks_out):
            for j in range(2):
                (b, P, t), = projF(f"{tag}{j}", X, XLo, xk, T)
                t = V(lambda e: e.scalar_tensor_tensor(dst3[:, 2 * j:2 * j + 2, :], v3(P[:, :], T), scl,
                                                       bc2(rs_[:, 0:T]), ALU.mult, ALU.mult), t, t_rs)
                free[b] = t
                toks_out.append(t)
                yield

        mq_tok, bq_tok = [], []

        def compress():
            yield
            r_t = []
            for kv, pe_n in enumerate(("pek", "pev")):
                for g in range(2):
                    Rv = R[kv].rearrange("p (c g n) -> p c g n", g=2, n=15)[:, :, g, :]
                    base = X25[:, kv, g, :].rearrange("p (n c) -> p c n", c=8)
                    pe = sm(pe_n).unsqueeze(2)
                    for hf in range(2):
                        t = V(lambda e: e.tensor_tensor(
                            Rv[:, hf * 8:(hf + 1) * 8, :], base[:, :, hf:hf + 15],
                            pe[:, hf * 8:(hf + 1) * 8, :].broadcast_to([128, 8, 15]), ALU.add), t_x2)
                r_t.append(t)
            yield
            t_g = []
            for kv in range(2):
                b, P = bank("B")
                nm = "ck" if kv == 0 else "cv"
                for half in range(2):
                    i, (src, _, _) = W.get(f"{nm}{half}")
                    for hid in range(2):
                        for c in range(8):
                            cc = half * 8 + c
                            mm(P[:, hid * 32:hid * 32 + 30], v3(src, 256)[:, c, hid * 128:(hid + 1) * 128],
                               R[kv][:, cc * 30:(cc + 1) * 30], half == 0 and hid == 0 and c == 0,
                               half == 1 and c == 7, r_t[kv], W.landed[i], skip=True)
                    t = mark()
                    W.release(i, t)
                t = A(lambda e: e.activation(v3(gT[:, kv * 60:(kv + 1) * 60], 30), v3(P[:, 0:64], 32)[:, :, 0:30],
                                             ACT.Gelu_apprx_tanh), t)
                free[b] = t
                t_g.append(t)
            yield
            g4 = gT.rearrange("p (v c g n) -> p v c g n", v=2, c=2, g=2)
            b, P = bank("B")
            for g in range(2):
                for c in range(2):
                    mm(P[g * 64:(g + 1) * 64, 0:15], sm("wck2")[:, c * 64:(c + 1) * 64], g4[:, 0, c, g, :],
                       c == 0, c == 1, t_g)
            tk["kcm"] = V(lambda e: e.tensor_copy(kcm[:, 0:15], P[:, 0:15]), mark())
            free[b] = tk["kcm"]
            b, P = bank("B")
            for g in range(2):
                for c in range(2):
                    mm(P[0:15, g * 64:(g + 1) * 64], g4[:, 1, c, g, :], sm("wcv2")[:, c * 64:(c + 1) * 64], c == 0, c == 1)
            tk["vcm"] = V(lambda e: e.tensor_copy(vcm[0:15, :], P[0:15, 0:128]), mark())
            free[b] = tk["vcm"]

        def gates():
            b, P = bank("A")
            for i in range(2):
                for c in range(8):
                    a = 128 + c * 24
                    xa, xb = X(c)[:, i * 128:(i + 1) * 128], XLo(c)[:, i * 128:(i + 1) * 128]
                    o = P[:, i * 24:i * 24 + 24]
                    mm(o, xa, smh[:, a:a + 24], c == 0, False, xk[c])
                    mm(o, xb, smh[:, a:a + 24], False, False)
                    mm(o, xa, sml[:, a:a + 24], False, c == 7)
            t = mark()
            for i in range(2):
                t2 = A(lambda e: e.activation(gt[:, i * 24:i * 24 + 24], P[:, i * 24:i * 24 + 24], ACT.Sigmoid,
                                              scale=rst_[:, i:i + 1]), t, t_rst)
            free[b] = t2
            g0 = gt[:, 0:24].rearrange("p (h n) -> p h n", n=3)[:, :, 0]
            tk["gt"] = V(lambda e: e.tensor_scalar(g0, g0, cn("valid", 0, 1), None, ALU.mult), t2, t_cst)

        pair = {}
        last = {}

        def nsa_head(j, g, key):
            h = g * 4 + j
            r = g * 64
            EE, PT = slot[key][:, 0:800], slot[key][:, 800:1824]
            st = scb[:, key * 16:key * 16 + 12]
            war = [last.get(key)]
            q = lambda i: bq[r:r + 64, j, i * 128:(i + 1) * 128]
            ks = lambda w: kk[r:r + 64, w * 256:(w + 1) * 256]
            b1, P1 = bank("A")
            for w in range(2):
                mm(P1[:, w * 256:(w + 1) * 256], q(1), ks(w), True, True, bq_tok, ktoks, tk["kcm"])
            t1 = mark()
            b0, P0 = bank("A")
            for w in range(2):
                mm(P0[:, w * 128:(w + 1) * 128], q(0), ks(w)[:, 0:128], True, True)
            for i in range(2):
                mm(P0[:, 256 + i * 16:256 + i * 16 + 15], q(i), kcm[r:r + 64, 0:15], True, True)
            t0 = mark()
            t2 = V(lambda e: e.tensor_tensor(v3(EE[:, 0:512], 256), v3(P1[:, :], 256), bc2(al(h)), ALU.add),
                   t1, t_nsac, war)
            free[b1] = t2
            t5 = V(lambda e: e.tensor_reduce(st[:, 0:2], v3(EE[:, 0:512], 256), AX.X, ALU.max, negate=True), t2)
            for n in range(2):
                t8 = A(lambda e: e.activation(EE[:, n * 256:(n + 1) * 256], EE[:, n * 256:(n + 1) * 256], ACT.Exp,
                                              bias=st[:, n:n + 1], accum_out=st[:, 6 + n:7 + n]), t5, war)
            t3 = V(lambda e: e.tensor_tensor(v3(EE[:, 512:768], 128), v3(P0[:, 0:256], 128), bc2(al(h)[:, 128:256]),
                                             ALU.add), t0, war)
            t4 = V(lambda e: e.tensor_tensor(v3(EE[:, 768:798], 15), v3(P0[:, 256:288], 16)[:, :, 0:15],
                                             v3(cb_(h), 16)[:, :, 0:15], ALU.add), t0)
            free[b0] = t4
            t6 = V(lambda e: e.tensor_reduce(st[:, 2:4], v3(EE[:, 512:768], 128), AX.X, ALU.max, negate=True), t3)
            t7 = V(lambda e: e.tensor_reduce(st[:, 4:6], v3(EE[:, 768:798], 15), AX.X, ALU.max, negate=True), t4)
            for n, (a, z) in enumerate([(512, 640), (640, 768), (768, 783), (783, 798)]):
                t8 = A(lambda e: e.activation(EE[:, a:z], EE[:, a:z], ACT.Exp, bias=st[:, 2 + n:3 + n],
                                              accum_out=st[:, 8 + n:9 + n]), t7)
            t9 = V(lambda e: e.reciprocal(st[:, 6:12], st[:, 6:12]), t8)
            ga = gt[:, 24 + 3 * h + 1:24 + 3 * h + 3]
            gb = gt[:, 3 * h + 1:3 * h + 3]
            gc = gt.rearrange("p (i x) -> p i x", i=2)[:, :, 3 * h]
            t10 = V(lambda e: e.tensor_tensor(st[:, 6:8], st[:, 6:8], ga, ALU.mult), t9, tk["gt"])
            t11 = V(lambda e: e.tensor_tensor(st[:, 8:10], st[:, 8:10], gb, ALU.mult), t9)
            t12 = V(lambda e: e.tensor_tensor(st[:, 10:12], st[:, 10:12], gc, ALU.mult), t9)
            t13 = []
            for a, z, n, o in ((512, 768, 128, 8), (0, 512, 256, 6), (768, 798, 15, 10)):
                t13 = V(lambda e: e.tensor_tensor(v3(EE[:, a:z], n), v3(EE[:, a:z], n),
                                                  st[:, o:o + 2].unsqueeze(2).broadcast_to([128, 2, n]), ALU.mult), t12)
            yield
            bx, Px = bank("B")
            for w in range(2):
                transpose(Px[:, w * 256:w * 256 + 128], EE[:, 512 + w * 128:640 + w * 128], t13)
                transpose(Px[:, w * 256 + 128:w * 256 + 256], EE[:, w * 256:w * 256 + 128])
            tx = mark()
            by, Py = bank("B")
            for w in range(2):
                transpose(Py[:, w * 128:w * 128 + 128], EE[:, w * 256 + 128:w * 256 + 256])
            for i in range(2):
                transpose(Py[0:15, 256 + i * 128:384 + i * 128], EE[:, 768 + i * 15:783 + i * 15])
            ty = mark()
            t14 = A(lambda e: e.copy(PT[:, 0:512], Px[:, :]), tx, war)
            free[bx] = t14
            t15 = A(lambda e: e.copy(PT[:, 512:768], Py[:, 0:256]), ty, war)
            t16 = A(lambda e: e.copy(PT[0:15, 768:1024], Py[0:15, 256:512]), ty)
            free[by] = t16
            yield
            if g == 0:
                pair[j] = bank("A")
            bo, Po = pair[j]
            O = Po[r:r + 64, 0:256]
            vs = lambda i, w: vv[:, i * 256 + w * 128 + g * 64:i * 256 + w * 128 + g * 64 + 64]
            mm(O, vcm[0:15, g * 64:(g + 1) * 64], PT[0:15, 768:1024], True, False, tk["vcm"], t_vv, t14, t16, skip=True)
            mm(O, vs(0, 0), PT[:, 0:256], False, False, skip=True)
            mm(O, vs(0, 1), PT[:, 256:512], False, False, skip=True)
            mm(O[:, 128:256], vs(1, 0), PT[:, 512:640], False, False, skip=True)
            mm(O[:, 128:256], vs(1, 1), PT[:, 640:768], False, True, skip=True)
            last[key] = mark()
            if g == 1:
                t18 = split_p(coh[:, j, :], col[:, j, :], Po[:, 0:T], last[key], t_kvpe)
                free[bo] = t18
                co_tok[j] = t18
            yield

        def mem_heads1():
            yield from pipeline([mem_head(1, h, mq, mq_tok, slot[h % 2][:, 0:512], slot[h % 2][:, 512:1024],
                                          scb[:, (h % 2) * 16:(h % 2) * 16 + 4], h % 2, last, [t_kvpe]) for h in range(4)], 2)

        gates()
        weave(queries("Bm", mq, 128.0 ** -0.5, mq_tok))
        weave(compress(), after(1, mem_heads1()), after(3, queries("Bq", bq, 0.125, bq_tok)))
        weave(pipeline([nsa_head(j, g, (2 * j + g) % 3) for j in range(4) for g in range(2)], 3))
        toks, xk = out_proj(["Bo0", "Bo1", "Bo2", "Bo3"], "gffn1")
        at_[0] = 0
        selc, meta_ = area(1536), area(8 * NM)
        meta = v3(meta_, NM)
        d_meta = sem("d_meta")
        load(selc, sel_d, d_meta, toks[-1], [last.get(k) for k in range(3)])
        load(meta_, meta_d, d_meta)
        t_meta = (d_meta, 32)
        gp = area(8)
        qn8 = area(1)
        t_gp = V(lambda e: e.tensor_tensor(gp, sm("gfin"), sm("n1"), ALU.mult), toks[-1])
        t_qn = V(lambda e: e.tensor_scalar(qn8, sm("qn"), 0.125, None, ALU.mult))
        new, t_pe = ffn("f1", xk, toks, "cw1", "cb1")

        at_[0] = 2048 + 4 * TM
        cq_, ck_ = area(1024), area(4 * TM)
        cq, ck = v3(cq_, T), v3(ck_, TM)
        cv_ = area(3 * 512)
        cvv = v3(cv_, 512)
        cT = area(TM)
        uT = area(4 * TM)
        uu = v3(uT, TM)
        pa, pb = area(TM), area(TM)
        sqh = area(2 * 2 * TM)
        r1b = sqh[:, 0:T]
        hs = area(160)
        sl2 = [area(1056) for _ in range(3)]
        r2 = area(16)
        XF = lambda c: xh[:, c, :]
        XFL = lambda c: xl[:, c, :]
        xk = []
        for c in range(8):
            ta = split_x(xs[c], gp[:, c:c + 1], X(c), XLo(c), new[c], t_gp, war=t_pe)
            xk.append([ta])
        for c in range(8):
            xk[c].append(split_x(meta[:, c, :], sm("n1", c, c + 1), xh[:, c, 0:NM], xl[:, c, 0:NM], t_meta, war=t_pe))
        xq = [t[0] for t in xk]
        qbk = [projF("Cq0", X, XLo, xq, T)[0]]
        b, P = bank("B")
        for c in range(8):
            for v, (src, sc, tt) in enumerate(((xs[c], 1.0, new[c]), (xs[c], sm("gfin", c, c + 1), new[c]),
                                               (meta[:, c, :], 1.0, t_meta))):
                k, s, t = square(src, tt, sc)
                if v < 2:
                    for n in range(2):
                        mm(P[:, 2 * v + n:2 * v + n + 1], s[:, n * 128:(n + 1) * 128], cn("one"),
                           c == 0 and v == 0 and n == 0, c == 7, t, skip=True)
                else:
                    mm(P[0:NM, 4:5], s[:, 0:NM], cn("one"), False, c == 7, t, skip=True)
                sq_free[k] = mark()
        t = sq_free[k]
        ta = V(lambda e: e.tensor_scalar(r2[:, 0:4], P[:, 0:4], 1.0 / D, None, ALU.mult), t)
        tb = V(lambda e: e.tensor_scalar(r2[0:NM, 4:5], P[0:NM, 4:5], 1.0 / D, EPS, ALU.mult, ALU.add), t)
        free[b] = tb
        tc = V(lambda e: e.tensor_scalar(r2[:, 0:2], r2[:, 0:2], EPS, None, ALU.add), ta)
        t1 = power(r2[:, 6:8], r2[:, 0:2], 2, tc)
        td = V(lambda e: e.tensor_tensor(r2[:, 2:4], r2[:, 2:4], r2[:, 6:8], ALU.mult), t1)
        td = V(lambda e: e.tensor_tensor(r2[:, 2:4], r2[:, 2:4], r2[:, 6:8], ALU.mult), td)
        td = V(lambda e: e.tensor_scalar(r2[:, 2:4], r2[:, 2:4], EPS, None, ALU.add), td)
        t2 = power(r2[:, 8:10], r2[:, 2:4], 2, td)
        t3 = power(rst_[0:NM, 2:3], r2[0:NM, 4:5], 1, tb)
        t_rst = V(lambda e: e.tensor_tensor(rst_[:, 0:2], r2[:, 6:8], r2[:, 8:10], ALU.mult), t2, t3)
        qbk.append(projF("Cq1", X, XLo, xq, T)[0])
        t_rs = spread(rs_[:, :], rst_, [(2, 0, NM), (0, NM, 128), (1, NM + 128, 128)], t_rst)
        t_r1 = spread(r1b, r2[:, 6:8], TT, t1)
        kbk = projF("Ck0", XF, XFL, xk, TM)
        cq_tok, ck_tok = [], []
        for j, (b, P, t) in enumerate(qbk):
            t = V(lambda e: e.tensor_tensor(cq[:, 2 * j:2 * j + 2, :], v3(P[:, :], T), bc2(rs_[:, NM:TM]), ALU.mult), t, t_rs)
            free[b] = t
            cq_tok.append(t)
        for n, (b, P, t) in enumerate(kbk):
            t = V(lambda e: e.tensor_tensor(ck[:, n, :], P[:, 0:TM], rs_[:, :], ALU.mult), t, t_rs)
            free[b] = t
            ck_tok.append(t)
        for c in range(8):
            new[c] = V(lambda e: e.scalar_tensor_tensor(xs[c], xs[c], sm("gfin", c, c + 1), r1b, ALU.mult, ALU.mult),
                       t_r1, sq_free)
        t_sq = [new[-1], None]

        def head_norm(buf, dst3, w, tiles, gn, toks, out):
            s4 = sqh[:, 0:4 * w]
            tsq = [A(lambda e: e.activation(v3(s4, w)[:, 2 * j:2 * j + 2, :], dst3[:, 2 * j:2 * j + 2, :], ACT.Square),
                     toks, t_sq[0]) for j in range(2)]
            yield
            b, P = bank("B")
            for j in range(4):
                for n, (a, m) in enumerate(tiles):
                    mm(P[0:m, n * 8 + 2 * j:n * 8 + 2 * j + 2], v3(s4, w)[:, j, a:a + m], cn("halves"),
                       j == 0 and n == 0, j == 3, tsq, skip=True)
            t_sq[0] = mark()
            hv, hr = buf[:, 0:24], buf[:, 24:48]
            tp = []
            for n, (a, m) in enumerate(tiles):
                t = V(lambda e: e.tensor_scalar(hv[0:m, n * 8:n * 8 + 8], P[0:m, n * 8:n * 8 + 8], 1.0 / 64, EPS,
                                                ALU.mult, ALU.add), t_sq[0])
                tp.append(power(hr[0:m, n * 8:n * 8 + 8], hv[0:m, n * 8:n * 8 + 8], 8, t))
            free[b] = t
            yield
            b, P = bank("B")
            for n, (a, m) in enumerate(tiles):
                transpose(P[0:8, a:a + m], hr[0:m, n * 8:n * 8 + 8], tp)
            rows = s4[0:8, 0:w]
            t_r = V(lambda e: e.tensor_copy(rows, P[0:8, 0:w]), mark())
            free[b] = t_r
            yield
            for j in range(4):
                b, P = bank("B")
                mm(P[:, 0:w], selc[0:8, 1024 + j * 128:1024 + (j + 1) * 128], rows, True, True, t_r, t_meta)
                t_sq[0] = mark()
                t = V(lambda e: e.scalar_tensor_tensor(dst3[:, j, :], dst3[:, j, :], gn, P[:, 0:w], ALU.mult, ALU.mult),
                      t_sq[0], tsq)
                free[b] = t
                out.append(t)

        cv_tok = []
        fin_q, fin_k = [], []
        ub = []

        def forget():
            fz, fa, fb, lf = hs[:, 48:72], hs[:, 72:96], hs[:, 96:120], hs[:, 120:144]
            b, P = bank("A")
            for n, a in enumerate((NM, NM + 128, 0)):
                for c in range(8):
                    o, s = P[:, n * 8:n * 8 + 8], 320 + c * 8
                    mm(o, XF(c)[:, a:a + 128], smh[:, s:s + 8], c == 0, False, xk[c])
                    mm(o, XFL(c)[:, a:a + 128], smh[:, s:s + 8], False, False)
                    mm(o, XF(c)[:, a:a + 128], sml[:, s:s + 8], False, c == 7)
            t = mark()
            t1 = V(lambda e: e.memset(fz, 0.0))
            for n in range(3):
                m = 128 if n < 2 else NM
                t2 = V(lambda e: e.scalar_tensor_tensor(
                    fz[0:m, n * 8:n * 8 + 8], P[0:m, n * 8:n * 8 + 8], rst_[0:m, n:n + 1], sm("bfg")[0:m, :],
                    ALU.mult, ALU.add), t, t_rst, t1)
            free[b] = t2
            t_lf = softplus_neg(lf, fz, t2, fa, fb)
            yield
            t1 = V(lambda e: e.memset(cT, 0.0))
            b, P = bank("B")
            two = cst[:, CN["tri"][0]:CN["tri"][0] + 256]
            for r in (0, 64):
                mm(P[r:r + 8, 0:TM], lf[0:NM, 16:24], cn("trim")[0:NM, :], True, False, t_lf, skip=True)
                mm(P[r:r + 8, NM:TM], lf[:, 0:8], two, False, False, skip=True)
                mm(P[r:r + 8, NM + 128:TM], lf[:, 8:16], cn("tri"), False, True, skip=True)
            t = mark()
            for r in (0, 64):
                tk["cT"] = V(lambda e: e.tensor_copy(cT[r:r + 8, :], P[r:r + 8, 0:TM]), t, t1)
            free[b] = tk["cT"]

        def units2():
            for n, (b, P, t) in enumerate(projF("Ck1", XF, XFL, xk, TM)):
                t = V(lambda e: e.tensor_tensor(ck[:, 2 + n, :], P[:, 0:TM], rs_[:, :], ALU.mult), t, t_rs)
                free[b] = t
                ck_tok.append(t)
            yield
            for j in range(2):
                res = projT(f"Cv{j}", XF, XFL, xk, [NM, NM + 128, 0])
                for i in range(3):
                    b, P, t = res[i // 2]
                    n = 128 if i < 2 else NM
                    t = V(lambda e: e.tensor_scalar(
                        cvv[0:n, i, j * 256:(j + 1) * 256], P[0:n, (i % 2) * 256:(i % 2) * 256 + 256],
                        rst_[0:n, i:i + 1], None, ALU.mult), t, t_rst)
                    if i > 0:
                        free[b] = t
                cv_tok.append(t)
                yield

        def pools(g, key):
            b, P, t = ubk[g]
            u = uu[:, g, :]
            t = V(lambda e: e.tensor_tensor(u, P[:, 0:TM], rs_[:, :], ALU.mult), t, t_rs)
            free[b] = t
            src, bufs, n, lo = u, [pa, pb], 1, 0
            for s in range(g + 1):
                dst = bufs[s % 2]
                lo += n
                t = V(lambda e: e.tensor_tensor(dst[:, lo:TM], src[:, lo:TM], src[:, lo - n:TM - n], ALU.add),
                      t, tk.get("pool"))
                src = dst
                n *= 2
            dst = bufs[(g + 1) % 2]
            t = V(lambda e: e.scalar_tensor_tensor(dst[:, NM:TM], src[:, NM:TM], 1.0 / n, u[:, NM:TM], ALU.mult,
                                                   ALU.subtract), t, tk.get("pool"))
            yield
            b, P = bank("B")
            mm(P[:, 0:T], sm("wpool", g * 128, (g + 1) * 128), dst[:, NM:TM], True, True, t)
            tk["pool"] = mark()
            H, L = coh[:, 4 + g, :], col[:, 4 + g, :]
            t = A(lambda e: e.activation(H, P[:, 0:T], ACT.Copy, scale=sm("pscale", g, g + 1)), tk["pool"])
            t = V(lambda e: e.scalar_tensor_tensor(L, P[:, 0:T], sm("pscale", g, g + 1), f32(H), ALU.mult,
                                                   ALU.subtract), t)
            free[b] = t
            co_tok[4 + g] = t

        weave(head_norm(hs, cq, T, [(0, 128), (128, 128)], qn8, cq_tok + [t_qn], fin_q), units2(), after(1, forget()))
        last = {}

        def head2(j, hh, key):
            h, r = 2 * j + hh, hh * 64
            EE, PT, PM = sl2[key][:, 0:416], sl2[key][:, 416:800], sl2[key][:, 800:1056]
            st = hs[:, 144 + key * 4:148 + key * 4]
            war = last.get(key)
            sel = selc[r:r + 64, h * 128:(h + 1) * 128]
            b, P = bank("A")
            for i, (o, n) in enumerate(((272, 144), (0, 272))):
                mm(P[:, o:o + n], cq[r:r + 64, j, i * 128:(i + 1) * 128], ck[r:r + 64, j, 0:n], True, False,
                   fin_q, fin_k, tk["cT"], t_meta)
                mm(P[:, o:o + n], sel, cT[r:r + 64, 0:n], False, True)
            t = mark()
            m2 = cn("mask2")
            t1 = V(lambda e: e.tensor_tensor(EE[:, 0:272], P[:, 0:272], m2, ALU.add), t, war)
            t2 = V(lambda e: e.tensor_tensor(EE[:, 272:416], P[:, 272:416], m2[:, 128:272], ALU.add), t)
            free[b] = t2
            t3 = V(lambda e: e.tensor_reduce(st[:, 0:1], EE[:, 0:272], AX.X, ALU.max, negate=True), t1)
            t4 = V(lambda e: e.tensor_reduce(st[:, 1:2], EE[:, 272:416], AX.X, ALU.max, negate=True), t2)
            for n, (a, z) in enumerate(((0, 272), (272, 416))):
                t5 = A(lambda e: e.activation(EE[:, a:z], EE[:, a:z], ACT.Exp, bias=st[:, n:n + 1],
                                              accum_out=st[:, 2 + n:3 + n]), t4)
            t6 = V(lambda e: e.reciprocal(st[:, 2:4], st[:, 2:4]), t5)
            for n, (a, z) in enumerate(((0, 272), (272, 416))):
                t7 = V(lambda e: e.tensor_scalar(EE[:, a:z], EE[:, a:z], st[:, 2 + n:3 + n], None, ALU.mult), t6)
            yield
            bx, Px = bank("B")
            transpose(Px[:, 0:128], EE[:, 272 + NM:416], t7)
            transpose(Px[:, 128:256], EE[:, NM:NM + 128])
            transpose(Px[:, 256:384], EE[:, NM + 128:272])
            tx = mark()
            by, Py = bank("B")
            transpose(Py[0:NM, 0:128], EE[:, 272:272 + NM])
            transpose(Py[0:NM, 128:256], EE[:, 0:NM])
            ty = mark()
            t8 = A(lambda e: e.copy(PT, Px[:, 0:384]), tx, war)
            free[bx] = t8
            t9 = A(lambda e: e.copy(PM[0:NM, :], Py[0:NM, 0:256]), ty, war)
            free[by] = t9
            yield
            if hh == 0:
                pair[j] = bank("A")
            bo, Po = pair[j]
            O = Po[r:r + 64, 0:256]
            vs = lambda i, n: cvv[0:n, i, h * 64:(h + 1) * 64]
            mm(O, vs(2, NM), PM[0:NM, :], True, False, cv_tok, t8, t9, skip=True)
            mm(O, vs(0, 128), PT[:, 0:256], False, False, skip=True)
            mm(O[:, 128:256], vs(1, 128), PT[:, 256:384], False, True, skip=True)
            last[key] = mark()
            if hh == 1:
                t18 = split_p(coh[:, j, :], col[:, j, :], Po[:, 0:T], last[key])
                free[bo] = t18
                co_tok[j] = t18
            yield

        ubk = []

        def units3():
            ubk.extend(projF("Cu0", XF, XFL, xk, TM))
            yield
            yield from pools(0, 0)
            yield
            yield from pools(1, 0)
            yield
            ubk.extend(projF("Cu1", XF, XFL, xk, TM))
            yield
            yield from pools(2, 0)
            yield
            yield from pools(3, 0)

        u3 = units3()
        weave(head_norm(hs, ck, TM, [(NM, 128), (NM + 128, 128), (0, NM)], sm("kn"), ck_tok, fin_k), (x for x in [next(u3)]))
        weave(pipeline([head2(j, hh, (2 * j + hh) % 3) for j in range(4) for hh in range(2)], 3), u3)
        toks, xk = out_proj(["Co0", "Co1", "Co2", "Co3"], "n2")
        new, t_pe = ffn("f2", xk, toks, None, None)
        s_out = sem("s_out")
        for c in range(8):
            SP.quiet(lambda e: e.dma_start(out_d[:, c * T:(c + 1) * T], xs[c]).then_inc(s_out, 16), new[c])
        SP.wait((s_out, 128))


def constants():
    f = np.float32
    p = np.arange(128)
    tri = (p[:, None] <= p[None, :]).astype(f)
    c = {
        "ident": np.eye(128, dtype=f), "ones": np.ones((128, 128), f), "tri": tri,
        "halves": (p[:, None] // 64 == np.arange(2)[None, :]).astype(f), "mhalf": np.full((128, 32), -0.5, f),
        "trim": (p[:, None] <= np.arange(TM)[None, :]).astype(f),
        "valid": np.stack([(p >= 31).astype(f), np.ones(128, f)], 1),
        "one": np.ones((128, 1), f),
    }
    causal = np.where(p[None, :] <= p[:, None], 0, NEG).astype(f)
    c["mask2"] = np.concatenate([np.zeros((128, 144), f), causal], 1)
    sel = np.zeros((128, 8, 128), f)
    for h in range(8):
        sel[h, h] = sel[64 + h, h] = -1
    spr = np.zeros((128, 4, 128), f)
    for h in range(8):
        spr[h, h // 2, (h % 2) * 64:(h % 2 + 1) * 64] = 1
    sel = np.concatenate([sel.reshape(128, -1), spr.reshape(128, -1)], 1)
    cst = np.concatenate([c[n] for n, _ in CONST], 1)
    gm = []
    for m in LEVELS:
        s, t = p[:, None], p[None, :]
        if m:
            gm.append((s // (2 * m) == t // (2 * m)) & (s % (2 * m) < m) & (t % (2 * m) >= m))
        else:
            gm.append(s == t)
    gm = np.concatenate(gm, 1).astype(f)
    al, cb = [], []
    for h in range(8):
        slope = f(2.0 ** -(h + 1))
        t, s = p[:, None], p[None, :]
        diag = np.where(s <= t, -slope * (t - s), NEG).astype(f)
        off = (-slope * (128 + t - s)).astype(f)
        al.append(np.concatenate([off, diag], 1))
        e = np.arange(16)[None, :] * 16 + 31
        for i in range(2):
            d = i * 128 + t - e
            cb.append(np.where(d >= 0, -slope * d, NEG).astype(f))
    ns = np.concatenate(al + cb, 1)
    return cst, gm, ns, sel


def pack(i):
    d = {}

    def cols(w, a, b):
        k = w.shape[0] // 128
        return w.reshape(k, 128, -1)[:, :, a:b].transpose(1, 0, 2).reshape(128, -1)

    units = {}

    def put(prefix, w, a, n):
        for j in range(n):
            units[f"{prefix}{j}"] = cols(w, a + 256 * j, a + 256 * (j + 1))

    aw = i["a_w_in"][0]
    units["Aq"], units["Ak"] = cols(aw, 0, 256), cols(aw, 256, 512)
    put("Av", aw, 512, 2)
    put("Ar", aw, 1024, 2)
    put("Am", aw, 1552, 2)
    for l in range(2):
        put(f"m{l}k", i["w_mem_kv"][l], 0, 2)
        put(f"m{l}v", i["w_mem_kv"][l], 512, 2)
    put("Ao", i["a_w_out"][0], 0, 4)

    def ffn(tag, wa, wb, wd):
        for f in range(NF):
            c = slice(f * 128, (f + 1) * 128)
            units[f"{tag}u{f}"] = cols(np.concatenate([wa[:, c], wb[:, c]], 1), 0, 256)
        for p in range(11):
            units[f"{tag}d{p}"] = cols(wd[p * 256:(p + 1) * 256], 0, 1024)

    for l in range(2):
        ffn(f"f{l}", i["w_up"][l][:, :2816], i["w_up"][l][:, 2816:], i["w_down"][l])
    ffn("f2", i["w_gate_2"][0], i["w_up_2"][0], i["w_down_2"][0])
    kv = i["w_kv"]
    seg = lambda n: kv[:, n * 128:(n + 1) * 128]
    units["kvc"] = cols(kv[:, 0:256], 0, 256)
    units["kvk"] = cols(np.concatenate([seg(2), seg(4)], 1), 0, 256)
    units["kvv"] = cols(np.concatenate([seg(3), seg(5)], 1), 0, 256)
    for n, w in (("ck", i["w_ck1"]), ("cv", i["w_cv1"])):
        for j in range(2):
            units[f"{n}{j}"] = cols(w[j * 1024:(j + 1) * 1024], 0, 256)
    bw = i["b_w_in"][0]
    order = [0, 4, 1, 5, 2, 6, 3, 7]
    bq = bw[:, :512].reshape(D, 8, 64)[:, order].reshape(D, 512)
    put("Bq", bq, 0, 2)
    put("Bm", bw, 536, 2)
    bo = i["b_w_out"][0]
    bo = np.concatenate([bo[:512].reshape(8, 64, D)[order].reshape(512, D), bo[512:]], 0)
    put("Bo", bo, 0, 4)
    cw = i["w_in_2"][0]
    put("Cq", cw, 0, 2)
    put("Ck", cw, 512, 2)
    put("Cv", cw, 1024, 2)
    put("Cu", cw, 1544, 2)
    put("Co", i["w_out_2"][0], 0, 4)
    d["w"] = np.stack([units[n] for n in unit_names()])

    vec = lambda v: v.reshape(-1, 128).T
    bc = lambda v: np.broadcast_to(v.reshape(1, -1), (128, v.size))
    s = {
        "gmix0": vec(i["g_mix"][0]), "gmix1": vec(i["g_mix"][1]), "gffn0": vec(i["g_ffn"][0]),
        "gffn1": vec(i["g_ffn"][1]), "gmem0": vec(i["g_mem"][0]), "gmem1": vec(i["g_mem"][1]),
        "gkv": vec(i["g_kv"]), "gfin": vec(i["g_final"]), "n1": vec(i["norm1_w_2"][0]), "n2": vec(i["norm2_w_2"][0]),
        "ghead": vec(i["a_g_head"][0]), "pscale": vec(i["pool_scale_2"][0]),
        "qn": vec(np.concatenate([i["q_norm_w_2"][0]] * 2)), "kn": vec(np.concatenate([i["k_norm_w_2"][0]] * 2)),
        "bfg": bc(i["b_fgate_2"][0]),
        "pek": i["pe_k"].reshape(16, 128).T, "pev": i["pe_v"].reshape(16, 128).T,
        "cb0": vec(i["conv_b"][0]), "cb1": vec(i["conv_b"][1]),
        "walr": cols(aw, 1536, 1552), "wgl": cols(bw, 512, 536), "wfg": cols(cw, 1536, 1544),
        "balpha": bc(i["a_b_alpha"][0]), "wck2": cols(i["w_ck2"], 0, 64), "wcv2": cols(i["w_cv2"], 0, 64),
        "wpool": i["w_pool_2"][0].transpose(1, 0, 2).reshape(128, 512),
    }
    for l in range(2):
        s[f"cw{l}"] = np.concatenate([vec(i["conv_w"][l][n]) for n in range(3)], 1)
    wa = np.zeros((128, 256), np.float32)
    wa[:16] = i["a_w_alpha"][0]
    s["walpha"] = wa
    d["small"] = np.concatenate([s[n] for n, _ in SMALL], 1)
    d["x"] = cols(i["x"][0].T, 0, T)
    d["mem"] = cols(i["mem"][0].T, 0, T)
    d["meta"] = cols(i["meta_tokens_2"].T, 0, NM)
    d["const"], d["gmask"], d["nsac"], d["sel"] = constants()
    return {k: np.ascontiguousarray(v) for k, v in d.items()}


_ORDER = ["w", "x", "mem", "meta", "small", "const", "gmask", "nsac", "sel"]


def kernel(**inputs):
    import concourse.bacc as _bacc
    from concourse.bass_utils import run_bass_kernel_spmd as _run

    d = pack({k: np.asarray(v) for k, v in inputs.items()})
    nc = _bacc.Bacc("TRN2", target_bir_lowering=False, num_devices=1)
    args, arrays = [], {}
    for n in _ORDER:
        arrays[f"in_{n}"] = d[n]
        args.append(nc.dram_tensor(f"in_{n}", d[n].shape, F32, kind="ExternalInput").ap())
    args.append(nc.dram_tensor("out_0", (128, 8 * T), F32, kind="ExternalOutput").ap())
    build(nc, *args)
    r = _run(nc, [arrays], core_ids=[0])
    o = np.asarray(r.results[0]["out_0"])
    return np.ascontiguousarray(o.reshape(128, 8, T).transpose(2, 1, 0).reshape(1, T, D))
```

```python
import numpy as np

import concourse.bass as bass
from concourse import mybir
from contextlib import ExitStack

F32 = mybir.dt.float32
F32R = mybir.dt.float32r
U32 = mybir.dt.uint32
ALU = mybir.AluOpType
ACT = mybir.ActivationFunctionType
AX = mybir.AxisListType
EPS = 1e-6
NEG = -1.0e30

D = 1024
T = 256
NM = 16
TM = T + NM
NF = 22
UW = 2048
LEVELS = [64, 32, 16, 8, 4, 2, 1, 0]


def unit_names():
    up = lambda tag: [f"{tag}u0", f"{tag}u1"] + [
        n for p in range(1, 11) for n in (f"{tag}u{2 * p}", f"{tag}u{2 * p + 1}", f"{tag}d{p - 1}")
    ] + [f"{tag}d10"]
    return (
        ["Aq", "Ak", "Am0", "Am1", "m0k0", "m0k1", "m0v0", "m0v1", "Av0", "Av1", "m1k0", "m1k1", "m1v0", "m1v1",
         "Ar0", "Ar1", "Ao0", "Ao1", "Ao2", "Ao3"]
        + up("f0")
        + ["kvc", "kvk", "kvv", "Bq0", "Bq1", "Bm0", "Bm1", "ck0", "ck1", "cv0", "cv1",
           "Bo0", "Bo1", "Bo2", "Bo3"]
        + up("f1")
        + ["Cq0", "Cq1", "Ck0", "Ck1", "Cv0", "Cv1", "Cu0", "Cu1", "Co0", "Co1", "Co2", "Co3"]
        + up("f2")
    )


SMALL = [
    ("gmix0", 8), ("gmix1", 8), ("gffn0", 8), ("gffn1", 8), ("gmem0", 8), ("gmem1", 8),
    ("gkv", 8), ("gfin", 8), ("n1", 8), ("n2", 8), ("ghead", 1), ("pscale", 4), ("qn", 1),
    ("kn", 1), ("bfg", 8), ("pek", 16), ("pev", 16), ("cw0", 66), ("cw1", 66), ("cb0", 22),
    ("cb1", 22), ("walr", 128), ("wgl", 192), ("wfg", 64), ("balpha", 256), ("walpha", 256),
    ("wck2", 128), ("wcv2", 128), ("wpool", 512),
]
CONST = [
    ("ident", 128), ("tri", 128), ("ones", 128), ("trim", TM), ("mask2", TM), ("halves", 2),
    ("valid", 2), ("one", 1), ("mhalf", 32),
]
NSAC = [("dist", 256), ("cdist", 32)]


def columns(table):
    at, out = 0, {}
    for name, n in table:
        out[name] = (at, n)
        at += n
    return out, at


SM, NSM = columns(SMALL)
CN, NCN = columns(CONST)
_, NNS = columns(NSAC)


class Queue:

    def __init__(self, eng, sem):
        self.eng, self.sem, self.n, self.past, self.last = eng, sem, 0, {}, None

    def wait(self, *toks):
        for t in toks:
            if t is None:
                continue
            if isinstance(t, list):
                self.wait(*t)
                continue
            sem, v = t
            if self.past.get(id(sem), 0) < v:
                self.past[id(sem)] = v
                self.eng.wait_ge(sem, v)

    def do(self, f, *toks):
        self.wait(*toks)
        self.n += 1
        self.last = f(self.eng).then_inc(self.sem, 1)
        return (self.sem, self.n)

    def quiet(self, f, *toks):
        self.wait(*toks)
        self.last = f(self.eng)

    def mark(self):
        self.last.then_inc(self.sem, 1)
        self.n += 1
        return (self.sem, self.n)


def build(nc, w_d, x_d, mem_d, meta_d, small_d, const_d, gmask_d, nsac_d, sel_d, out_d):
    ctx = ExitStack()
    with ctx:
        def sb(name, cols, dt=F32):
            return ctx.enter_context(nc.sbuf_tensor(name, [128, cols], dt))

        def sem(name):
            return ctx.enter_context(nc.semaphore(name))

        PE = Queue(nc.tensor, sem("s_pe"))
        ACTE = Queue(nc.scalar, sem("s_act"))
        DVE = Queue(nc.vector, sem("s_dve"))
        SP = Queue(nc.sync, sem("s_sp"))
        POOL = Queue(nc.gpsimd, sem("s_pool"))

        NR, NH, AHEAD = 3, 3, 2
        raw = sb("raw", NR * UW)
        wh = sb("wh", NH * UW, F32R)
        wl = sb("wl", NH * UW, F32R)
        xt_ = sb("xt", 8 * T)
        xh_ = sb("xh", 8 * TM, F32R)
        xl_ = sb("xl", 8 * TM, F32R)
        coh_ = sb("coh", 8 * T, F32R)
        col_ = sb("col", 8 * T, F32R)
        memkv = sb("memkv", 4 * 1024)
        small = sb("small", NSM)
        smh = sb("smh", 384, F32R)
        sml = sb("sml", 384, F32R)
        cst = sb("cst", NCN)
        ARW = 13700
        arena = sb("arena", ARW)
        fh_ = sb("fh", 4 * T, F32R)
        fl_ = sb("fl", 4 * T, F32R)
        rs_ = sb("rs", TM)
        rst_ = sb("rst", 16)
        meta_ = sb("meta", 8 * NM)[:, :]
        gw_ = sb("gw", 16)[:, :]
        banks = [ctx.enter_context(nc.psum_tensor(f"ps{i}", [128, 512], F32)) for i in range(8)]

        v3 = lambda ap, n: ap.rearrange("p (a b) -> p a b", b=n)
        xt = v3(xt_[:, :], T)
        xh, xl = v3(xh_[:, :], TM), v3(xl_[:, :], TM)
        coh, col = v3(coh_[:, :], T), v3(col_[:, :], T)
        f32 = lambda ap: ap.bitcast(F32)

        def sm(name, a=0, b=None):
            at, n = SM[name]
            return small[:, at + a:at + (n if b is None else b)]

        def cn(name, a=0, b=None):
            at, n = CN[name]
            return cst[:, at + a:at + (n if b is None else b)]

        at_ = [0]

        def area(n):
            at_[0] += n
            assert at_[0] <= ARW, at_[0]
            return arena[:, at_[0] - n:at_[0]]

        loaded = {}

        def load(dst, src, s, *toks):
            SP.wait(*toks)
            SP.quiet(lambda e: e.dma_start(dst, src).then_inc(s, 16))
            loaded[id(s)] = loaded.get(id(s), 0) + 16
            return (s, loaded[id(s)])

        memsc = area(2560)
        memT_ = memsc[:, 0:8 * T]
        memT = v3(memT_, T)
        NG = SM["ghead"][0]
        t_gain = load(small[:, 0:NG], small_d[:, 0:NG], sem("d_gain"))
        t_x0 = load(xt_[:, 0:512], x_d[:, 0:512], sem("d_x0"))
        first_half = raw[:, 0:UW // 2]
        t_w0 = load(first_half, w_d[0][:, 0:UW // 2], sem("d_w0a"))
        t_x1 = load(xt_[:, 512:1024], x_d[:, 512:1024], sem("d_x1"))
        t_x2 = load(xt_[:, 1024:2048], x_d[:, 1024:2048], sem("d_x2"))
        t_x = [t_x0] * 2 + [t_x1] * 2 + [t_x2] * 4

        names = unit_names()
        ring_sem = [sem(f"d_w{i}") for i in range(NR)]

        class Stream:

            dma_n = split_n = got = hslots = 0
            ahead = AHEAD
            raw_free = {}
            part_free = {}
            landed = {}
            parts = {}

            def fetch(self, upto=None):
                i = self.dma_n
                if i == upto or i >= len(names) or (i >= NR and (i - NR) not in self.raw_free):
                    return
                s = ring_sem[i % NR]
                SP.wait(self.raw_free.get(i - NR))
                dst = raw[:, (i % NR) * UW:(i % NR + 1) * UW]
                if i == 0:
                    h = UW // 2
                    SP.quiet(lambda e: e.dma_start(dst[:, h:UW], w_d[0][:, h:UW]).then_inc(s, 16))
                else:
                    SP.quiet(lambda e: e.dma_start(dst, w_d[i]).then_inc(s, 16))
                self.landed[i] = (s, 16 * (i // NR + 1))
                self.dma_n += 1
                self.fetch(upto)

            def split(self):
                i = self.split_n
                self.split_n += 1
                src = raw[:, (i % NR) * UW:(i % NR + 1) * UW]
                k = self.hslots
                self.hslots += 1
                free = self.part_free[k - NH] if k >= NH else None
                H = wh[:, (k % NH) * UW:(k % NH + 1) * UW]
                L = wl[:, (k % NH) * UW:(k % NH + 1) * UW]
                hw = UW // 2
                tl = []
                for a in (0, hw):
                    landed = t_w0 if i == 0 and a == 0 else self.landed[i]
                    th = ACTE.do(lambda e, a=a: e.copy(H[:, a:a + hw], src[:, a:a + hw]), landed, free)
                    tl.append(DVE.do(lambda e, a=a: e.tensor_tensor(
                        L[:, a:a + hw], src[:, a:a + hw], f32(H[:, a:a + hw]), ALU.subtract),
                        landed, free, th))
                self.raw_free[i] = tl[1]
                self.parts[i] = (H, L, tl, k)
                self.fetch()

            def get(self, name):
                i = self.got
                self.got += 1
                assert names[i] == name, (names[i], name)
                while self.split_n <= min(i + self.ahead, len(names) - 1):
                    if self.split_n > i and self.split_n >= self.dma_n:
                        break
                    self.split()
                return i, self.parts[i]

            def release(self, i, tok):
                self.part_free[self.parts[i][3]] = tok

        W = Stream()
        W.fetch(1)
        t_small = load(small[:, NG:NSM], small_d[:, NG:NSM], sem("d_small"))
        t_cst = load(cst[:, :], const_d, sem("d_cst"))
        W.fetch(2)
        t_mem = load(memT_, mem_d, sem("d_mem"))
        d_tab = sem("d_tab")
        t_meta = load(meta_, meta_d, d_tab)
        W.fetch()

        free = [None] * 8
        turn = {"A": [0, 1, 2, 3], "B": [4, 5, 6, 7]}

        def bank(ring):
            b = next(n for n in turn[ring] if free[n] != "held")
            turn[ring].remove(b)
            turn[ring].append(b)
            PE.wait(free[b])
            free[b] = "held"
            return b, banks[b]

        def mm(out, lhsT, rhs, start, stop, *toks, skip=False):
            PE.quiet(lambda e: e.matmul(out, lhsT, rhs, start=start, stop=stop, skip_group_check=skip), *toks)

        def mark():
            return PE.mark()

        def mm3(out, wH, wL, XH, XL, start, stop, *toks, skip=False):
            mm(out, wH, XH, start, False, *toks, skip=skip)
            mm(out, wH, XL, False, False, skip=skip)
            mm(out, wL, XH, False, stop, skip=skip)

        def V(f, *t):
            return DVE.do(f, *t)

        def A(f, *t):
            return ACTE.do(f, *t)

        def split_x(src, g, H, L, *toks, war=None):
            th = A(lambda e: e.activation(H, src, ACT.Copy, scale=g), war, *toks)
            return V(lambda e: e.scalar_tensor_tensor(L, src, g, f32(H), ALU.mult, ALU.subtract), th, war, *toks)

        def split_p(H, L, P, *toks):
            th = A(lambda e: e.copy(H, P), *toks)
            return V(lambda e: e.tensor_tensor(L, P, f32(H), ALU.subtract), th)

        def power(dst, src, n, *toks):
            m = src.shape[0]
            return POOL.do(lambda e: e.tensor_tensor(dst, src, cn("mhalf")[0:m, 0:n], ALU.pow), t_cst, *toks)

        def transpose(out, src, *toks):
            m = src.shape[0]
            PE.quiet(lambda e: e.transpose(out, src, cn("ident")[0:m, 0:m]), t_cst, *toks)

        def spread(dst, col, tiles, tok, war=None):
            b, P = bank("B")
            for n, a, m in tiles:
                transpose(P[:, a:a + m], col[0:m, n:n + 1].broadcast_to([m, 128]), tok)
            w = max(a + m for _, a, m in tiles)
            t = V(lambda e: e.tensor_copy(dst, P[:, 0:w]), mark(), war)
            free[b] = t
            return t

        sqb = area(4 * TM)
        sq2 = [sqb[:, n * TM:(n + 1) * TM] for n in range(4)]
        sq_free = [None] * 4
        sq_n = [0]
        TT = [(0, 0, 128), (1, 128, 128)]

        def square(src, tok, scale=1.0):
            while sq_free[sq_n[0] % 4] == "held":
                sq_n[0] += 1
            k = sq_n[0] % 4
            sq_n[0] += 1
            s = sq2[k][:, 0:src.shape[-1]]
            return k, s, A(lambda e: e.activation(s, src, ACT.Square, scale=scale), tok, sq_free[k])

        def token_sums(srcs, toks):
            sums = [None, None]
            for c in range(8):
                k, s, t = square(srcs[c], toks[c])
                if c < 2:
                    sums[c] = k, s, t
                    sq_free[k] = "held"
                else:
                    ka, acc, ta = sums[c % 2]
                    sq_free[k] = V(lambda e: e.tensor_tensor(acc, acc, s, ALU.add), t, ta)
                    sums[c % 2] = ka, acc, sq_free[k]
            return sums

        def token_rstd(sums, cold, war=None):
            b, P = bank("B")
            for c, (k, s, t) in enumerate(sums):
                for n in range(2):
                    mm(P[:, n:n + 1], s[:, n * 128:(n + 1) * 128], cn("one"), c == 0 and n == 0, c == 1, t, t_cst, skip=True)
                sq_free[k] = mark()
            t = V(lambda e: e.tensor_scalar(rst_[:, 8:10], P[:, 0:2], 1.0 / D, EPS, ALU.mult, ALU.add), sq_free[k], war)
            free[b] = t
            t_c = power(cold, rst_[:, 8:10], 2, t, war)
            return t_c

        KORD = list(range(8))

        def projF(name, XH, XL, xtoks, out_w, order=KORD):
            i, (H, L, tl, k) = W.get(name)
            H3, L3 = v3(H, 256), v3(L, 256)
            res = []
            if out_w <= 256:
                b, P = bank("A")
                for n, c in enumerate(order):
                    for j in range(2):
                        mm3(P[:, j * 256:j * 256 + out_w], H3[:, c, j * 128:(j + 1) * 128],
                            L3[:, c, j * 128:(j + 1) * 128], XH(c), XL(c), n == 0 and j == 0, n == 7,
                            xtoks[c], tl[c // 4], skip=True)
                res.append((b, P, mark()))
            else:
                for j in range(2):
                    b, P = bank("A")
                    for n, c in enumerate(order):
                        mm3(P[:, 0:out_w], H3[:, c, j * 128:(j + 1) * 128], L3[:, c, j * 128:(j + 1) * 128],
                            XH(c), XL(c), n == 0, n == 7, xtoks[c], tl[c // 4])
                    res.append((b, P, mark()))
            W.release(i, res[-1][2])
            return res

        def projT(name, XH, XL, xtoks, tiles):
            i, (H, L, tl, k) = W.get(name)
            H3, L3 = v3(H, 256), v3(L, 256)
            res = []
            for n, a in enumerate(tiles):
                if n % 2 == 0:
                    b, P = bank("A")
                O = P[:, (n % 2) * 256:(n % 2) * 256 + 256]
                for c in range(8):
                    mm(O, XH(c)[:, a:a + 128], H3[:, c, :], c == 0, False, xtoks[c], tl[c // 4])
                    mm(O, XL(c)[:, a:a + 128], H3[:, c, :], False, False)
                    mm(O, XH(c)[:, a:a + 128], L3[:, c, :], False, c == 7)
                if n % 2 == 1 or n == len(tiles) - 1:
                    res.append((b, P, mark()))
            W.release(i, res[-1][2])
            return res

        def bc2(ap, n=2):
            return ap.unsqueeze(1).broadcast_to([128, n, ap.shape[-1]])

        X = lambda c: xh[:, c, NM:TM]
        XLo = lambda c: xl[:, c, NM:TM]
        CH = lambda c: coh[:, c, :]
        CL = lambda c: col[:, c, :]

        def enter(srcs, toks, g, war, H=X, L=XLo):
            return [split_x(s, sm(g, c, c + 1), H(c), L(c), toks[c], t_gain, war=war) for c, s in enumerate(srcs)]

        def softplus_neg(dst, z, tok, tmpa, tmpb):
            t1 = V(lambda e: e.scalar_tensor_tensor(tmpa, z, -1.0, z, ALU.mult, ALU.max), tok)
            t2 = A(lambda e: e.activation(tmpb, tmpa, ACT.Exp, scale=-1.0), t1)
            t3 = A(lambda e: e.activation(tmpa, tmpb, ACT.Ln, bias=cn("one")), t2, t_cst)
            return V(lambda e: e.scalar_tensor_tensor(dst, z, 0.0, tmpa, ALU.min, ALU.subtract), t3)

        def weave(*gens):
            live = list(gens)
            while live:
                for g in list(live):
                    try:
                        next(g)
                    except StopIteration:
                        live.remove(g)

        def pipeline(gens, depth):
            todo, live = list(gens), []
            while todo or live:
                if todo and len(live) < depth:
                    live.append([todo.pop(0), 0])
                old = [g for g in live if g[1] == depth - 1]
                for g in old + live[::-1]:
                    if next(g[0], "end") == "end":
                        live.remove(g)
                for g in live:
                    g[1] += 1
                yield

        def after(n, gen):
            for _ in range(n):
                yield
            yield from gen

        co_tok = [None] * 8
        tk = {}
        mem_tok = {0: [], 1: []}
        mk = lambda l: v3(memkv[:, l * 2048:l * 2048 + 1024], T)
        mv = lambda l: v3(memkv[:, l * 2048 + 1024:l * 2048 + 2048], 512)

        def mem_head(l, h, mq, mq_tok, buf, sc, last, war, done):
            key, pkey = h % 3, 3 + h % 2
            Eh, PT = buf[:, key * 512:key * 512 + 512], buf[:, pkey * 512:pkey * 512 + 512]
            mx, su = sc[:, key * 4:key * 4 + 2], sc[:, key * 4 + 2:key * 4 + 4]
            was = last.get(("E", key))
            b, P = bank("B")
            for i in range(2):
                mm(P[:, i * 256:(i + 1) * 256], mq[:, h, i * 128:(i + 1) * 128], mk(l)[:, h, :], True, True,
                   mq_tok, mem_tok[l])
            t = mark()
            t1 = V(lambda e: e.tensor_reduce(mx, v3(P[:, :], 256), AX.X, ALU.max, negate=True), t, was, war)
            for i in range(2):
                t2 = A(lambda e: e.activation(Eh[:, i * 256:(i + 1) * 256], P[:, i * 256:(i + 1) * 256], ACT.Exp,
                                              bias=mx[:, i:i + 1], accum_out=su[:, i:i + 1]), t1, was, war)
            free[b] = t2
            yield
            t3 = V(lambda e: e.reciprocal(su, su), t2)
            t4 = V(lambda e: e.tensor_tensor(v3(Eh, 256), v3(Eh, 256), su.unsqueeze(2).broadcast_to([128, 2, 256]),
                                             ALU.mult), t3)
            yield
            b, P = bank("B")
            for mi in range(2):
                for i in range(2):
                    transpose(P[:, mi * 256 + i * 128:mi * 256 + (i + 1) * 128],
                              Eh[:, i * 256 + mi * 128:i * 256 + (mi + 1) * 128], t4)
            last["E", key] = mark()
            t6 = A(lambda e: e.copy(PT, P[:, :]), last["E", key], last.get(pkey), war)
            free[b] = t6
            yield
            b, P = bank("B")
            for mi in range(2):
                mm(P[:, 0:T], mv(l)[:, mi, h * 128:(h + 1) * 128], PT[:, mi * 256:(mi + 1) * 256], mi == 0, mi == 1, t6)
            last[pkey] = mark()
            yield
            H, L = coh[:, 4 + h, :], col[:, 4 + h, :]
            th = A(lambda e: e.copy(H, P[:, 0:T]), last[pkey], tk[done])
            yield
            free[b] = co_tok[4 + h] = V(lambda e: e.tensor_tensor(L, P[:, 0:T], f32(H), ALU.subtract), th)

        xs = [xt[:, c, :] for c in range(8)]
        ms = [memT[:, c, :] for c in range(8)]
        xtok = enter(xs[0:2], t_x[0:2], "gmix0", None)
        W.split()
        for c in range(2, 8):
            xtok.append(split_x(xs[c], sm("gmix0", c, c + 1), X(c), XLo(c), t_x[c], t_gain))
        at0 = SM["walr"][0]
        r_ = area(1024)
        alrT = r_[:, 0:256]
        qkb = area(1024)
        q_, k_ = qkb[:, 0:512], qkb[:, 512:1024]
        W.ahead = 0
        (bq0, Pq0, tq0), = projF("Aq", X, XLo, xtok, T)
        W.ahead = AHEAD
        t = A(lambda e: e.copy(smh[:, :], small[:, at0:at0 + 384]), t_small)
        t_sml = V(lambda e: e.tensor_tensor(sml[:, :], small[:, at0:at0 + 384], f32(smh[:, :]), ALU.subtract), t)
        W.split()
        b0, P0 = bank("A")
        for c in range(8):
            a = c * 16
            mm3(P0[:, 0:T], smh[:, a:a + 128], sml[:, a:a + 128], X(c), XLo(c), c == 0, c == 7, xtok[c], t_sml)
        t_alr0 = mark()
        sums = token_sums(xs, t_x)
        W.ahead = 1
        (b, P, t), = projF("Ak", X, XLo, xtok, T)
        W.ahead = AHEAD
        t_rst = token_rstd(sums, rst_[:, 0:2])
        Am0 = projF("Am0", X, XLo, xtok, T)
        t_rs = spread(rs_[:, 0:T], rst_, TT, t_rst)
        t_alr = V(lambda e: e.tensor_tensor(alrT[0:16, :], P0[0:16, 0:T], rs_[0:16, 0:T], ALU.mult), t_alr0, t_rs)
        free[b0] = t_alr
        t_q = V(lambda e: e.scalar_tensor_tensor(v3(q_, T), v3(Pq0[:, :], T), 0.125, bc2(rs_[:, 0:T]), ALU.mult, ALU.mult),
                tq0, t_rs)
        free[bq0] = t_q
        mtok = enter(ms, [t_mem] * 8, "gmem0", None, CH, CL)
        t_k = V(lambda e: e.tensor_tensor(v3(k_, T), v3(P[:, :], T), bc2(rs_[:, 0:T]), ALU.mult), t, t_rs)
        free[b] = t_k
        qk_tok = [t_q, t_k]

        mrs = area(T)
        mrst = area(2)
        gm = area(1024)
        t_gm = load(gm, gmask_d, d_tab)
        v_ = area(1024)
        v4 = v3(v_, 512)
        AT_ = area(1024)
        ATo = area(512)
        t_at0 = POOL.do(lambda e: e.memset(AT_, 0.0))
        b_ = area(512)
        lv = area(5 * 512)
        E_ = lv[:, 0:512]
        QK = [(lv[:, 512:1024], lv[:, 1024:1536]), (lv[:, 1536:2048], lv[:, 2048:2560])]
        mq_ = area(1024)
        mq = v3(mq_, T)
        scb = area(16)
        rr_ = ATo[:, 0:128]

        def mem_unit(l, kind, j, mtok):
            if kind == "k":
                (b, P, t), = projF(f"m{l}k{j}", CH, CL, mtok, T)
                if (l, j) == (0, 0):
                    tk["msums"], tk["k0"] = token_sums(ms, [t_mem] * 8), (b, P, t)
                    return t
                if l == 0:
                    tk["mrst"], tk["k1"] = token_rstd(tk["msums"], mrst), (b, P, t)
                    return t
                t2 = V(lambda e: e.tensor_tensor(mk(l)[:, 2 * j:2 * j + 2, :], v3(P[:, :], T), bc2(mrs), ALU.mult), t, tk["mrs"])
            else:
                (b, P, t), = projT(f"m{l}v{j}", CH, CL, mtok, [0, 128])
                if (l, j) == (0, 0):
                    tk["mrs"] = spread(mrs, mrst, TT, tk["mrst"])
                    for n in range(2):
                        bk, Pk, t_k = tk[f"k{n}"]
                        free[bk] = V(lambda e: e.tensor_tensor(mk(l)[:, 2 * n:2 * n + 2, :], v3(Pk[:, :], T), bc2(mrs),
                                                               ALU.mult), t_k, tk["mrs"])
                        mem_tok[l].append(free[bk])
                for i in range(2):
                    t2 = V(lambda e: e.tensor_scalar(mv(l)[:, i, j * 256:(j + 1) * 256], P[:, i * 256:(i + 1) * 256],
                                                     mrst[:, i:i + 1], None, ALU.mult), t, tk["mrst"])
            free[b] = t2
            mem_tok[l].append(t2)
            return t

        def values():
            tk["v"] = []
            for j in range(2):
                (b, P, t), = projT(f"Av{j}", X, XLo, xtok, [0, 128])
                for i in range(2):
                    t2 = V(lambda e: e.tensor_scalar(v4[:, i, j * 256:(j + 1) * 256], P[:, i * 256:(i + 1) * 256],
                                                     rst_[:, i:i + 1], None, ALU.mult), t, t_rst)
                free[b] = t2
                tk["v"].append(t2)
                if j == 0:
                    for c in range(4, 8):
                        tk["m1"].append(split_x(ms[c], sm("gmem1", c, c + 1), CH(c), CL(c), t_mem, war=tk["m0"]))
                yield

        def units():
            yield from mem_queries()
            for kind in "kv":
                for j in range(2):
                    tk["m0"] = mem_unit(0, kind, j, mtok)
                    yield
            tk["m1"] = enter(ms[0:4], [t_mem] * 4, "gmem1", tk["m0"], CH, CL)
            yield from values()
            for kind in "kv":
                for j in range(2):
                    tk["m1pe"] = mem_unit(1, kind, j, tk["m1"])
                    yield
            tk["r"] = []
            for j in range(2):
                (b, P, t), = projF(f"Ar{j}", X, XLo, xtok, T)
                t = V(lambda e: e.tensor_tensor(v3(r_[:, j * 512:(j + 1) * 512], T), v3(P[:, :], T),
                                                bc2(rs_[:, 0:T]), ALU.mult), t, t_rs, tk["z"])
                free[b] = t
                tk["r"].append(t)
                yield
        def mem_queries():
            tk["mq"] = []
            for j in range(2):
                (b, P, t), = projF(f"Am{j}", X, XLo, xtok, T) if j else Am0
                t = V(lambda e: e.scalar_tensor_tensor(mq[:, 2 * j:2 * j + 2, :], v3(P[:, :], T), 128.0 ** -0.5,
                                                       bc2(rs_[:, 0:T]), ALU.mult, ALU.mult), t, t_rs)
                free[b] = t
                tk["mq"].append(t)
                if j:
                    yield

        KOUT = [4, 5, 6, 7, 0, 1, 2, 3]

        def out_first(names2, first, n):
            W.ahead = 1
            for nm in names2:
                first.append((bank("A"), W.get(nm)))
                out_half(first[-1], KOUT[0:n])
                yield
            W.ahead = AHEAD

        def out_half(unit, chunks):
            (b, P), (i, (H, L, tl, _)) = unit
            assert all(co_tok[c] for c in chunks)
            H3, L3 = v3(H, 256), v3(L, 256)
            for c in chunks:
                for j in range(2):
                    mm3(P[:, j * 256:j * 256 + 256], H3[:, c, j * 128:(j + 1) * 128], L3[:, c, j * 128:(j + 1) * 128],
                        CH(c), CL(c), c == 4 and j == 0, c == 3, co_tok[c], tl[c // 4], skip=True)

        def decay():
            la, (ea, eb) = E_, QK[1]
            b, P = bank("B")
            for i in range(2):
                mm(P[:, i * 256:(i + 1) * 256], alrT[0:16, i * 128:(i + 1) * 128], sm("walpha")[0:16, :], True, True, t_alr)
            tk["z"] = mark()
            t = V(lambda e: e.tensor_tensor(v3(la, 256), v3(P[:, :], 256), bc2(sm("balpha")), ALU.add), tk["z"], t_small)
            free[b] = t
            t_la = softplus_neg(la, la, t, ea, eb)
            yield
            b, P = bank("B")
            for dt in range(2):
                for i in range(2):
                    mm(P[:, (dt * 2 + i) * 128:(dt * 2 + i + 1) * 128],
                       la[:, i * 256 + dt * 128:i * 256 + dt * 128 + 128], cn("tri"), True, True, t_la, t_cst)
            t = mark()
            tk["b"] = V(lambda e: e.tensor_scalar(b_, P[:, :], 1.0 / 16, None, ALU.mult), t)
            free[b] = tk["b"]
            yield
            used = [None, None]

            def prep(li):
                m = LEVELS[li]
                if not m:
                    return q_, k_, qk_tok
                Q, K = QK[li % 2]
                bv = b_.rearrange("p (a c) -> p a c", c=2 * m)
                ev = E_.rearrange("p (a c) -> p a c", c=2 * m)
                t = V(lambda e: e.tensor_tensor(ev, bv, bv[:, :, m - 1:m].broadcast_to([128, 512 // (2 * m), 2 * m]),
                                                ALU.subtract), tk["b"], tk.get("E"))
                t = A(lambda e: e.activation(E_, E_, ACT.Abs), t)
                t = A(lambda e: e.activation(E_, E_, ACT.Exp, scale=-1.0), t)
                ta = V(lambda e: e.tensor_tensor(Q, q_, E_, ALU.mult), t, qk_tok[0], used[li % 2])
                tb = V(lambda e: e.tensor_tensor(K, k_, E_, ALU.mult), t, qk_tok[1], used[li % 2])
                tk["E"] = [ta, tb]
                return Q, K, [ta, tb]

            ready = prep(0)
            at_tok = [t_at0, t_at0]
            yield
            for li in range(8):
                nxt = prep(li + 1) if li < 7 else None
                QQ, KK, tt = ready
                for half in range(2):
                    b, P = bank("B")
                    r = half * 64
                    for hh in range(2):
                        for i in range(2):
                            s = (hh * 2 + i) * 128
                            mm(P[:, s:s + 128], KK[r:r + 64, s:s + 128], QQ[r:r + 64, s:s + 128], True, True, tt)
                    t = mark()
                    mask = gm[:, li * 128:(li + 1) * 128].bitcast(U32)
                    t2 = V(lambda e: e.copy_predicated(v3(AT_[:, half * 512:(half + 1) * 512], 128), bc2(mask, 4),
                                                       v3(P[:, :], 128)), t, t_gm, at_tok[half])
                    free[b] = at_tok[half] = t2
                used[li % 2] = t
                ready = nxt
                yield
            Q, K = QK[1]
            tq = []
            for dt in range(2):
                s0, s1 = (dt * 2) * 128, (dt * 2 + 1) * 128
                t = A(lambda e: e.activation(E_[:, s0:s0 + 128], b_[:, s0:s0 + 128], ACT.Exp, scale=-1.0,
                                             bias=b_[:, s0 + 127:s0 + 128]), tk["b"], tk["E"])
                t3 = V(lambda e: e.tensor_tensor(K[:, s0:s0 + 128], k_[:, s0:s0 + 128], E_[:, s0:s0 + 128], ALU.mult),
                       t, used)
                t = A(lambda e: e.activation(E_[:, s1:s1 + 128], b_[:, s1:s1 + 128], ACT.Exp), tk["b"], tk["E"])
                t4 = V(lambda e: e.tensor_tensor(Q[:, s1:s1 + 128], q_[:, s1:s1 + 128], E_[:, s1:s1 + 128], ALU.mult),
                       t, used)
                tq += [t3, t4]
            t_lev = at_tok
            yield
            for r in (0, 64):
                b, P = bank("B")
                for dt in range(2):
                    mm(P[:, dt * 128:(dt + 1) * 128], K[r:r + 64, dt * 256:dt * 256 + 128],
                       Q[r:r + 64, dt * 256 + 128:dt * 256 + 256], True, True, tq)
                t = mark()
                t_ao = V(lambda e: e.tensor_copy(ATo[:, r * 4:r * 4 + 256], P[:, 0:256]), t)
                free[b] = t_ao
            yield
            AT4 = v3(AT_, 128)
            rr = area(16)
            ts = []
            for half in range(2):
                b, P = bank("B")
                for hh in range(2):
                    h = half * 2 + hh
                    vc = lambda i: v4[:, i, h * 128:(h + 1) * 128]
                    ha = (h % 2) * 4 + h // 2 * 2
                    ho = (h % 2) * 256 + h // 2 * 128
                    mm(P[:, hh * 256:hh * 256 + 128], vc(0), AT4[:, ha, :], True, True, t_lev, t_ao, tk["v"])
                    mm(P[:, hh * 256 + 128:hh * 256 + 256], vc(0), ATo[:, ho:ho + 128], True, False)
                    mm(P[:, hh * 256 + 128:hh * 256 + 256], vc(1), AT4[:, ha + 1, :], False, True)
                t_o = mark()
                o = qkb[:, half * 512:(half + 1) * 512]
                t_c = V(lambda e: e.tensor_copy(o, P[:, :]), t_o)
                free[b] = t_c
                sq = b_ if half == 0 else E_
                ts.append(A(lambda e: e.activation(sq, o, ACT.Square), t_c, tq))
            yield
            b, P = bank("B")
            for n in range(8):
                sq = b_ if n < 4 else E_
                mm(P[:, n:n + 1], sq[:, (n % 4) * 128:(n % 4 + 1) * 128], cn("one"), n == 0, n == 7, ts[n // 4], skip=True)
            t = V(lambda e: e.tensor_scalar(rr[:, 0:8], P[:, 0:8], 1.0 / 128, EPS, ALU.mult, ALU.add), mark())
            free[b] = t
            t = power(rr[:, 8:16], rr[:, 0:8], 8, t)
            yield
            while len(tk["r"]) < 2:
                yield
            t_sr = A(lambda e: e.activation(r_, r_, ACT.Silu), tk["r"])
            for half in range(2):
                o = qkb[:, half * 512:(half + 1) * 512]
                b, P = bank("B")
                for n in range(4):
                    transpose(P[:, n * 128:(n + 1) * 128], rr[:, 8 + half * 4 + n:9 + half * 4 + n].broadcast_to([128, 128]), t)
                t2 = V(lambda e: e.scalar_tensor_tensor(o, o, sm("ghead"), P[:, :], ALU.mult, ALU.mult), mark(), ts)
                free[b] = t2
                t2 = V(lambda e: e.tensor_tensor(o, o, r_[:, half * 512:half * 512 + 512], ALU.mult), t2, t_sr)
                dst = slice(half * 512, half * 512 + 512)
                th = A(lambda e: e.copy(coh_[:, dst], o), t2, tk["m1pe"])
                t2 = V(lambda e: e.tensor_tensor(col_[:, dst], o, f32(coh_[:, dst]), ALU.subtract), th)
                co_tok[2 * half] = co_tok[2 * half + 1] = t2

        memlast = {}

        def mem_heads0():
            war = tk["m1"]
            yield from pipeline([mem_head(0, h, mq, tk["mq"], memsc, scb, memlast, war, "m1pe") for h in range(4)], 5)

        meta = v3(meta_, NM)
        gw = gw_.rearrange("p (c two) -> p c two", two=2)
        t = V(lambda e: e.memset(gw_, 1.0))
        t_gw = V(lambda e: e.tensor_tensor(gw[:, :, 1], sm("gfin"), sm("gfin"), ALU.mult), t, t_gain)
        metok = []

        def meta_parts():
            metok.extend([split_x(meta[:, c, :], sm("n1", c, c + 1), xh[:, c, 0:NM], xl[:, c, 0:NM], t_meta, t_gain) for c in range(8)])
            yield
            mq2 = rr_[:, 0:8 * NM]
            t = A(lambda e: e.activation(mq2, meta_, ACT.Square), t_meta)
            b, P = bank("B")
            for c in range(8):
                mm(P[0:NM, 0:1], mq2[:, c * NM:(c + 1) * NM], cn("one"), c == 0, c == 7, t, t_cst)
            t = V(lambda e: e.tensor_scalar(rst_[0:NM, 10:11], P[0:NM, 0:1], 1.0 / D, EPS, ALU.mult, ALU.add), mark())
            free[b] = t
            tk["mr"] = power(rst_[0:NM, 2:3], rst_[0:NM, 10:11], 1, t)

        A_first = []
        weave(decay(), units(), after(7, mem_heads0()), after(9, meta_parts()), after(14, out_first(["Ao0", "Ao1"], A_first, 4)))

        def out_proj(names4, g, first, n):
            toks, xk, done = [], [], []
            for unit in first:
                out_half(unit, KOUT[n:8])
                done.append(mark())
                W.release(unit[1][0], done[-1])
            ready, co_tok[:] = list(co_tok), [None] * 8
            for j, nm in enumerate(names4):
                if j < 2:
                    (b, P), t = first[j][0], done[j]
                else:
                    (b, P, t), = projF(nm, CH, CL, ready, T, KOUT)
                for c in (2 * j, 2 * j + 1):
                    t2 = V(lambda e: e.tensor_tensor(xs[c], P[:, (c % 2) * T:(c % 2 + 1) * T], xs[c], ALU.add), t)
                    toks.append(t2)
                free[b] = t2
                for c in (2 * j, 2 * j + 1):
                    xk.append(split_x(xs[c], sm(g, c, c + 1), X(c), XLo(c), toks[c]))
            return toks, xk

        base = ARW - 1024 - 2 * (T + 2)
        YB, AB = arena[:, base:base + 1024], arena[:, base + 1024:ARW]

        def ffn(tag, xk, toks, cw, cb, then):
            yb = [YB[:, 0:512], YB[:, 512:1024]]
            abuf = [AB[:, 0:T + 2], AB[:, T + 2:2 * (T + 2)]]
            t_pad = None
            if cw is not None:
                for n in range(2):
                    t_pad = V(lambda e: e.memset(abuf[n][:, 0:2], 0.0))
            acc = [banks[4 + o // 2][:, (o % 2) * 256:(o % 2) * 256 + 256] for o in range(8)]
            f_pe = [None] * 4
            ftok = {}
            y_free = [None, None]
            rs = rs_[:, 0:T]

            def mix(f, b, P, t, t_rs):
                s = f % 2
                y, g2 = yb[s][:, 0:T], yb[s][:, T:2 * T]
                if cw is not None:
                    Ab = abuf[s]
                    w = lambda n: sm(cw, n * 22 + f, n * 22 + f + 1)
                    t1 = V(lambda e: e.tensor_tensor(Ab[:, 2:2 + T], P[:, 0:T], rs, ALU.mult), t, t_rs, y_free[s], t_pad)
                    t2 = A(lambda e: e.activation(y, Ab[:, 0:T], ACT.Copy, scale=w(0)), t1, y_free[s])
                    t3 = V(lambda e: e.tensor_tensor(g2, P[:, T:2 * T], rs, ALU.mult), t, t_rs, y_free[s])
                    free[b] = t3
                    yield
                    t4 = V(lambda e: e.scalar_tensor_tensor(y, Ab[:, 1:1 + T], w(1), y, ALU.mult, ALU.add), t2)
                    t5 = V(lambda e: e.scalar_tensor_tensor(y, Ab[:, 2:2 + T], w(2), y, ALU.mult, ALU.add), t4)
                    t6 = A(lambda e: e.activation(y, y, ACT.Silu, bias=sm(cb, f, f + 1)), t5)
                else:
                    t1 = V(lambda e: e.tensor_tensor(y, P[:, 0:T], rs, ALU.mult), t, t_rs, y_free[s])
                    t3 = V(lambda e: e.tensor_tensor(g2, P[:, T:2 * T], rs, ALU.mult), t, t_rs, y_free[s])
                    free[b] = t3
                    t6 = A(lambda e: e.activation(y, y, ACT.Silu), t1)
                yield
                t7 = V(lambda e: e.tensor_tensor(g2, y, g2, ALU.mult), t6, t3)
                H, L = fh_[:, (f % 4) * T:(f % 4 + 1) * T], fl_[:, (f % 4) * T:(f % 4 + 1) * T]
                t8 = A(lambda e: e.copy(H, g2), t7, f_pe[f % 4])
                yield
                y_free[s] = ftok[f] = V(lambda e: e.tensor_tensor(L, g2, f32(H), ALU.subtract), t8, f_pe[f % 4])

            def down(p):
                i, (H, L, tl, _) = W.get(f"{tag}d{p}")
                H, L = v3(H, 1024), v3(L, 1024)
                if p == 0:
                    for b in range(4, 8):
                        assert free[b] != "held"
                        PE.wait(free[b])
                        free[b] = "held"
                if p == 10:
                    marks = []
                    for o in range(8):
                        cs = slice(o * 128, (o + 1) * 128)
                        for j in range(2):
                            f = 2 * p + j
                            FH, FL = fh_[:, (f % 4) * T:(f % 4 + 1) * T], fl_[:, (f % 4) * T:(f % 4 + 1) * T]
                            mm3(acc[o], H[:, j, cs], L[:, j, cs], FH, FL, False, j == 1, ftok[f], tl[j], skip=True)
                        marks.append(mark())
                    W.release(i, marks[-1])
                    return marks
                for j in range(2):
                    f = 2 * p + j
                    FH, FL = fh_[:, (f % 4) * T:(f % 4 + 1) * T], fl_[:, (f % 4) * T:(f % 4 + 1) * T]
                    for o in range(8):
                        cs = slice(o * 128, (o + 1) * 128)
                        mm3(acc[o], H[:, j, cs], L[:, j, cs], FH, FL, f == 0 and o % 2 == 0, False,
                            ftok[f], tl[j], skip=True)
                    f_pe[f % 4] = mark()
                W.release(i, f_pe[f % 4])

            first = projF(f"{tag}u0", X, XLo, xk, T)[0]
            sums = token_sums(xs, toks)
            second = projF(f"{tag}u1", X, XLo, xk, T)[0]
            t_rst = token_rstd(sums, rst_[:, 0:2])
            u = [projF(f"{tag}u2", X, XLo, xk, T)[0]]
            t_rs = spread(rs, rst_, TT, t_rst)
            weave(mix(0, *first, t_rs), mix(1, *second, t_rs))
            for p in range(1, 11):
                while len(u) < 2:
                    u.append(projF(f"{tag}u{2 * p + len(u)}", X, XLo, xk, T)[0])
                weave(mix(2 * p, *u[0], t_rs), mix(2 * p + 1, *u[1], t_rs))
                down(p - 1)
                t_x, u = u[1][2], []
            W.ahead = 1
            marks = down(10)
            W.ahead = AHEAD
            new = []
            for q in range(4):
                for o in (2 * q, 2 * q + 1):
                    t = V(lambda e: e.tensor_tensor(xs[o], acc[o], xs[o], ALU.add), marks[2 * q + 1])
                    new.append(t)
                free[4 + q] = t
                for o in (2 * q, 2 * q + 1):
                    then(o, new[o], t_x)
            return new, marks[-1]

        toks, xk = out_proj(["Ao0", "Ao1", "Ao2", "Ao3"], "gffn0", A_first, 4)
        ktk = []
        new, t_pe = ffn("f0", xk, toks, "cw0", "cb0",
                        lambda c, t, t_x: ktk.append(split_x(xs[c], sm("gkv", c, c + 1), CH(c), CL(c), t)))

        at_[0] = 0
        at_[0] = 2560 + 4 * TM
        nsac = area(NNS)
        t_nsac = load(nsac, nsac_d, d_tab, toks[-1])
        dist, cdist = nsac[:, 0:256], nsac[:, 256:288]
        EB = [area(800) for _ in range(3)]
        cblk = area(2496)
        PB = [cblk[:, 0:1024], cblk[:, 1024:2048]]
        X2, ev, kc = cblk[:, 0:512], cblk[:, 512:1024], cblk[:, 1984:2496]
        R = [cblk[:, 1024:1504], cblk[:, 1504:1984]]
        kk, vv = area(512), area(512)
        gT, kcm, vcm, gt, gh = area(120), area(16), area(128), area(48), memsc[:, 1536:2048]
        scb = area(60)
        mq_ = area(1024)
        mq = v3(mq_, T)
        bq_ = area(1024)
        bq = v3(bq_, T)

        kvb = projF("kvc", CH, CL, ktk, T)
        xk = enter(xs, new, "gmix1", t_pe)
        kvb += projF("kvk", CH, CL, ktk, T)
        sums = token_sums(xs, new)
        (bv, Pv, tv), = projT("kvv", CH, CL, ktk, [0, 128])
        t_rst = token_rstd(sums, rst_[:, 0:2])
        Bq0 = projF("Bq0", X, XLo, xk, T)
        t_rs = spread(rs_[:, 0:T], rst_, TT, t_rst)
        ktoks = []
        for dst, (b, P, t) in zip((kc, kk), kvb):
            t = V(lambda e: e.tensor_tensor(v3(dst, T), v3(P[:, :], T), bc2(rs_[:, 0:T]), ALU.mult), t, t_rs)
            free[b] = t
            ktoks.append(t)
        ev5 = ev.rearrange("p (v two m) -> p v two m", two=2, m=128)
        X25 = X2.rearrange("p (v g m) -> p v g m", g=2, m=128)
        t_ev = V(lambda e: e.tensor_copy(ev5, kc.rearrange("p (v m two) -> p v two m", two=2, m=128)), ktoks[0])
        d_x2 = sem("d_par")
        for g in range(2):
            for par in range(2):
                src = ev5[g * 64:(g + 1) * 64, :, par, :]
                dst = X25[par * 64:(par + 1) * 64, :, g, :]
                ACTE.quiet(lambda e: e.dma_start(dst, src).then_inc(d_x2, 16), t_ev)
        t_x2 = (d_x2, 64)
        t_kvpe = tk["kvpe"] = tv
        for i in range(2):
            t_vv = V(lambda e: e.tensor_scalar(vv[:, i * 256:(i + 1) * 256], Pv[:, i * 256:(i + 1) * 256],
                                               rst_[:, i:i + 1], None, ALU.mult), tv, t_rst)
        free[bv] = t_vv

        def queries(tag, dst3, scl, toks_out):
            for j in range(2):
                (b, P, t), = Bq0 if f"{tag}{j}" == "Bq0" else projF(f"{tag}{j}", X, XLo, xk, T)
                t = V(lambda e: e.scalar_tensor_tensor(dst3[:, 2 * j:2 * j + 2, :], v3(P[:, :], T), scl,
                                                       bc2(rs_[:, 0:T]), ALU.mult, ALU.mult), t, t_rs)
                free[b] = t
                toks_out.append(t)
                yield

        mq_tok, bq_tok = [], []

        def compress():
            r_t = []
            for kv, pe_n in enumerate(("pek", "pev")):
                for g in range(2):
                    Rv = R[kv].rearrange("p (c g n) -> p c g n", g=2, n=15)[:, :, g, :]
                    base = X25[:, kv, g, :].rearrange("p (n c) -> p c n", c=8)
                    pe = sm(pe_n).unsqueeze(2)
                    for hf in range(2):
                        t = V(lambda e: e.tensor_tensor(
                            Rv[:, hf * 8:(hf + 1) * 8, :], base[:, :, hf:hf + 15],
                            pe[:, hf * 8:(hf + 1) * 8, :].broadcast_to([128, 8, 15]), ALU.add), t_x2)
                rh, rl = (B[:, kv * 480:(kv + 1) * 480] for B in (fh_, fl_))
                t = A(lambda e: e.copy(rh, R[kv]), t, t_pe)
                r_t.append(V(lambda e: e.tensor_tensor(rl, R[kv], f32(rh), ALU.subtract), t, t_pe))
            yield
            t_g = []
            for kv in range(2):
                b, P = bank("B")
                nm = "ck" if kv == 0 else "cv"
                for half in range(2):
                    i, (H, L, tl, _) = W.get(f"{nm}{half}")
                    for c in range(8):
                        cc = half * 8 + c
                        rh, rl = (B[:, kv * 480 + cc * 30:kv * 480 + (cc + 1) * 30] for B in (fh_, fl_))
                        mm(P[0:30, 0:256], rh, v3(H, 256)[:, c, :], cc == 0, False, r_t[kv], tl[c // 4])
                        mm(P[0:30, 0:256], rl, v3(H, 256)[:, c, :], False, False)
                        mm(P[0:30, 0:256], rh, v3(L, 256)[:, c, :], False, cc == 15)
                    t = mark()
                    W.release(i, t)
                g_ = gh[0:30, kv * 256:(kv + 1) * 256]
                t_g.append(A(lambda e: e.activation(g_, P[0:30, 0:256], ACT.Gelu_apprx_tanh), t, tk["gz"]))
                free[b] = t_g[-1]
                yield
            b, P = bank("B")
            for n in range(4):
                transpose(P[:, n * 30:(n + 1) * 30], gh[0:30, n * 128:(n + 1) * 128], t_g)
            t_g = V(lambda e: e.tensor_copy(gT, P[:, 0:120]), mark())
            free[b] = t_g
            yield
            g4 = gT.rearrange("p (v c g n) -> p v c g n", v=2, c=2, g=2)
            b, P = bank("B")
            for g in range(2):
                for c in range(2):
                    mm(P[g * 64:(g + 1) * 64, 0:15], sm("wck2")[:, c * 64:(c + 1) * 64], g4[:, 0, c, g, :],
                       c == 0, c == 1, t_g)
            tk["kcm"] = V(lambda e: e.tensor_copy(kcm[:, 0:15], P[:, 0:15]), mark())
            free[b] = tk["kcm"]
            b, P = bank("B")
            for g in range(2):
                for c in range(2):
                    mm(P[0:15, g * 64:(g + 1) * 64], g4[:, 1, c, g, :], sm("wcv2")[:, c * 64:(c + 1) * 64], c == 0, c == 1)
            tk["vcm"] = V(lambda e: e.tensor_copy(vcm[0:15, :], P[0:15, 0:128]), mark())
            free[b] = tk["vcm"]

        def gates():
            b, P = bank("A")
            for c in range(8):
                a = 128 + c * 24
                mm3(P[0:24, 0:T], smh[:, a:a + 24], sml[:, a:a + 24], X(c), XLo(c), c == 0, c == 7, xk[c])
            gz = gh[0:24, 0:T]
            t = V(lambda e: e.tensor_copy(gz, P[0:24, 0:T]), mark())
            free[b] = t
            b, P = bank("B")
            for i in range(2):
                transpose(P[:, i * 24:i * 24 + 24], gz[:, i * 128:(i + 1) * 128], t)
            t = mark()
            for i in range(2):
                t2 = A(lambda e: e.activation(gt[:, i * 24:i * 24 + 24], P[:, i * 24:i * 24 + 24], ACT.Sigmoid,
                                              scale=rst_[:, i:i + 1]), t, t_rst)
            free[b] = t2
            g0 = gt[:, 0:24].rearrange("p (h n) -> p h n", n=3)[:, :, 0]
            tk["gz"] = t
            tk["gt"] = V(lambda e: e.tensor_scalar(g0, g0, cn("valid", 0, 1), None, ALU.mult), t2, t_cst)

        pair = {}
        last = {}

        def nsa_head(j, g, key, pkey):
            h = g * 4 + j
            r = g * 64
            EE, PT = EB[key], PB[pkey]
            st = scb[:, key * 16:key * 16 + 12]
            war = [tk.get(("E", key))]
            q = lambda i: bq[r:r + 64, j, i * 128:(i + 1) * 128]
            ks = lambda w: kk[r:r + 64, w * 256:(w + 1) * 256]
            b1, P1 = bank("A")
            for w in range(2):
                mm(P1[:, w * 256:(w + 1) * 256], q(1), ks(w), True, True, bq_tok, ktoks)
            t1 = mark()
            b0, P0 = bank("A")
            for w in range(2):
                mm(P0[:, w * 128:(w + 1) * 128], q(0), ks(w)[:, 0:128], True, True)
            for i in range(2):
                mm(P0[:, 256 + i * 16:256 + i * 16 + 15], q(i), kcm[r:r + 64, 0:15], True, True, tk["kcm"])
            t0 = mark()
            slope = 2.0 ** -(h + 1)
            t2 = V(lambda e: e.scalar_tensor_tensor(v3(EE[:, 0:512], 256), bc2(dist), slope, v3(P1[:, :], 256),
                                                    ALU.mult, ALU.add), t1, t_nsac, war)
            free[b1] = t2
            t5 = V(lambda e: e.tensor_reduce(st[:, 0:2], v3(EE[:, 0:512], 256), AX.X, ALU.max, negate=True), t2)
            for n in range(2):
                t8 = A(lambda e: e.activation(EE[:, n * 256:(n + 1) * 256], EE[:, n * 256:(n + 1) * 256], ACT.Exp,
                                              bias=st[:, n:n + 1], accum_out=st[:, 6 + n:7 + n]), t5, war)
            t3 = V(lambda e: e.scalar_tensor_tensor(v3(EE[:, 512:768], 128), bc2(dist[:, 128:256]), slope,
                                                    v3(P0[:, 0:256], 128), ALU.mult, ALU.add), t0, war)
            t4 = V(lambda e: e.scalar_tensor_tensor(v3(EE[:, 768:798], 15), v3(cdist, 16)[:, :, 0:15], slope,
                                                    v3(P0[:, 256:288], 16)[:, :, 0:15], ALU.mult, ALU.add), t0)
            free[b0] = t4
            t6 = V(lambda e: e.tensor_reduce(st[:, 2:4], v3(EE[:, 512:768], 128), AX.X, ALU.max, negate=True), t3)
            t7 = V(lambda e: e.tensor_reduce(st[:, 4:6], v3(EE[:, 768:798], 15), AX.X, ALU.max, negate=True), t4)
            for n, (a, z) in enumerate([(512, 640), (640, 768), (768, 783), (783, 798)]):
                t8 = A(lambda e: e.activation(EE[:, a:z], EE[:, a:z], ACT.Exp, bias=st[:, 2 + n:3 + n],
                                              accum_out=st[:, 8 + n:9 + n]), t7)
            yield
            t9 = V(lambda e: e.reciprocal(st[:, 6:12], st[:, 6:12]), t8)
            ga = gt[:, 24 + 3 * h + 1:24 + 3 * h + 3]
            gb = gt[:, 3 * h + 1:3 * h + 3]
            gc = gt.rearrange("p (i x) -> p i x", i=2)[:, :, 3 * h]
            t10 = V(lambda e: e.tensor_tensor(st[:, 6:8], st[:, 6:8], ga, ALU.mult), t9, tk["gt"])
            t11 = V(lambda e: e.tensor_tensor(st[:, 8:10], st[:, 8:10], gb, ALU.mult), t9)
            t12 = V(lambda e: e.tensor_tensor(st[:, 10:12], st[:, 10:12], gc, ALU.mult), t9)
            t13 = []
            for a, z, n, o in ((512, 768, 128, 8), (0, 512, 256, 6), (768, 798, 15, 10)):
                t13 = V(lambda e: e.tensor_tensor(v3(EE[:, a:z], n), v3(EE[:, a:z], n),
                                                  st[:, o:o + 2].unsqueeze(2).broadcast_to([128, 2, n]), ALU.mult), t12)
            yield
            bx, Px = bank("B")
            for w in range(2):
                transpose(Px[:, w * 256:w * 256 + 128], EE[:, 512 + w * 128:640 + w * 128], t13)
                transpose(Px[:, w * 256 + 128:w * 256 + 256], EE[:, w * 256:w * 256 + 128])
            tx = mark()
            by, Py = bank("B")
            for w in range(2):
                transpose(Py[:, w * 128:w * 128 + 128], EE[:, w * 256 + 128:w * 256 + 256])
            for i in range(2):
                transpose(Py[0:15, 256 + i * 128:384 + i * 128], EE[:, 768 + i * 15:783 + i * 15])
            ty = tk["E", key] = mark()
            war = last.get(pkey)
            t14 = A(lambda e: e.copy(PT[:, 0:512], Px[:, :]), tx, war)
            free[bx] = t14
            t15 = A(lambda e: e.copy(PT[:, 512:768], Py[:, 0:256]), ty, war)
            t16 = A(lambda e: e.copy(PT[0:15, 768:1024], Py[0:15, 256:512]), ty)
            free[by] = t16
            yield
            if g == 0:
                pair[j] = bank("A")
            bo, Po = pair[j]
            O = Po[r:r + 64, 0:256]
            vs = lambda i, w: vv[:, i * 256 + w * 128 + g * 64:i * 256 + w * 128 + g * 64 + 64]
            mm(O, vcm[0:15, g * 64:(g + 1) * 64], PT[0:15, 768:1024], True, False, tk["vcm"], t_vv, t14, t16, skip=True)
            mm(O, vs(0, 0), PT[:, 0:256], False, False, skip=True)
            mm(O, vs(0, 1), PT[:, 256:512], False, False, skip=True)
            mm(O[:, 128:256], vs(1, 0), PT[:, 512:640], False, False, skip=True)
            mm(O[:, 128:256], vs(1, 1), PT[:, 640:768], False, True, skip=True)
            last[pkey] = mark()
            av = last[pkey]
            yield
            if g == 1:
                H, L = coh[:, j, :], col[:, j, :]
                th = A(lambda e: e.copy(H, Po[:, 0:T]), av, t_kvpe)
            yield
            if g == 1:
                free[bo] = co_tok[j] = V(lambda e: e.tensor_tensor(L, Po[:, 0:T], f32(H), ALU.subtract), th)

        def mem_heads1():
            yield from pipeline([mem_head(1, h, mq, mq_tok, memsc, scb[:, 48:60], memlast, None, "kvpe") for h in range(4)], 5)

        for _ in queries("Bq", bq, 0.125, bq_tok):
            pass
        gates()
        cg, qg = compress(), queries("Bm", mq, 128.0 ** -0.5, mq_tok)
        mg = mem_heads1()
        for g in (cg, qg, qg):
            next(g)
        W.ahead = 1
        for g in (cg, mg, cg, mg, cg, mg, cg, None, None, qg):
            if g:
                next(g, None)
            else:
                W.split()
        W.ahead = AHEAD
        B_first = []
        weave(pipeline([nsa_head(j, g, (2 * j + g) % 3, g) for j in range(4) for g in range(2)], 5), mg, after(9, out_first(["Bo0", "Bo1"], B_first, 7)))
        toks, xk = out_proj(["Bo0", "Bo1", "Bo2", "Bo3"], "gffn1", B_first, 7)
        at_[0] = 0
        selc = area(1536)
        t_sel = load(selc, sel_d, d_tab, toks[-1])
        gp = area(8)
        qn8 = area(1)
        t_gp = V(lambda e: e.tensor_tensor(gp, sm("gfin"), sm("n1"), ALU.mult), toks[-1])
        t_qn = V(lambda e: e.tensor_scalar(qn8, sm("qn"), 0.125, None, ALU.mult))
        xh0 = []
        new, t_pe = ffn("f1", xk, toks, "cw1", "cb1",
                        lambda c, t, t_x: xh0.append(split_x(xs[c], gp[:, c:c + 1], X(c), XLo(c), t, t_gp, war=t_x)))

        at_[0] = 2560 + 4 * TM
        cq_, ck_ = area(1024), area(4 * TM)
        cq, ck = v3(cq_, T), v3(ck_, TM)
        cv_ = area(3 * 512)
        cvv = v3(cv_, 512)
        cT = area(TM)
        uT = area(4 * TM)
        uu = v3(uT, TM)
        pa, pb = area(TM), area(TM)
        sqh = area(4 * TM)
        r1b = sqh[:, 0:T]
        hs = area(208)
        sl2_ = area(3 * 1056)
        sl2 = [sl2_[:, n * 1056:(n + 1) * 1056] for n in range(3)]
        r2 = area(16)
        XF = lambda c: xh[:, c, :]
        XFL = lambda c: xl[:, c, :]
        xk = [[t] for t in xh0]
        for c in range(8):
            xk[c].append(metok[c])
        xq = [t[0] for t in xk]
        qbk = [projF(nm, X, XLo, xq, T)[0] for nm in ("Cq0", "Cq1")]
        b, P = bank("B")
        for c in range(8):
            k, s, t = square(xs[c], new[c])
            for n in range(2):
                mm(P[:, 2 * n:2 * n + 2], s[:, n * 128:(n + 1) * 128], gw[:, c, :], c == 0 and n == 0, c == 7, t, t_gw, skip=True)
            sq_free[k] = mark()
        ta = V(lambda e: e.tensor_scalar(r2[:, 0:4].rearrange("p (v n) -> p n v", v=2), v3(P[:, 0:4], 2), 1.0 / D, None,
                                         ALU.mult), sq_free[k])
        free[b] = ta
        tc = V(lambda e: e.tensor_scalar(r2[:, 0:2], r2[:, 0:2], EPS, None, ALU.add), ta)
        t1 = power(r2[:, 6:8], r2[:, 0:2], 2, tc)
        td = V(lambda e: e.tensor_tensor(r2[:, 2:4], r2[:, 2:4], r2[:, 6:8], ALU.mult), t1)
        td = V(lambda e: e.tensor_tensor(r2[:, 2:4], r2[:, 2:4], r2[:, 6:8], ALU.mult), td)
        td = V(lambda e: e.tensor_scalar(r2[:, 2:4], r2[:, 2:4], EPS, None, ALU.add), td)
        t2 = power(r2[:, 8:10], r2[:, 2:4], 2, td)
        t_rst = V(lambda e: e.tensor_tensor(rst_[:, 0:2], r2[:, 6:8], r2[:, 8:10], ALU.mult), t2, tk["mr"])
        kbk = projF("Ck0", XF, XFL, xk, TM)
        t_rs = spread(rs_[:, :], rst_, [(2, 0, NM), (0, NM, 128), (1, NM + 128, 128)], t_rst)
        t_r1 = spread(r1b, r2[:, 6:8], TT, t1)
        cq_tok, ck_tok = [], []
        for j, (b, P, t) in enumerate(qbk):
            t = V(lambda e: e.tensor_tensor(cq[:, 2 * j:2 * j + 2, :], v3(P[:, :], T), bc2(rs_[:, NM:TM]), ALU.mult), t, t_rs)
            free[b] = t
            cq_tok.append(t)
        for n in range(4):
            b, P, t = kbk[n]
            t = V(lambda e: e.tensor_tensor(ck[:, n, :], P[:, 0:TM], rs_[:, :], ALU.mult), t, t_rs)
            free[b] = t
            ck_tok.append(t)
            if n == 1:
                kbk += projF("Ck1", XF, XFL, xk, TM)
        for c in range(8):
            new[c] = V(lambda e: e.scalar_tensor_tensor(xs[c], xs[c], sm("gfin", c, c + 1), r1b, ALU.mult, ALU.mult),
                       t_r1, sq_free)
        t_sq = [new[-1], None]

        def head_norm(buf, sq4, dst3, w, tiles, gn, toks, out):
            s4 = sq4[:, 0:4 * w]
            tsq = [A(lambda e: e.activation(v3(s4, w)[:, 2 * j:2 * j + 2, :], dst3[:, 2 * j:2 * j + 2, :], ACT.Square),
                     toks, t_sq[0]) for j in range(2)]
            yield
            b, P = bank("B")
            for j in range(4):
                for n, (a, m) in enumerate(tiles):
                    mm(P[0:m, n * 8 + 2 * j:n * 8 + 2 * j + 2], v3(s4, w)[:, j, a:a + m], cn("halves"),
                       j == 0 and n == 0, j == 3, tsq, skip=True)
            t_h = mark()
            hv, hr = buf[:, 0:24], buf[:, 24:48]
            tp = []
            for n, (a, m) in enumerate(tiles):
                t = V(lambda e: e.tensor_scalar(hv[0:m, n * 8:n * 8 + 8], P[0:m, n * 8:n * 8 + 8], 1.0 / 64, EPS,
                                                ALU.mult, ALU.add), t_h)
                tp.append(power(hr[0:m, n * 8:n * 8 + 8], hv[0:m, n * 8:n * 8 + 8], 8, t))
            free[b] = t
            yield
            b, P = bank("B")
            for n, (a, m) in enumerate(tiles):
                transpose(P[0:8, a:a + m], hr[0:m, n * 8:n * 8 + 8], tp)
            rows = s4[0:8, 0:w]
            t_r = V(lambda e: e.tensor_copy(rows, P[0:8, 0:w]), mark(), t_h)
            free[b] = t_r
            yield
            for j in range(4):
                b, P = bank("B")
                mm(P[:, 0:w], selc[0:8, 1024 + j * 128:1024 + (j + 1) * 128], rows, True, True, t_r, t_sel)
                t = V(lambda e: e.scalar_tensor_tensor(dst3[:, j, :], dst3[:, j, :], gn, P[:, 0:w], ALU.mult, ALU.mult),
                      mark(), tsq)
                free[b] = t
                out.append(t)

        cv_tok = []
        fin_q, fin_k = [], []
        ub = []

        def forget():
            fz, fa, fb, lf = hs[:, 48:72], hs[:, 72:96], hs[:, 96:120], hs[:, 120:144]
            b, P = bank("A")
            for c in range(8):
                s = 320 + c * 8
                mm3(P[0:8, 0:TM], smh[:, s:s + 8], sml[:, s:s + 8], XF(c), XFL(c), c == 0, c == 7, xk[c])
            t = V(lambda e: e.tensor_copy(cT[0:8, :], P[0:8, 0:TM]), mark())
            free[b] = t
            yield
            b, P = bank("B")
            for n, a in enumerate((NM, NM + 128, 0)):
                m = 128 if n < 2 else NM
                transpose(P[0:m, n * 8:n * 8 + 8], cT[0:8, a:a + m], t)
            t = mark()
            t1 = V(lambda e: e.memset(fz, 0.0))
            for n in range(3):
                m = 128 if n < 2 else NM
                t2 = V(lambda e: e.scalar_tensor_tensor(
                    fz[0:m, n * 8:n * 8 + 8], P[0:m, n * 8:n * 8 + 8], rst_[0:m, n:n + 1], sm("bfg")[0:m, :],
                    ALU.mult, ALU.add), t, t_rst, t1)
            free[b] = t2
            t_lf = softplus_neg(lf, fz, t2, fa, fb)
            yield
            yield
            t1 = V(lambda e: e.memset(cT, 0.0), t)
            b, P = bank("B")
            two = cst[:, CN["tri"][0]:CN["tri"][0] + 256]
            for r in (0, 64):
                mm(P[r:r + 8, 0:TM], lf[0:NM, 16:24], cn("trim")[0:NM, :], True, False, t_lf, skip=True)
                mm(P[r:r + 8, NM:TM], lf[:, 0:8], two, False, False, skip=True)
                mm(P[r:r + 8, NM + 128:TM], lf[:, 8:16], cn("tri"), False, True, skip=True)
            t = mark()
            for r in (0, 64):
                tk["cT"] = V(lambda e: e.tensor_copy(cT[r:r + 8, :], P[r:r + 8, 0:TM]), t, t1)
            free[b] = tk["cT"]

        def units2():
            for j in range(2):
                res = projT(f"Cv{j}", XF, XFL, xk, [NM, NM + 128, 0])
                for i in range(3):
                    b, P, t = res[i // 2]
                    n = 128 if i < 2 else NM
                    t = V(lambda e: e.tensor_scalar(
                        cvv[0:n, i, j * 256:(j + 1) * 256], P[0:n, (i % 2) * 256:(i % 2) * 256 + 256],
                        rst_[0:n, i:i + 1], None, ALU.mult), t, t_rst)
                    if i > 0:
                        free[b] = t
                cv_tok.append(t)
                yield

        def pools(g):
            b, P, t = ubk[g]
            u = uu[:, g, :]
            t = V(lambda e: e.tensor_tensor(u, P[:, 0:TM], rs_[:, :], ALU.mult), t, t_rs)
            free[b] = t
            src, bufs, n, lo = u, [pa, pb] if g % 2 == 0 else [sqh[:, 0:TM], sqh[:, TM:2 * TM]], 1, 0
            for s in range(g + 1):
                dst = bufs[s % 2]
                lo += n
                t = POOL.do(lambda e: e.tensor_tensor(dst[:, lo:TM], src[:, lo:TM], src[:, lo - n:TM - n], ALU.add),
                            t, tk.get(("pool", g % 2)))
                src = dst
                n *= 2
            yield
            dst = bufs[(g + 1) % 2]
            t = V(lambda e: e.scalar_tensor_tensor(dst[:, NM:TM], src[:, NM:TM], 1.0 / n, u[:, NM:TM], ALU.mult,
                                                   ALU.subtract), t, tk.get(("pool", g % 2)))
            yield
            b, P = bank("B")
            mm(P[:, 0:T], sm("wpool", g * 128, (g + 1) * 128), dst[:, NM:TM], True, True, t)
            tk["pool", g % 2] = mark()
            H, L = coh[:, 4 + g, :], col[:, 4 + g, :]
            t = A(lambda e: e.activation(H, P[:, 0:T], ACT.Copy, scale=sm("pscale", g, g + 1)), tk["pool", g % 2])
            t = V(lambda e: e.scalar_tensor_tensor(L, P[:, 0:T], sm("pscale", g, g + 1), f32(H), ALU.mult,
                                                   ALU.subtract), t)
            free[b] = t
            co_tok[4 + g] = t

        kn_sq = sl2_[:, 0:4 * TM]
        def fill():
            yield from units2()
            next(u3)
            yield
            next(u3)

        last = {}

        def head2(j, hh, key):
            h, r = 2 * j + hh, hh * 64
            EE, PT, PM = sl2[key][:, 0:416], sl2[key][:, 416:800], sl2[key][:, 800:1056]
            st = hs[:, 144 + key * 4:148 + key * 4]
            war = tk.get(("E2", key))
            sel = selc[r:r + 64, h * 128:(h + 1) * 128]
            b, P = bank("A")
            for i, (o, n) in enumerate(((272, 144), (0, 272))):
                mm(P[:, o:o + n], cq[r:r + 64, j, i * 128:(i + 1) * 128], ck[r:r + 64, j, 0:n], True, False,
                   fin_q, fin_k, tk["cT"], t_sel)
                mm(P[:, o:o + n], sel, cT[r:r + 64, 0:n], False, True)
            t = mark()
            m2 = cn("mask2")
            t1 = V(lambda e: e.tensor_tensor(EE[:, 0:272], P[:, 0:272], m2, ALU.add), t, war)
            t2 = V(lambda e: e.tensor_tensor(EE[:, 272:416], P[:, 272:416], m2[:, 128:272], ALU.add), t)
            free[b] = t2
            t3 = V(lambda e: e.tensor_reduce(st[:, 0:1], EE[:, 0:272], AX.X, ALU.max, negate=True), t1)
            t4 = V(lambda e: e.tensor_reduce(st[:, 1:2], EE[:, 272:416], AX.X, ALU.max, negate=True), t2)
            for n, (a, z) in enumerate(((0, 272), (272, 416))):
                t5 = A(lambda e: e.activation(EE[:, a:z], EE[:, a:z], ACT.Exp, bias=st[:, n:n + 1],
                                              accum_out=st[:, 2 + n:3 + n]), t4)
            yield
            t6 = V(lambda e: e.reciprocal(st[:, 2:4], st[:, 2:4]), t5)
            for n, (a, z) in enumerate(((0, 272), (272, 416))):
                t7 = V(lambda e: e.tensor_scalar(EE[:, a:z], EE[:, a:z], st[:, 2 + n:3 + n], None, ALU.mult), t6)
            yield
            bx, Px = bank("B")
            transpose(Px[:, 0:128], EE[:, 272 + NM:416], t7)
            transpose(Px[:, 128:256], EE[:, NM:NM + 128])
            transpose(Px[:, 256:384], EE[:, NM + 128:272])
            tx = mark()
            by, Py = bank("B")
            transpose(Py[0:NM, 0:128], EE[:, 272:272 + NM])
            transpose(Py[0:NM, 128:256], EE[:, 0:NM])
            ty = tk["E2", key] = mark()
            war = last.get(key)
            t8 = A(lambda e: e.copy(PT, Px[:, 0:384]), tx, war)
            free[bx] = t8
            t9 = A(lambda e: e.copy(PM[0:NM, :], Py[0:NM, 0:256]), ty, war)
            free[by] = t9
            yield
            if hh == 0:
                pair[j] = bank("A")
            bo, Po = pair[j]
            O = Po[r:r + 64, 0:256]
            vs = lambda i, n: cvv[0:n, i, h * 64:(h + 1) * 64]
            mm(O, vs(2, NM), PM[0:NM, :], True, False, cv_tok, t8, t9, skip=True)
            mm(O, vs(0, 128), PT[:, 0:256], False, False, skip=True)
            mm(O[:, 128:256], vs(1, 128), PT[:, 256:384], False, True, skip=True)
            last[key] = mark()
            av = last[key]
            yield
            if hh == 1:
                H, L = coh[:, j, :], col[:, j, :]
                th = A(lambda e: e.copy(H, Po[:, 0:T]), av)
            yield
            if hh == 1:
                free[bo] = co_tok[j] = V(lambda e: e.tensor_tensor(L, Po[:, 0:T], f32(H), ALU.subtract), th)

        ubk = []

        def units3():
            ubk.extend(projF("Cu0", XF, XFL, xk, TM))
            yield
            g = [pools(n) for n in range(4)]
            for step in ((0,), (1, 0), (1, 0), (1, "Cu1"), (2, 3), (2, 3), (2, 3)):
                for n in step:
                    if n == "Cu1":
                        ubk.extend(projF(n, XF, XFL, xk, TM))
                    else:
                        next(g[n], None)
                yield

        u3 = units3()
        weave(head_norm(hs[:, 0:48], sqh, cq, T, [(0, 128), (128, 128)], qn8, cq_tok + [t_qn], fin_q),
              head_norm(hs[:, 160:208], kn_sq, ck, TM, [(NM, 128), (NM + 128, 128), (0, NM)], sm("kn"), ck_tok, fin_k),
              fill(), forget())
        C_first = []
        weave(pipeline([head2(j, hh, (2 * j + hh) % 3) for j in range(4) for hh in range(2)], 5), after(0, u3),
              after(9, out_first(["Co0", "Co1"], C_first, 6)))
        toks, xk = out_proj(["Co0", "Co1", "Co2", "Co3"], "n2", C_first, 6)
        s_out = sem("s_out")
        ffn("f2", xk, toks, None, None, lambda c, t, t_x: SP.quiet(
            lambda e: e.dma_start(out_d[:, c * T:(c + 1) * T], xs[c]).then_inc(s_out, 16), t))
        SP.wait((s_out, 128))


def constants():
    f = np.float32
    p = np.arange(128)
    tri = (p[:, None] <= p[None, :]).astype(f)
    c = {
        "ident": np.eye(128, dtype=f), "ones": np.ones((128, 128), f), "tri": tri,
        "halves": (p[:, None] // 64 == np.arange(2)[None, :]).astype(f), "mhalf": np.full((128, 32), -0.5, f),
        "trim": (p[:, None] <= np.arange(TM)[None, :]).astype(f),
        "valid": np.stack([(p >= 31).astype(f), np.ones(128, f)], 1),
        "one": np.ones((128, 1), f),
    }
    causal = np.where(p[None, :] <= p[:, None], 0, NEG).astype(f)
    c["mask2"] = np.concatenate([np.zeros((128, 144), f), causal], 1)
    sel = np.zeros((128, 8, 128), f)
    for h in range(8):
        sel[h, h] = sel[64 + h, h] = -1
    spr = np.zeros((128, 4, 128), f)
    for h in range(8):
        spr[h, h // 2, (h % 2) * 64:(h % 2 + 1) * 64] = 1
    sel = np.concatenate([sel.reshape(128, -1), spr.reshape(128, -1)], 1)
    cst = np.concatenate([c[n] for n, _ in CONST], 1)
    gm = []
    for m in LEVELS:
        s, t = p[:, None], p[None, :]
        if m:
            gm.append((s // (2 * m) == t // (2 * m)) & (s % (2 * m) < m) & (t % (2 * m) >= m))
        else:
            gm.append(s == t)
    gm = np.concatenate(gm, 1).astype(f)
    t, s = p[:, None], p[None, :]
    e = np.arange(16)[None, :] * 16 + 31
    cmp = [np.where(i * 128 + t - e >= 0, -(i * 128 + t - e), NEG) for i in range(2)]
    ns = np.concatenate([-(128 + t - s), np.where(s <= t, -(t - s), NEG)] + cmp, 1).astype(f)
    return cst, gm, ns, sel


def pack(i):
    d = {}

    def cols(w, a, b):
        k = w.shape[0] // 128
        return w.reshape(k, 128, -1)[:, :, a:b].transpose(1, 0, 2).reshape(128, -1)

    units = {}

    def put(prefix, w, a, n):
        for j in range(n):
            units[f"{prefix}{j}"] = cols(w, a + 256 * j, a + 256 * (j + 1))

    aw = i["a_w_in"][0]
    units["Aq"], units["Ak"] = cols(aw, 0, 256), cols(aw, 256, 512)
    put("Av", aw, 512, 2)
    put("Ar", aw, 1024, 2)
    put("Am", aw, 1552, 2)
    for l in range(2):
        put(f"m{l}k", i["w_mem_kv"][l], 0, 2)
        put(f"m{l}v", i["w_mem_kv"][l], 512, 2)
    put("Ao", i["a_w_out"][0], 0, 4)

    def ffn(tag, wa, wb, wd):
        for f in range(NF):
            c = slice(f * 128, (f + 1) * 128)
            units[f"{tag}u{f}"] = cols(np.concatenate([wa[:, c], wb[:, c]], 1), 0, 256)
        for p in range(11):
            units[f"{tag}d{p}"] = cols(wd[p * 256:(p + 1) * 256], 0, 1024)

    for l in range(2):
        ffn(f"f{l}", i["w_up"][l][:, :2816], i["w_up"][l][:, 2816:], i["w_down"][l])
    ffn("f2", i["w_gate_2"][0], i["w_up_2"][0], i["w_down_2"][0])
    kv = i["w_kv"]
    seg = lambda n: kv[:, n * 128:(n + 1) * 128]
    units["kvc"] = cols(kv[:, 0:256], 0, 256)
    units["kvk"] = cols(np.concatenate([seg(2), seg(4)], 1), 0, 256)
    units["kvv"] = cols(np.concatenate([seg(3), seg(5)], 1), 0, 256)
    for n, w in (("ck", i["w_ck1"]), ("cv", i["w_cv1"])):
        for j in range(2):
            units[f"{n}{j}"] = cols(w[j * 1024:(j + 1) * 1024], 0, 256)
    bw = i["b_w_in"][0]
    order = [0, 4, 1, 5, 2, 6, 3, 7]
    bq = bw[:, :512].reshape(D, 8, 64)[:, order].reshape(D, 512)
    put("Bq", bq, 0, 2)
    put("Bm", bw, 536, 2)
    bo = i["b_w_out"][0]
    bo = np.concatenate([bo[:512].reshape(8, 64, D)[order].reshape(512, D), bo[512:]], 0)
    put("Bo", bo, 0, 4)
    cw = i["w_in_2"][0]
    put("Cq", cw, 0, 2)
    put("Ck", cw, 512, 2)
    put("Cv", cw, 1024, 2)
    put("Cu", cw, 1544, 2)
    put("Co", i["w_out_2"][0], 0, 4)
    d["w"] = np.stack([units[n] for n in unit_names()])

    vec = lambda v: v.reshape(-1, 128).T
    bc = lambda v: np.broadcast_to(v.reshape(1, -1), (128, v.size))
    s = {
        "gmix0": vec(i["g_mix"][0]), "gmix1": vec(i["g_mix"][1]), "gffn0": vec(i["g_ffn"][0]),
        "gffn1": vec(i["g_ffn"][1]), "gmem0": vec(i["g_mem"][0]), "gmem1": vec(i["g_mem"][1]),
        "gkv": vec(i["g_kv"]), "gfin": vec(i["g_final"]), "n1": vec(i["norm1_w_2"][0]), "n2": vec(i["norm2_w_2"][0]),
        "ghead": vec(i["a_g_head"][0]), "pscale": vec(i["pool_scale_2"][0]),
        "qn": vec(np.concatenate([i["q_norm_w_2"][0]] * 2)), "kn": vec(np.concatenate([i["k_norm_w_2"][0]] * 2)),
        "bfg": bc(i["b_fgate_2"][0]),
        "pek": i["pe_k"].reshape(16, 128).T, "pev": i["pe_v"].reshape(16, 128).T,
        "cb0": vec(i["conv_b"][0]), "cb1": vec(i["conv_b"][1]),
        "walr": cols(aw, 1536, 1552), "wgl": cols(bw, 512, 536), "wfg": cols(cw, 1536, 1544),
        "balpha": bc(i["a_b_alpha"][0]), "wck2": cols(i["w_ck2"], 0, 64), "wcv2": cols(i["w_cv2"], 0, 64),
        "wpool": i["w_pool_2"][0].transpose(1, 0, 2).reshape(128, 512),
    }
    for l in range(2):
        s[f"cw{l}"] = np.concatenate([vec(i["conv_w"][l][n]) for n in range(3)], 1)
    wa = np.zeros((128, 256), np.float32)
    wa[:16] = i["a_w_alpha"][0]
    s["walpha"] = wa
    d["small"] = np.concatenate([s[n] for n, _ in SMALL], 1)
    d["x"] = cols(i["x"][0].T, 0, T)
    d["mem"] = cols(i["mem"][0].T, 0, T)
    d["meta"] = cols(i["meta_tokens_2"].T, 0, NM)
    d["const"], d["gmask"], d["nsac"], d["sel"] = constants()
    return {k: np.ascontiguousarray(v) for k, v in d.items()}


_ORDER = ["w", "x", "mem", "meta", "small", "const", "gmask", "nsac", "sel"]


def kernel(**inputs):
    import concourse.bacc as _bacc
    from concourse.bass_utils import run_bass_kernel_spmd as _run

    d = pack({k: np.asarray(v) for k, v in inputs.items()})
    nc = _bacc.Bacc("TRN2", target_bir_lowering=False, num_devices=1)
    args, arrays = [], {}
    for n in _ORDER:
        arrays[f"in_{n}"] = d[n]
        args.append(nc.dram_tensor(f"in_{n}", d[n].shape, F32, kind="ExternalInput").ap())
    args.append(nc.dram_tensor("out_0", (128, 8 * T), F32, kind="ExternalOutput").ap())
    build(nc, *args)
    r = _run(nc, [arrays], core_ids=[0])
    o = np.asarray(r.results[0]["out_0"])
    return np.ascontiguousarray(o.reshape(128, 8, T).transpose(2, 1, 0).reshape(1, T, D))
```
